# Optimizing a Trainium2 kernel written in Bass

```python
import math
import jax, jax.numpy as jnp
from jax import lax
import numpy as np

D_MODEL = 1024
BATCH = 1
SEQ = 256
DEPTH = 2

D_MIX = D_MODEL
D_GROUP = D_MIX // 4
HEAD_DIM = 64
RET_HEADS = D_GROUP // HEAD_DIM
ML_HEADS = D_GROUP // HEAD_DIM
CHUNK = 128
S5_CH = 16
S5_GROUPS = D_GROUP // S5_CH
S5_STATE = 64
HY_ORDER = 2
HY_EMB = 33
HY_BANDS = (HY_EMB - 1) // 2
HY_FFN = 64
HY_FAST_DECAY = 0.3
HY_SLOW_DECAY = 1.5
HY_TARGET = 1e-2
SHORT_CONV = 3
D_FF = 2816
N_EXPERTS = 8
TOP_K = 2
D_FF_EXPERT = 3584
ROPE_BASE = 10000.0
EPS = 1e-5
DN_ALPHA = (2 * DEPTH) ** 0.25
DN_BETA = (8 * DEPTH) ** -0.25
N_DENSE = (DEPTH + 1) // 2
N_MOE = DEPTH // 2

RET_COLS = 4 * D_GROUP
S5_COLS = D_GROUP
HY_COLS = (HY_ORDER + 1) * D_GROUP
ML_COLS = 4 * D_GROUP + 4 * ML_HEADS
D_IN = RET_COLS + S5_COLS + HY_COLS + ML_COLS

kernel_name = "hybrid_parallel_heads_encoder"

def layer_norm(x, w, b):
    xf = x.astype(jnp.float32)
    mu = jnp.mean(xf, -1, keepdims=True)
    var = jnp.mean(jnp.square(xf - mu), -1, keepdims=True)
    y = (xf - mu) * lax.rsqrt(var + EPS) * w.astype(jnp.float32) + b.astype(jnp.float32)
    return y.astype(x.dtype)

def head_norm(h, w):
    mu = jnp.mean(h, -1, keepdims=True)
    var = jnp.mean(jnp.square(h - mu), -1, keepdims=True)
    y = (h - mu) * lax.rsqrt(var + EPS)
    return y.reshape(h.shape[0], h.shape[1], -1) * w.astype(jnp.float32)

def flip(t):
    return t[:, ::-1]

def short_conv(x, w, b):
    L = x.shape[1]
    pad = SHORT_CONV // 2
    xp = jnp.pad(x, ((0, 0), (pad, pad), (0, 0)))
    y = b
    for j in range(SHORT_CONV):
        y = y + xp[:, j:j + L] * w[j]
    return y

def rotary(t):
    L = t.shape[1]
    half = HEAD_DIM // 2
    inv = ROPE_BASE ** (-jnp.arange(half, dtype=jnp.float32) / half)
    ang = jnp.arange(L, dtype=jnp.float32)[:, None] * inv[None, :]
    cos = jnp.cos(ang)[None, :, None, :]
    sin = jnp.sin(ang)[None, :, None, :]
    t1, t2 = t[..., :half], t[..., half:]
    return jnp.concatenate([t1 * cos - t2 * sin, t2 * cos + t1 * sin], -1)

def to_chunks(t):
    B_, L = t.shape[:2]
    t = t.reshape(B_, L // CHUNK, CHUNK, *t.shape[2:])
    return jnp.moveaxis(t, (1, 3), (0, 2))

def from_chunks(t):
    t = jnp.moveaxis(t, (0, 2), (1, 3))
    return t.reshape(t.shape[0], -1, *t.shape[3:])

def retention_scan(q, k, v, log_gamma, include_diag):
    B_, L, H, d = q.shape
    pos = jnp.arange(CHUNK, dtype=jnp.float32)
    lag = pos[:, None] - pos[None, :]
    mask = lag >= 0 if include_diag else lag > 0
    d_in = jnp.where(mask[None], jnp.exp(log_gamma[:, None, None] * jnp.maximum(lag, 0.0)[None]), 0.0)
    q_dec = jnp.exp(log_gamma[:, None] * (pos[None, :] + 1.0))[None, :, :, None]
    k_dec = jnp.exp(log_gamma[:, None] * (CHUNK - 1.0 - pos[None, :]))[None, :, :, None]
    c_dec = jnp.exp(log_gamma * CHUNK)[None, :, None, None]

    def step(state, blk):
        qi, ki, vi = blk
        s = jnp.einsum("bhnd,bhmd->bhnm", qi, ki) * d_in
        out = jnp.einsum("bhnm,bhme->bhne", s, vi) + jnp.einsum("bhnd,bhde->bhne", qi, state) * q_dec
        state = state * c_dec + jnp.einsum("bhmd,bhme->bhde", ki * k_dec, vi)
        return state, out

    state0 = jnp.zeros((B_, H, d, d), jnp.float32)
    _, out = lax.scan(step, state0, (to_chunks(q), to_chunks(k), to_chunks(v)))
    return from_chunks(out)

def retention_mixer(p, gn_w):
    B_, L, _ = p.shape
    q, k, v, g = jnp.split(p.astype(jnp.float32), 4, axis=-1)
    shp = (B_, L, RET_HEADS, HEAD_DIM)
    q = rotary(q.reshape(shp))
    k = rotary(k.reshape(shp)) * HEAD_DIM ** -0.5
    v = v.reshape(shp)
    log_gamma = jnp.log(1.0 - 2.0 ** (-5.0 - jnp.arange(RET_HEADS, dtype=jnp.float32)))
    o = retention_scan(q, k, v, log_gamma, True) + flip(retention_scan(flip(q), flip(k), flip(v), log_gamma, False))
    return jax.nn.silu(g) * head_norm(o, gn_w)

def s5_mixer(u, a_re, a_im, log_dt, b_re, b_im, c_re, c_im, d_skip, w_glu):
    B_, L, _ = u.shape
    f32 = jnp.float32
    uf = u.astype(f32)
    ug = uf.reshape(B_, L, S5_GROUPS, S5_CH)
    a = lax.complex(a_re.astype(f32), a_im.astype(f32))
    delta = jnp.exp(log_dt.astype(f32))[..., None]
    a_bar = jnp.exp(a * delta)
    b = lax.complex(b_re.astype(f32), b_im.astype(f32))
    b_bar = ((a_bar - 1.0) / a)[..., None] * b[None]
    c = lax.complex(c_re.astype(f32), c_im.astype(f32))

    def combine(e1, e2):
        a1, x1 = e1
        a2, x2 = e2
        return a1 * a2, a2 * x1 + x2

    def run(direction, reverse):
        bu = jnp.einsum("gpc,blgc->blgp", b_bar[direction], ug)
        decay = jnp.broadcast_to(a_bar[direction], bu.shape)
        _, states = lax.associative_scan(combine, (decay, bu), reverse=reverse, axis=1)
        return jnp.einsum("gcp,blgp->blgc", c[direction], states).real

    y = (run(0, False) + run(1, True)).reshape(B_, L, D_GROUP) + d_skip.astype(f32) * uf
    z = jax.nn.gelu(y)
    return z * jax.nn.sigmoid(z @ w_glu.astype(f32))

def hyena_filters(L, w1, b1, w2, b2, w3, freq):
    f32 = jnp.float32
    t = jnp.linspace(0.0, 1.0, L, dtype=f32)[:, None]
    w = 2.0 * math.pi * jnp.arange(L, dtype=f32)[:, None] / L
    bands = jnp.linspace(1e-4, HY_BANDS - 1, HY_BANDS, dtype=f32)[None, :]
    z = jnp.concatenate([t, jnp.cos(bands * w), -jnp.sin(bands * w)], axis=-1)
    fr = freq.astype(f32)
    h = jnp.sin(fr * (z @ w1.astype(f32) + b1.astype(f32)))
    h = jnp.sin(fr * (h @ w2.astype(f32) + b2.astype(f32)))
    h = (h @ w3.astype(f32)).reshape(L, HY_ORDER, 2, D_GROUP)
    max_decay = math.log(HY_TARGET) / HY_FAST_DECAY
    min_decay = math.log(HY_TARGET) / HY_SLOW_DECAY
    rates = jnp.abs(jnp.linspace(min_decay, max_decay, D_GROUP, dtype=f32))
    h = h * jnp.exp(-t * rates)[:, None, None, :]
    return h * lax.rsqrt(jnp.sum(jnp.square(h), axis=(0, 2), keepdims=True))

def fft_long_conv(u, h_fwd, h_bwd):
    L = u.shape[1]
    kern = jnp.concatenate([h_fwd, jnp.zeros_like(h_fwd[:1]), h_bwd[:0:-1]], axis=0)
    kf = jnp.fft.rfft(kern, n=2 * L, axis=0)
    uf = jnp.fft.rfft(u, n=2 * L, axis=1)
    return jnp.fft.irfft(uf * kf[None], n=2 * L, axis=1)[:, :L]

def hyena_mixer(p, conv_w, conv_b, w1, b1, w2, b2, w3, freq, bias):
    L = p.shape[1]
    f32 = jnp.float32
    pc = short_conv(p.astype(f32), conv_w.astype(f32), conv_b.astype(f32))
    parts = jnp.split(pc, HY_ORDER + 1, axis=-1)
    filt = hyena_filters(L, w1, b1, w2, b2, w3, freq)
    bias = bias.astype(f32)
    z = parts[0]
    for n in range(HY_ORDER):
        z = parts[n + 1] * (fft_long_conv(z, filt[:, n, 0], filt[:, n, 1]) + z * bias[n])
    return z

def mlstm_scan(q, k, v, log_i, log_f):
    B_, L, H, d = q.shape
    causal = jnp.tril(jnp.ones((CHUNK, CHUNK), bool))

    def step(carry, blk):
        c_mem, n_mem, m_prev = carry
        qi, ki, vi, ii, fi = blk
        a = jnp.cumsum(fi, axis=-1)
        a_end = a[..., -1]
        dmat = jnp.where(causal, a[..., :, None] - a[..., None, :] + ii[..., None, :], -jnp.inf)
        inter = a + m_prev[..., None]
        m_row = jnp.maximum(inter, jnp.max(dmat, -1))
        s = jnp.einsum("bhnd,bhmd->bhnm", qi, ki) * jnp.exp(dmat - m_row[..., None])
        w_inter = jnp.exp(inter - m_row)
        num = jnp.einsum("bhnm,bhme->bhne", s, vi) + w_inter[..., None] * jnp.einsum("bhnd,bhde->bhne", qi, c_mem)
        den = jnp.sum(s, -1) + w_inter * jnp.einsum("bhnd,bhd->bhn", qi, n_mem)
        h = num / jnp.maximum(jnp.abs(den), jnp.exp(-m_row))[..., None]
        g = a_end[..., None] - a + ii
        m_new = jnp.maximum(a_end + m_prev, jnp.max(g, -1))
        wk = jnp.exp(g - m_new[..., None])[..., None] * ki
        carry_decay = jnp.exp(a_end + m_prev - m_new)
        c_mem = carry_decay[..., None, None] * c_mem + jnp.einsum("bhmd,bhme->bhde", wk, vi)
        n_mem = carry_decay[..., None] * n_mem + jnp.sum(wk, axis=2)
        return (c_mem, n_mem, m_new), h

    carry0 = (jnp.zeros((B_, H, d, d), jnp.float32), jnp.zeros((B_, H, d), jnp.float32), jnp.zeros((B_, H), jnp.float32))
    _, h = lax.scan(step, carry0, (to_chunks(q), to_chunks(k), to_chunks(v), to_chunks(log_i), to_chunks(log_f)))
    return from_chunks(h)

def mlstm_mixer(p, conv_w, conv_b, gate_b, gn_w):
    B_, L, _ = p.shape
    f32 = jnp.float32
    pf = p.astype(f32)
    qk, v, o, gates = jnp.split(pf, [2 * D_GROUP, 3 * D_GROUP, 4 * D_GROUP], axis=-1)
    qk = jax.nn.silu(short_conv(qk, conv_w.astype(f32), conv_b.astype(f32)))
    q, k = jnp.split(qk, 2, axis=-1)
    shp = (B_, L, ML_HEADS, HEAD_DIM)
    q = q.reshape(shp)
    k = k.reshape(shp) * HEAD_DIM ** -0.5
    v = v.reshape(shp)
    gates = gates.reshape(B_, L, 4, ML_HEADS) + gate_b.astype(f32)
    i_fw, f_fw, i_bw, f_bw = gates[:, :, 0], gates[:, :, 1], gates[:, :, 2], gates[:, :, 3]
    h_fw = mlstm_scan(q, k, v, i_fw, jax.nn.log_sigmoid(f_fw))
    h_bw = flip(mlstm_scan(flip(q), flip(k), flip(v), flip(i_bw), flip(jax.nn.log_sigmoid(f_bw))))
    return jax.nn.sigmoid(o) * head_norm(h_fw + h_bw, gn_w)

def token_mixer(h, w_in, w_out, ret_gn_w,
                s5_a_re, s5_a_im, s5_log_dt, s5_b_re, s5_b_im, s5_c_re, s5_c_im, s5_d, s5_w_glu,
                hy_conv_w, hy_conv_b, hy_w1, hy_b1, hy_w2, hy_b2, hy_w3, hy_freq, hy_bias,
                ml_conv_w, ml_conv_b, ml_gate_b, ml_gn_w):
    proj = h @ w_in
    p_ret, p_s5, p_hy, p_ml = jnp.split(proj, [RET_COLS, RET_COLS + S5_COLS, RET_COLS + S5_COLS + HY_COLS], axis=-1)
    y = jnp.concatenate([
        retention_mixer(p_ret, ret_gn_w),
        s5_mixer(p_s5, s5_a_re, s5_a_im, s5_log_dt, s5_b_re, s5_b_im, s5_c_re, s5_c_im, s5_d, s5_w_glu),
        hyena_mixer(p_hy, hy_conv_w, hy_conv_b, hy_w1, hy_b1, hy_w2, hy_b2, hy_w3, hy_freq, hy_bias),
        mlstm_mixer(p_ml, ml_conv_w, ml_conv_b, ml_gate_b, ml_gn_w),
    ], axis=-1)
    return y.astype(h.dtype) @ w_out

def swiglu(x, w1, w3, w2):
    return (jax.nn.silu(x @ w1) * (x @ w3)) @ w2

def moe_swiglu(x, router, w1, w3, w2):
    B_, L, D = x.shape
    xt = x.reshape(B_ * L, D)
    logits = (xt @ router).astype(jnp.float32)
    top_val, top_idx = lax.top_k(logits, TOP_K)
    gate = jax.nn.softmax(top_val, axis=-1)
    combine = jnp.einsum("tk,tke->te", gate, jax.nn.one_hot(top_idx, N_EXPERTS, dtype=jnp.float32))
    out = jnp.zeros_like(xt)
    for e in range(N_EXPERTS):
        out = out + combine[:, e:e + 1].astype(x.dtype) * swiglu(xt, w1[e], w3[e], w2[e])
    return out.reshape(B_, L, D)

def setup_inputs(seed: int = 0) -> dict:
    key = jax.random.key(seed)
    ks = iter(jax.random.split(key, 64))
    f32 = jnp.float32

    def nrm(shape, scale):
        return jax.random.normal(next(ks), shape, f32) * scale

    def gain(shape):
        return 1.0 + nrm(shape, 0.02)

    G, P = S5_GROUPS, S5_STATE
    ig = nrm((DEPTH, 2, ML_HEADS), 0.1)
    fg = jnp.linspace(3.0, 6.0, ML_HEADS, dtype=f32) + nrm((DEPTH, 2, ML_HEADS), 0.01)
    return {
        "x": nrm((BATCH, SEQ, D_MODEL), 1.0),
        "ln_in_w": gain((D_MODEL,)),
        "ln_in_b": nrm((D_MODEL,), 0.02),
        "w_in": nrm((DEPTH, D_MODEL, D_IN), D_MODEL ** -0.5),
        "w_out": nrm((DEPTH, D_MIX, D_MODEL), DN_BETA * D_MIX ** -0.5),
        "ret_gn_w": gain((DEPTH, D_GROUP)),
        "s5_a_re": -0.5 + nrm((DEPTH, 2, G, P), 0.01),
        "s5_a_im": math.pi * jnp.arange(P, dtype=f32) + nrm((DEPTH, 2, G, P), 0.01),
        "s5_log_dt": jax.random.uniform(next(ks), (DEPTH, 2, G), f32, math.log(1e-3), math.log(1e-1)),
        "s5_b_re": nrm((DEPTH, G, P, S5_CH), (2 * S5_CH) ** -0.5),
        "s5_b_im": nrm((DEPTH, G, P, S5_CH), (2 * S5_CH) ** -0.5),
        "s5_c_re": nrm((DEPTH, 2, G, S5_CH, P), (2 * P) ** -0.5),
        "s5_c_im": nrm((DEPTH, 2, G, S5_CH, P), (2 * P) ** -0.5),
        "s5_d": nrm((DEPTH, D_GROUP), 1.0),
        "s5_w_glu": nrm((DEPTH, D_GROUP, D_GROUP), D_GROUP ** -0.5),
        "hy_conv_w": nrm((DEPTH, SHORT_CONV, HY_COLS), SHORT_CONV ** -0.5),
        "hy_conv_b": nrm((DEPTH, HY_COLS), 0.02),
        "hy_w1": nrm((DEPTH, HY_EMB, HY_FFN), HY_EMB ** -0.5),
        "hy_b1": nrm((DEPTH, HY_FFN), 0.1),
        "hy_w2": nrm((DEPTH, HY_FFN, HY_FFN), HY_FFN ** -0.5),
        "hy_b2": nrm((DEPTH, HY_FFN), 0.1),
        "hy_w3": nrm((DEPTH, HY_FFN, HY_ORDER * 2 * D_GROUP), HY_FFN ** -0.5),
        "hy_freq": 1.0 + nrm((DEPTH, HY_FFN), 0.01),
        "hy_bias": nrm((DEPTH, HY_ORDER, D_GROUP), 1.0),
        "ml_conv_w": nrm((DEPTH, SHORT_CONV, 2 * D_GROUP), SHORT_CONV ** -0.5),
        "ml_conv_b": nrm((DEPTH, 2 * D_GROUP), 0.02),
        "ml_gate_b": jnp.stack([ig[:, 0], fg[:, 0], ig[:, 1], fg[:, 1]], axis=1),
        "ml_gn_w": gain((DEPTH, D_GROUP)),
        "ln1_w": gain((DEPTH, D_MODEL)),
        "ln1_b": nrm((DEPTH, D_MODEL), 0.02),
        "ln2_w": gain((DEPTH, D_MODEL)),
        "ln2_b": nrm((DEPTH, D_MODEL), 0.02),
        "ffn_w1": nrm((N_DENSE, D_MODEL, D_FF), D_MODEL ** -0.5),
        "ffn_w3": nrm((N_DENSE, D_MODEL, D_FF), D_MODEL ** -0.5),
        "ffn_w2": nrm((N_DENSE, D_FF, D_MODEL), DN_BETA * D_FF ** -0.5),
        "moe_router": nrm((N_MOE, D_MODEL, N_EXPERTS), D_MODEL ** -0.5),
        "moe_w1": nrm((N_MOE, N_EXPERTS, D_MODEL, D_FF_EXPERT), D_MODEL ** -0.5),
        "moe_w3": nrm((N_MOE, N_EXPERTS, D_MODEL, D_FF_EXPERT), D_MODEL ** -0.5),
        "moe_w2": nrm((N_MOE, N_EXPERTS, D_FF_EXPERT, D_MODEL), DN_BETA * D_FF_EXPERT ** -0.5),
    }

def reference(x, ln_in_w, ln_in_b, w_in, w_out, ret_gn_w,
              s5_a_re, s5_a_im, s5_log_dt, s5_b_re, s5_b_im, s5_c_re, s5_c_im, s5_d, s5_w_glu,
              hy_conv_w, hy_conv_b, hy_w1, hy_b1, hy_w2, hy_b2, hy_w3, hy_freq, hy_bias,
              ml_conv_w, ml_conv_b, ml_gate_b, ml_gn_w,
              ln1_w, ln1_b, ln2_w, ln2_b,
              ffn_w1, ffn_w3, ffn_w2, moe_router, moe_w1, moe_w3, moe_w2):
    h = layer_norm(x, ln_in_w, ln_in_b)
    for l in range(DEPTH):
        mix = token_mixer(h, w_in[l], w_out[l], ret_gn_w[l],
                          s5_a_re[l], s5_a_im[l], s5_log_dt[l], s5_b_re[l], s5_b_im[l],
                          s5_c_re[l], s5_c_im[l], s5_d[l], s5_w_glu[l],
                          hy_conv_w[l], hy_conv_b[l], hy_w1[l], hy_b1[l], hy_w2[l], hy_b2[l],
                          hy_w3[l], hy_freq[l], hy_bias[l],
                          ml_conv_w[l], ml_conv_b[l], ml_gate_b[l], ml_gn_w[l])
        h = layer_norm(DN_ALPHA * h + mix, ln1_w[l], ln1_b[l])
        if l % 2 == 0:
            f = swiglu(h, ffn_w1[l // 2], ffn_w3[l // 2], ffn_w2[l // 2])
        else:
            f = moe_swiglu(h, moe_router[l // 2], moe_w1[l // 2], moe_w3[l // 2], moe_w2[l // 2])
        h = layer_norm(DN_ALPHA * h + f, ln2_w[l], ln2_b[l])
    return h


_drawn_inputs = setup_inputs


def setup_inputs(seed=0):
    import zlib

    import numpy as np

    out = dict(_drawn_inputs(seed))
    spreads = {}
    factors = {'ret_gn_w': 8.0,
     's5_a_re': 64.0,
     's5_a_im': 54.408,
     's5_log_dt': 63.888,
     's5_b_re': 51.544,
     's5_b_im': 64.0,
     's5_c_re': 57.12,
     's5_c_im': 64.0,
     'hy_freq': 5.627,
     'ml_conv_b': 7.51,
     'ml_gn_w': 16.956,
     'hy_conv_b': 2.879}
    for name, (base, spread) in spreads.items():
        noise = np.random.default_rng([zlib.crc32(name.encode()), seed]).standard_normal(out[name].shape)
        drawn = base * np.exp(spread * noise) if base else spread * noise
        out[name] = __import__('jax').numpy.asarray(drawn.astype(out[name].dtype))
    for name, factor in factors.items():
        out[name] = (out[name] * factor).astype(out[name].dtype)
    return out
```

```python
import math
from contextlib import ExitStack

import numpy as np
import concourse.bass as bass
from concourse import mybir

F32 = mybir.dt.float32
I32 = mybir.dt.int32
ALU = mybir.AluOpType
ACT = mybir.ActivationFunctionType
AX = mybir.AxisListType

P = 128
D = 1024
L = 256
TT = L // P
KT = D // P
DEPTH = 2
DG = 256
HD = 64
H = DG // HD
N_STATE = 64
S5_CH = 16
D_FF = 2816
D_FFE = 3584
NE = 8
EPS = 1e-5
ALPHA = (2 * DEPTH) ** 0.25
FC = 256
NC_FF = D_FF // FC
NC_E = D_FFE // FC
SLOTS = 4
SLOT = 3 * KT * FC
WIN_COLS = SLOT // KT
RING_MIX = 6
G_FF = RING_MIX
G_MIX1 = G_FF + NC_FF
G_MOE = G_MIX1 + RING_MIX
MAGIC = 12582912.0
TURN = 6.2831850
INV2PI = 1.0 / (2.0 * math.pi)
NEG = -1.0e30


def columns(sizes):
    at, out = 0, {}
    for name, n in sizes:
        out[name] = (at, at + n)
        at += n
    return out, at


CONST, CONST_W = columns([
    ("decay", H * 3 * P), ("dft_c", 512), ("dft_s", 512), ("idft_c", 512), ("idft_s", 512),
    ("window", 512), ("rot_c", 128), ("rot_s", 128), ("mask_fw", P), ("mask_bw", P), ("before", P),
    ("iota", P), ("ident", P), ("ones", P), ("pos", 2 * L), ("pick", H * P),
    ("m0", 2), ("nm0", 2), ("halfpi", 1), ("lower", NE * NE)])

PAR, PAR_W = columns([
    ("conv", 10 * 4), ("hy_bias", 4), ("ret_gn", 2), ("ml_gn", 2), ("s5_d", 2),
    ("a_re", 16), ("a_im", 16), ("log_dt", 16), ("s5_c", 2 * 16 * 32), ("s5_b", 512), ("glu", 512),
    ("hy_w12", 64), ("hy_w3", 1024), ("hy_b1", 1), ("hy_b2", 1), ("hy_freq", 1),
    ("gate_w", KT * 16), ("gate_b", 16), ("router", KT * NE)])


def trunk(nc, x, ln, const, par, w_in, w_out, ffn, moe, tab, out):
    ctx = ExitStack()
    with ctx:
        def sb(name, shape, dt=F32):
            return ctx.enter_context(nc.sbuf_tensor(name, shape, dt))

        def sem(name):
            return ctx.enter_context(nc.semaphore(name))

        def bc(ap, axis, n):
            shape = list(ap.shape)
            shape.insert(axis, n)
            return ap.unsqueeze(axis).broadcast_to(shape)

        ring = [sb(f"ring{i}", [P, SLOT]) for i in range(SLOTS)]
        h = sb("h", [P, TT, D])
        lnb = sb("lnb", [P, 2 * D])
        cst = sb("cst", [P, CONST_W])
        pr = sb("pr", [P, PAR_W])
        hT = sb("hT", [P, KT, L])
        ret = sb("ret", [P, 2048])
        vo = sb("vo", [P, 1024])
        uT = sb("uT", [P, 2, L])
        cv = sb("cv", [P, 10, L])
        yT = sb("yT", [P, KT, L])
        spec = sb("spec", [P, 2, TT, 512])
        sc = sb("sc", [P, 2048])
        small = sb("small", [P, 360])
        over = sb("over", [P, 8], I32)
        bank = [ctx.enter_context(nc.psum_tensor(f"bank{i}", [P, 512], F32)) for i in range(8)]

        def K(name, rows=P):
            a, b = CONST[name]
            return cst[0:rows, a:b]

        def W(name, rows=P):
            a, b = PAR[name]
            return pr[0:rows, a:b]

        ident = K("ident")
        decay = K("decay").rearrange("p (h j) -> p h j", h=H)
        dft = [K(n).rearrange("p (t f) -> p t f", t=TT) for n in ("dft_c", "dft_s")]
        idft = [K(n).rearrange("p (t f) -> p t f", t=TT) for n in ("idft_c", "idft_s")]
        window = K("window").rearrange("p (t c) -> p t c", t=TT)
        rot = [K(n).rearrange("p (t c) -> p t c", t=TT) for n in ("rot_c", "rot_s")]
        z_feat = cst[64:97, CONST["pick"][0]:CONST["pick"][0] + L]
        w1_feat = pr[64:97, PAR["hy_w12"][0]:PAR["hy_w12"][1]]
        conv_w = W("conv").rearrange("p (t j) -> p t j", j=4)

        vg = ret[:, 0:1024].rearrange("p (t c) -> p t c", t=TT)
        qkT = ret[:, 1024:2048].rearrange("p (f n) -> p f n", f=4)
        lnf = lnb[:, :]
        rq = lnf[:, 0:1024].rearrange("p (t c) -> p t c", t=TT)
        rtmp = lnf[:, 1024:1536]
        cen = lnf[:, 0:512]
        sqr = lnf[:, 512:1024]
        ytm = lnf[:, 1024:1536].rearrange("p (t c) -> p t c", t=TT)
        st = sc[:, 512:1536].rearrange("p (b m n) -> p b m n", b=2, m=2)
        ztm = sc[:, 0:512].rearrange("p (t c) -> p t c", t=TT)
        hTf = hT[:, :, :].rearrange("p k n -> p (k n)")
        hy_t = [hTf[:, i * 512:(i + 1) * 512] for i in range(4)]
        g4 = hTf[0:H, 0:1024].rearrange("p (k n) -> p k n", k=4)
        lf = hTf[0:H, 1024:1536].rearrange("p (k n) -> p k n", k=2)
        ex = hTf[0:H, 1536:2048].rearrange("p (k n) -> p k n", k=2)
        acum = lnf[0:H, 0:512].rearrange("p (k n) -> p k n", k=2)
        brow = lnf[0:H, 512:1024].rearrange("p (k n) -> p k n", k=2)
        crow = lnf[0:H, 1024:1536].rearrange("p (k n) -> p k n", k=2)
        nmrow = lnf[0:H, 1536:2048].rearrange("p (k n) -> p k n", k=2)
        onerow = sc[0:H, 1792:2048]
        wmask = hTf[:, 0:1024].rearrange("p (q d b n) -> p q d b n", q=2, d=2, b=2)
        wml = sc[:, 256:1792].rearrange("p (q b n) -> p q b n", q=2, b=6)
        tabs = hTf.rearrange("p (b s d n) -> p b s d n", b=2, s=2, d=2)
        s5p = [ret[:, i * 1024:(i + 1) * 1024].rearrange("p (s d n) -> p s d n", s=2, d=2) for i in range(2)]
        s5x = [lnf[:, i * 1024:(i + 1) * 1024].rearrange("p (s d n) -> p s d n", s=2, d=2) for i in range(2)]
        s5y = sc[:, 0:512].rearrange("p (t c) -> p t c", t=TT)
        s5z = sc[:, 512:1024].rearrange("p (t n) -> p t n", t=2)
        s5s = sc[:, 1024:1536].rearrange("p (t n) -> p t n", t=2)
        cvf = cv[:, :, :].rearrange("p t n -> p (t n)")
        filt = ret[:, :].rearrange("p (t o d c) -> p t o d c", t=TT, o=2, d=2)
        fsq = vo[:, :].rearrange("p (o d c) -> p o d c", o=2, d=2)
        pm = cvf[:, 0:2048].rearrange("p (s t o c) -> p s t o c", s=2, t=TT, o=2)
        rnorm = cvf[:, 2048:2560]
        fx = [cvf[0:64, i * 256:(i + 1) * 256] for i in range(4)]
        yTf = yT[:, :, :].rearrange("p k n -> p (k n)")
        tst = yTf.rearrange("p (b s m) -> p b s m", b=2, s=2)
        tfr = uT[:, :, :].rearrange("p t n -> p (t n)")
        s5c = W("s5_c").rearrange("p (r j c) -> p r j c", r=2, c=32)
        ct = [yTf[:, i * 512:(i + 1) * 512].rearrange("p (j c) -> p j c", c=32) for i in range(4)]
        ncp = vo[:, 0:512].rearrange("p (j c) -> p j c", c=32)
        s5b = W("s5_b").rearrange("p (t r m) -> p t r m", t=2, r=2)

        def sm(a, n):
            return small[:, a:a + n]

        mv = sm(0, 4).rearrange("p (t s) -> p t s", t=2)
        bst = sm(4, 24).rearrange("p (t c s) -> p t c s", t=2, c=2)
        var, rstd = sm(28, 2), sm(30, 2)
        hmean, hvar, hrstd = sm(32, 8), sm(40, 8), sm(48, 8)
        gts = sm(56, 32).rearrange("p (t g) -> p t g", t=2)
        colsb = sm(88, 32)
        emm, den, rden = sm(120, 16), sm(136, 16), sm(152, 16)
        s5v = [sm(168 + 16 * i, 16) for i in range(11)]
        mexp = sm(344, 1)
        mhalf = sm(345, 8)
        rt = [vo[:, 16 * i:16 * i + 16].rearrange("p (t e) -> p t e", t=2) for i in range(8)]
        posx = vo[:, 128:160].rearrange("p (t e) -> p t e", t=2)
        comb = vo[:, 160:192].rearrange("p (t e) -> p t e", t=2)
        cmp1 = vo[:, 192:320].rearrange("p (t a b) -> p t a b", t=2, a=8)
        cmp2 = vo[:, 320:448].rearrange("p (t a b) -> p t a b", t=2, a=8)
        rt1 = vo[:, 448:456]
        sil = [sc[:, i * 256:(i + 1) * 256] for i in range(2)]
        mid = [sc[:, 512 + i * 256:768 + i * 256] for i in range(2)]
        onehot = sc[:, 1024:1280].rearrange("p (t s) -> p t s", t=2)
        gated = sc[:, 1280:1536].rearrange("p (t s) -> p t s", t=2)
        place = [sc[:, 1536 + i * 256:1792 + i * 256] for i in range(2)]
        acc = ret[:, :].rearrange("p (t d) -> p t d", t=2)
        xg = [cvf[:, i * 1024:(i + 1) * 1024].rearrange("p (k s) -> p k s", k=KT) for i in range(2)]
        yex = yTf[:, 0:1024]

        s_cst, s_x, s_par, s_ln = sem("const_in"), sem("x_in"), sem("params_in"), sem("ln_in")
        loaded = [sem(f"slot{i}_loaded") for i in range(SLOTS)]
        freed = sem("ring_freed")
        dch, ach, pch = sem("dve_chain"), sem("act_chain"), sem("pool_chain")
        ln_var, ln_rstd, h_ready, ht_ps, ht_ready = (
            sem("ln_var"), sem("ln_rstd"), sem("h_ready"), sem("ht_transposed"), sem("ht_ready"))
        mix_ready = sem("residual_psum")
        init = sem("init_done")
        f_mm, f_red, f_sin, f_raw, f_win, f_sq, f_sum, f_sqrt, f_pm, f_spm, f_spec = (
            sem("filt_mm"), sem("filt_reduced"), sem("filt_sin"), sem("filt_raw"), sem("filt_windowed"),
            sem("filt_squared"), sem("filt_norm_sum"), sem("filt_norm_sqrt"), sem("filt_plus_minus"),
            sem("filt_spec_mm"), sem("filt_spec"))
        c_dt, c_th, c_exp, c_cos = sem("s5_dt"), sem("s5_theta"), sem("s5_abs"), sem("s5_abar")
        t_ph, t_tab = sem("tab_phase"), sem("tab_sin")
        t_st = [sem(f"tab_stored{i}") for i in range(2)]
        s_tab = [sem(f"s5_table_in{i}") for i in range(2)]
        pj, u_ev, cv_c, cv_ev, rot_ev, vg_ev, vo_ev, gate_ev, silqk = (
            sem("proj_psum"), sem("u_evac"), sem("conv_centre"), sem("conv_done"), sem("rotary_done"),
            sem("ret_vg_ready"), sem("ml_vo_ready"), sem("gates_ready"), sem("ml_qk_ready"))
        z_tr, z_tm, z_sp, z_pr, z_iv, z_out = (
            sem("hy_z_transposed"), sem("hy_z_tm"), sem("hy_spec_psum"), sem("hy_product"),
            sem("hy_inverse"), sem("hy_z_ready"))
        r_tr, r_qk, r_s, r_st, r_o = (
            sem("ret_qk_transposed"), sem("ret_qkT"), sem("ret_scores"), sem("ret_decayed"), sem("ret_out"))
        n_var, n_rstd, n_y, n_tr, n_ev = (
            sem("hn_var"), sem("hn_rstd"), sem("hn_out"), sem("hn_transposed"), sem("hn_evac"))
        m_gt, m_g4, m_abs, m_exp, m_ln, m_rows, m_ct, m_cols, m_em, m_sc, m_msk, m_w, m_sw, m_nd = (
            sem("ml_gates_T"), sem("ml_gate_rows"), sem("ml_abs"), sem("ml_exp"), sem("ml_log"),
            sem("ml_rows"), sem("ml_cols_T"), sem("ml_cols"), sem("ml_floor"), sem("ml_scores"),
            sem("ml_masked"), sem("ml_weights"), sem("ml_weighted"), sem("ml_num_den"))
        b_mm, b_p, b_z, b_x, b_y, b_ysb, b_tr, b_v, b_g, b_glu, b_sig, b_out = (
            sem("s5_bu"), sem("s5_products"), sem("s5_scanned"), sem("s5_rotated"),
            sem("s5_y_psum"), sem("s5_y_tm"), sem("s5_y_transposed"), sem("s5_pre_gelu"),
            sem("s5_gelu"), sem("s5_glu_psum"), sem("s5_sigmoid"), sem("s5_out"))
        d_up, d_sil, d_mid = sem("ffn_up"), sem("ffn_silu"), sem("ffn_mid")
        q_lg, q_l, q_ex, q_sel, q_pos, q_px = (
            sem("router_logits"), sem("router_centred"), sem("router_exp"), sem("router_selected"),
            sem("router_pos_psum"), sem("router_done"))
        e_p, e_g, e_xg, e_tm, e_t, e_up, e_sil, e_mid, e_dn, e_y, e_sc, e_acc = (
            sem("ex_onehot"), sem("ex_gather_psum"), sem("ex_x"), sem("ex_place_psum"), sem("ex_place"),
            sem("ex_up"), sem("ex_silu"), sem("ex_mid"), sem("ex_down"), sem("ex_y"), sem("ex_scatter_psum"),
            sem("ex_accumulated"))
        s_out = sem("out_written")

        def slot_use(g):
            return g % SLOTS, 16 * (g // SLOTS + 1)

        def unit_evacuated(eng, l, i):
            if i == 0:
                eng.wait_ge(u_ev, l + 1)
            elif i < 6:
                eng.wait_ge(cv_ev, 5 * l + i)
            elif i < 8:
                eng.wait_ge(rot_ev, 2 * l + i - 5)
            elif i < 10:
                eng.wait_ge(vg_ev, 2 * l + i - 7)
            elif i < 12:
                eng.wait_ge(vo_ev, 2 * l + i - 9)

        NPRE = 21
        NLN = 5

        block = ctx.enter_context(nc.Block())

        @block.sync
        def _(sp):
            def load_slot(g, src, n=SLOT):
                s, _ = slot_use(g)
                if g >= SLOTS:
                    sp.wait_ge(freed, g - SLOTS + 1)
                sp.dma_start(ring[s][:, 0:n], src).then_inc(loaded[s], 16)

            def load_ln(n):
                if n:
                    sp.wait_ge(h_ready, n)
                sp.dma_start(lnb[:, :], ln[n]).then_inc(s_ln, 16)

            sp.dma_start(cst[:, :], const).then_inc(s_cst, 16)
            sp.dma_start(pr[:, :], par[0]).then_inc(s_par, 16)
            sp.dma_start(h[:, :, :], x.rearrange("(t p) d -> p t d", p=P)).then_inc(s_x, 16)
            load_ln(0)
            for l in range(DEPTH):
                g0 = l * G_MIX1
                for i in range(4):
                    load_slot(g0 + i, w_in[l, i])
                for i in range(2):
                    load_slot(g0 + 4 + i, w_out[l, i], KT * 512)
                for i in range(2):
                    if l == 0:
                        load_slot(G_FF + i, ffn[i])
                sp.wait_ge(n_y, 2 * l + 2)
                for q in range(2):
                    sp.wait_ge(t_st[q], 16 * 4 * (l + 1))
                for i in range(8):
                    if i >= 2:
                        sp.wait_ge(b_x, 2 * (8 * l + i - 1))
                    sp.dma_start(tabs[:, i % 2], tab[l, i].rearrange("p (s d n) -> p s d n", s=2, d=2)
                                 ).then_inc(s_tab[i % 2], 16)
                sp.wait_ge(b_y, 8 * (l + 1))
                load_ln(1 + 2 * l)
                if l == 0:
                    sp.wait_ge(b_out, 1)
                    sp.wait_ge(n_ev, 2)
                    sp.wait_ge(z_out, 2)
                    sp.dma_start(pr[:, :], par[1]).then_inc(s_par, 16)
                    for i in range(2, 4):
                        load_slot(G_FF + i, ffn[i])
                    load_ln(2)
                    for i in range(4, NC_FF):
                        load_slot(G_FF + i, ffn[i])
            for c in range(4):
                load_slot(G_MOE + c, moe[c])
            load_ln(4)
            for c in range(4, 2 * NC_E):
                load_slot(G_MOE + c, moe[c])

            def load_experts(first, g0):
                with sp.Fori(first, NE // 2) as i:
                    for c in range(2 * NC_E):
                        s, _ = slot_use(g0 + c)
                        sp.wait_ge(freed, i * (2 * NC_E) + (g0 + c - SLOTS + 1))
                        sp.dma_start(ring[s][:, :], moe[bass.ds(i * (2 * NC_E) + c, 1)].rearrange("a p n -> (a p) n")
                                     ).then_inc(loaded[s], 16)

            load_experts(1, G_MOE)
            sp.wait_ge(q_px, 1)
            crowded = sp.value_load(over[0:1, 0:1], min_val=0, max_val=1)
            with sp.If(crowded == 1):
                load_experts(0, G_MOE + NE * NC_E)
            sp.wait_ge(h_ready, NLN)
            sp.dma_start(out.rearrange("(t p) d -> p t d", p=P), h[:, :, :]).then_inc(s_out, 16)
            sp.wait_ge(s_out, 16)

        @block.gpsimd
        def _(po):
            nc.gpsimd.memset(mhalf, -0.5).then_inc(init, 1)
            po.wait_ge(init, 1)
            for n in range(NLN):
                if n in (1, 3):
                    for m in range(2):
                        k = n - 1 + m
                        po.wait_ge(n_var, k + 1)
                        nc.gpsimd.tensor_tensor(hrstd, hvar, mhalf, ALU.pow).then_inc(n_rstd, 1)
                po.wait_ge(ln_var, n + 1)
                nc.gpsimd.tensor_tensor(rstd, var, mhalf[:, 0:2], ALU.pow).then_inc(ln_rstd, 1)

        @block.tensor
        def _(pe):
            mm, tr = nc.tensor.matmul, nc.tensor.transpose

            def transposes_of_h(n):
                pe.wait_ge(h_ready, n + 1)
                for j in range(4):
                    for q in range(4):
                        k = 4 * (j % 2) + q
                        ins = tr(bank[j][:, q * P:(q + 1) * P], h[:, j // 2, k * P:(k + 1) * P], ident)
                    ins.then_inc(ht_ps, 1)

            def pre(l, k):
                if k == 0:
                    pe.wait_ge(s_par, 16 * (l + 1))
                    mm(bank[6][0:64, 0:L], w1_feat, z_feat, start=True, stop=True).then_inc(f_mm, 1)
                elif k == 1:
                    pe.wait_ge(f_sin, 2 * l + 1)
                    mm(bank[7][0:64, 0:L], W("hy_w12", 64), fx[3], start=True, stop=True).then_inc(f_mm, 1)
                elif k < 6:
                    j = k - 2
                    if j == 0:
                        pe.wait_ge(f_sin, 2 * l + 2)
                        pe.wait_ge(f_red, 2 * l + 2)
                    if j >= 2:
                        pe.wait_ge(f_win, 4 * l + j - 1)
                    mm(bank[6 + j % 2][:, :], fx[3][:, (j // 2) * P:(j // 2 + 1) * P],
                       W("hy_w3", 64)[:, (j % 2) * 512:(j % 2 + 1) * 512], start=True, stop=True).then_inc(f_raw, 1)
                elif k == 6:
                    pe.wait_ge(f_win, 4 * l + 4)
                    for t in range(TT):
                        pe.wait_ge(f_sq, 2 * l + t + 1)
                        for d in range(2):
                            ins = mm(bank[6][:, :], K("ones"), fsq2(t)[:, :, d, :], start=(t == 0 and d == 0),
                                     stop=(t == 1 and d == 1))
                    ins.then_inc(f_sum, 1)
                elif k < 11:
                    j = k - 7
                    pe.wait_ge(f_pm, l + 1)
                    pe.wait_ge(f_sqrt, l + 1)
                    if j >= 2:
                        pe.wait_ge(f_spec, 4 * l + j - 1)
                    s, ft = j // 2, j % 2
                    for t in range(TT):
                        ins = mm(bank[6 + (j + 1) % 2][:, :], dft[s][:, t, ft * P:(ft + 1) * P],
                                 pm[:, s, t].rearrange("p o c -> p (o c)"), start=(t == 0), stop=(t == 1))
                    ins.then_inc(f_spm, 1)

            def fsq2(t):
                return fsq if t == 0 else spec[:, 0].rearrange("p t n -> p (t n)").rearrange(
                    "p (o d c) -> p o d c", o=2, d=2)

            def project(l):
                g0 = l * G_MIX1
                pe.wait_ge(ht_ready, 8 * l + 4)
                for i in range(13):
                    b = bank[i % 4]
                    if i >= 4:
                        unit_evacuated(pe, l, i - 4)
                    if i in (0, 3, 6, 8, 10):
                        s, v = slot_use(g0 + {0: 0, 3: 1, 6: 2, 8: 3, 10: 3}[i])
                        pe.wait_ge(loaded[s], v)
                    if i < 6:
                        w = ring[(g0 + i // 3) % SLOTS][:, :].rearrange("p (k n) -> p k n", k=KT)
                        for q in range(2):
                            c = (2 * (i % 3) + q) * P
                            for k in range(KT):
                                ins = mm(b[:, q * L:(q + 1) * L], w[:, k, c:c + P], hT[:, k, :],
                                         start=(k == 0), stop=(k == KT - 1))
                    elif i < 12:
                        part, t = (i - 6) // 2, i % 2
                        w2 = [ring[(g0 + 2 + j) % SLOTS][:, :].rearrange("p (k n) -> p k n", k=KT) for j in range(2)]
                        pieces = [[(0, w2[0], 0, 512)], [(0, w2[0], 512, 256), (256, w2[1], 0, 256)],
                                  [(0, w2[1], 256, 512)]][part]
                        for o, w, c, n in pieces:
                            for k in range(KT):
                                ins = mm(b[:, o:o + n], hT[:, k, t * P:(t + 1) * P], w[:, k, c:c + n],
                                         start=(k == 0), stop=(k == KT - 1))
                    else:
                        gw = W("gate_w").rearrange("p (k n) -> p k n", k=KT)
                        for t in range(TT):
                            for k in range(KT):
                                ins = mm(b[:, t * 16:(t + 1) * 16], hT[:, k, t * P:(t + 1) * P], gw[:, k, :],
                                         start=(k == 0), stop=(k == KT - 1))
                    ins.then_inc(pj, 1)
                    if i in (2, 5, 9, 11):
                        pe.wait_ge(pj, 13 * l + i + 1)
                        pe.sem_inc(freed, 1)

            def hyena(l, n):
                u = 2 * l + n
                if n == 0:
                    pe.wait_ge(cv_ev, 5 * l + 3)
                    for i in range(9, 13):
                        unit_evacuated(pe, l, i)
                    pe.wait_ge(gate_ev, l + 1)
                else:
                    pe.wait_ge(z_out, 2 * l + 1)
                for t in range(TT):
                    for c in range(2):
                        src = cv[:, c, t * P:(t + 1) * P]
                        ins = tr(bank[0][:, t * DG + c * P:t * DG + (c + 1) * P], src, ident)
                ins.then_inc(z_tr, 1)
                pe.wait_ge(z_tm, u + 1)
                for s in range(2):
                    for ft in range(2):
                        for t in range(TT):
                            ins = mm(bank[1 + s][:, ft * DG:(ft + 1) * DG], dft[s][:, t, ft * P:(ft + 1) * P],
                                     ztm[:, t, :], start=(t == 0), stop=(t == 1))
                ins.then_inc(z_sp, 1)
                pe.wait_ge(z_pr, u + 1)
                for c in range(2):
                    for s in range(2):
                        for ft in range(2):
                            ins = mm(bank[3][:, c * L:(c + 1) * L],
                                     hy_t[2 * s][:, ft * DG + c * P:ft * DG + (c + 1) * P], idft[s][:, ft, :],
                                     start=(s == 0 and ft == 0), stop=(s == 1 and ft == 1))
                ins.then_inc(z_iv, 1)

            def head_out(m, b):
                pe.wait_ge(n_y, m + 1)
                for c in range(2):
                    for t in range(TT):
                        ins = tr(bank[b][:, c * L + t * P:c * L + (t + 1) * P], ytm[:, t, c * P:(c + 1) * P], ident)
                ins.then_inc(n_tr, 1)

            def retention(l):
                for half in range(2):
                    for q in range(2):
                        for t in range(TT):
                            pe.wait_ge(rot_ev, 2 * l + t + 1)
                            ft = 2 * half + q
                            ins = tr(bank[4 + half][:, q * L + t * P:q * L + (t + 1) * P],
                                     rq[:, t, ft * P:(ft + 1) * P], ident)
                    ins.then_inc(r_tr, 1)
                pe.wait_ge(r_qk, 2 * l + 2)
                pe.wait_ge(vg_ev, 2 * l + 2)

                def scores(a):
                    o = HD * (a % 2)
                    if a >= 2:
                        pe.wait_ge(r_st, 4 * l + a - 1)
                    for t in range(TT):
                        ins = mm(bank[6 + a % 2][:, t * L:(t + 1) * L], qkT[o:o + HD, 2 + a // 2, t * P:(t + 1) * P],
                                 qkT[o:o + HD, a // 2, :], start=True, stop=True)
                    ins.then_inc(r_s, 1)

                scores(0)
                for a in range(H):
                    if a + 1 < H:
                        scores(a + 1)
                    pe.wait_ge(r_st, 4 * l + a + 1)
                    for t in range(TT):
                        for m in range(TT):
                            ins = mm(bank[4][:, t * DG + a * HD:t * DG + (a + 1) * HD],
                                     st[:, a % 2, m, t * P:(t + 1) * P], vg[:, m, a * HD:(a + 1) * HD],
                                     start=(m == 0), stop=(m == 1))
                    if a == H - 1:
                        ins.then_inc(r_o, 1)
                head_out(2 * l, 5)

            def mlstm(l):
                pe.wait_ge(gate_ev, l + 1)
                pe.wait_ge(z_out, 2 * l + 2)
                for k in range(4):
                    for t in range(TT):
                        ins = tr(bank[6 + k // 2][0:H, (k % 2) * L + t * P:(k % 2) * L + (t + 1) * P],
                                 gts[:, t, 4 * k:4 * k + 4], ident)
                ins.then_inc(m_gt, 1)
                pe.wait_ge(m_rows, l + 1)
                for s, row in enumerate((brow, nmrow)):
                    for d in range(2):
                        for t in range(TT):
                            c = (s * 4 + d * 2 + t) * H
                            ins = tr(bank[6][:, c:c + H], row[:, d, t * P:(t + 1) * P], ident[0:H, 0:H])
                ins.then_inc(m_ct, 1)
                pe.wait_ge(silqk, 2 * l + 2)

                def scores(a):
                    o = HD * (a % 2)
                    if a >= 2:
                        pe.wait_ge(m_sw, 4 * l + a - 1)
                    for t in range(TT):
                        mm(bank[0 + a % 2][:, t * L:(t + 1) * L], cv[o:o + HD, 8 + a // 2, t * P:(t + 1) * P],
                           cv[o:o + HD, 6 + a // 2, :], start=True, stop=True)
                    for d in range(2):
                        ins = mm(bank[2 + a % 2][:, d * L:(d + 1) * L], K("pick", H)[:, a * P:(a + 1) * P],
                                 crow[:, d, :], start=True, stop=True)
                    ins.then_inc(m_sc, 1)

                scores(0)
                pe.wait_ge(m_cols, l + 1)
                pe.wait_ge(vo_ev, 2 * l + 2)
                ones = K("ones")[:, 0:1]
                for a in range(H):
                    if a + 1 < H:
                        scores(a + 1)
                    pe.wait_ge(m_sw, 4 * l + a + 1)
                    w = wml[:, a % 2]
                    for d in range(2):
                        for t in range(TT):
                            parts = [(w[:, 3 * d + t], t)]
                            if t == 1 - d:
                                parts.append((w[:, 3 * d + 2], d))
                            for j, (blk, m) in enumerate(parts):
                                s0, s1 = j == 0, j == len(parts) - 1
                                mm(bank[4 + d][:, t * DG + a * HD:t * DG + (a + 1) * HD], blk,
                                   vo[:, m * 512 + a * HD:m * 512 + (a + 1) * HD], start=s0, stop=s1)
                            for j, (blk, m) in enumerate(parts):
                                s0, s1 = j == 0, j == len(parts) - 1
                                c = (d * 2 + t) * H + a
                                ins = mm(bank[7][:, c:c + 1], blk, ones, start=s0, stop=s1)
                    if a == H - 1:
                        ins.then_inc(m_nd, 1)
                head_out(2 * l + 1, 6)

            def s5(l):
                def bu(i):
                    if i >= 2:
                        pe.wait_ge(b_p, 8 * l + i - 1)
                    r = 32 * (i % 4)
                    for s in range(2):
                        ins = mm(bank[i % 2][:, s * L:(s + 1) * L], s5b[r:r + 32, i // 4, s, :],
                                 uT[r:r + 32, i // 4, :], start=True, stop=True)
                    ins.then_inc(b_mm, 1)

                bu(0)
                for i in range(8):
                    if i + 1 < 8:
                        bu(i + 1)
                    pe.wait_ge(b_x, 2 * (8 * l + i + 1))
                    for t in range(TT):
                        n = 0
                        for d in range(2):
                            j = 2 * i + d
                            for xs, cs in ((s5x[0][:, 0], 0), (s5x[1][:, 1], 2), (s5x[0][:, 1], 1), (s5x[1][:, 0], 1)):
                                ins = mm(bank[2][:, t * DG + i * 32:t * DG + (i + 1) * 32],
                                         xs[:, d, t * P:(t + 1) * P], s5cp[cs][:, j, :], start=(n == 0), stop=(n == 7))
                                n += 1
                    ins.then_inc(b_y, 1)
                pe.wait_ge(b_ysb, l + 1)
                for c in range(2):
                    for t in range(TT):
                        ins = tr(bank[3][:, c * L + t * P:c * L + (t + 1) * P], s5y[:, t, c * P:(c + 1) * P], ident)
                ins.then_inc(b_tr, 1)
                pe.wait_ge(b_g, l + 1)
                wg = W("glu").rearrange("p (k n) -> p k n", k=2)
                for c in range(2):
                    for k in range(2):
                        ins = mm(bank[4][:, c * L:(c + 1) * L], wg[:, k, c * P:(c + 1) * P], s5z[:, k, :],
                                 start=(k == 0), stop=(k == 1))
                ins.then_inc(b_glu, 1)

            def out_projection(l):
                g0 = l * G_MIX1 + 4
                pe.wait_ge(n_ev, 2 * l + 2)
                pe.wait_ge(z_out, 2 * l + 2)
                pe.wait_ge(b_out, l + 1)
                for hf in range(2):
                    s, v = slot_use(g0 + hf)
                    pe.wait_ge(loaded[s], v)
                    w = ring[s][:, 0:KT * 512].rearrange("p (k n) -> p k n", k=KT)
                    for t in range(TT):
                        for k in range(KT):
                            ins = mm(bank[2 * t + hf][:, :], yT[:, k, t * P:(t + 1) * P], w[:, k, :],
                                     start=(k == 0), stop=(k == KT - 1))
                    ins.then_inc(freed, 1)
                pe.wait_ge(freed, g0 + 2)
                pe.sem_inc(mix_ready, 1)

            def dense():
                NU = 2 * NC_FF

                def up(u):
                    g = G_FF + u // 2
                    s, v = slot_use(g)
                    if u % 2 == 0:
                        pe.wait_ge(loaded[s], v)
                    for w in range(2):
                        wt = ring[s][:, w * KT * FC:(w + 1) * KT * FC].rearrange("p (k n) -> p k n", k=KT)
                        for k in range(KT):
                            ins = mm(bank[4 + u % 2][:, w * L:(w + 1) * L], wt[:, k, (u % 2) * P:(u % 2 + 1) * P],
                                     hT[:, k, :], start=(k == 0), stop=(k == KT - 1))
                    ins.then_inc(d_up, 1)

                def down(u):
                    s, _ = slot_use(G_FF + u // 2)
                    pe.wait_ge(d_mid, u + 1)
                    w2 = ring[s][:, 2 * KT * FC:].rearrange("p (f n) -> p f n", f=2)
                    for t in range(TT):
                        for hf in range(2):
                            ins = mm(bank[2 * t + hf][:, :], mid[u % 2][:, t * P:(t + 1) * P],
                                     w2[:, u % 2, hf * 512:(hf + 1) * 512], start=(u == 0), stop=(u == NU - 1))
                    if u % 2:
                        ins.then_inc(freed, 1)

                pe.wait_ge(ht_ready, 8)
                for u in range(NU):
                    up(u)
                    if u:
                        down(u - 1)
                    if u < NPRE:
                        pre(1, u)
                down(NU - 1)
                pe.wait_ge(freed, G_FF + NC_FF)
                pe.sem_inc(mix_ready, 1)

            s5cp = [W("s5_c").rearrange("p (r j c) -> p r j c", r=2, c=32)[:, 0],
                    W("s5_c").rearrange("p (r j c) -> p r j c", r=2, c=32)[:, 1],
                    ncp]

            pe.wait_ge(s_cst, 16)
            for k in range(NPRE):
                pre(0, k)
            transposes_of_h(0)
            for l in range(DEPTH):
                project(l)
                hyena(l, 0)
                retention(l)
                hyena(l, 1)
                mlstm(l)
                s5(l)
                out_projection(l)
                transposes_of_h(2 * l + 1)
                if l == 0:
                    dense()
                    transposes_of_h(2)

            pe.wait_ge(ht_ready, 16)
            rw = W("router").rearrange("p (k n) -> p k n", k=KT)
            for t in range(TT):
                for k in range(KT):
                    ins = mm(bank[6][:, t * NE:(t + 1) * NE], hT[:, k, t * P:(t + 1) * P], rw[:, k, :],
                             start=(k == 0), stop=(k == KT - 1))
            ins.then_inc(q_lg, 1)
            pe.wait_ge(q_sel, 1)
            sel = rt[1]
            mm(bank[7][:, 0:NE], K("before"), sel[:, 0, :], start=True, stop=True)
            mm(bank[7][:, NE:2 * NE], K("ones"), sel[:, 0, :], start=True, stop=False)
            mm(bank[7][:, NE:2 * NE], K("before"), sel[:, 1, :], start=False, stop=True)
            mm(bank[7][:, 2 * NE:3 * NE], K("ones"), sel[:, 0, :], start=True, stop=False)
            mm(bank[7][:, 2 * NE:3 * NE], K("ones"), sel[:, 1, :], start=False, stop=True).then_inc(q_pos, 1)

            def gather(v):
                pe.wait_ge(e_p, v + 1)
                for j in range(2):
                    for q in range(4):
                        k = 4 * j + q
                        for t in range(TT):
                            ins = mm(bank[6 + j][:, q * P:(q + 1) * P], h[:, t, k * P:(k + 1) * P],
                                     onehot[:, t, :], start=(t == 0), stop=(t == 1))
                    ins.then_inc(e_g, 1)

            def placing(v):
                pe.wait_ge(e_xg, v * 2 + 2)
                for t in range(TT):
                    ins = tr(bank[6][:, t * P:(t + 1) * P], gated[:, t, :], ident)
                ins.then_inc(e_tm, 1)

            def scatter(v, par, q0):
                if q0 == 0:
                    pe.wait_ge(e_y, v * 2 + 2)
                    pe.wait_ge(e_t, v + 1)
                for q in (q0, q0 + 1):
                    if q >= 2:
                        pe.wait_ge(e_acc, v * 4 + (q - 1))
                    mm(bank[6 + q % 2][:, :], place[par][:, (q // 2) * P:(q // 2 + 1) * P],
                       yex[:, (q % 2) * 512:(q % 2 + 1) * 512], start=True, stop=True).then_inc(e_sc, 1)

            def expert(v, n, j, loads):
                def up(c):
                    s = slot_use(G_MOE + j * NC_E + c)[0]
                    pe.wait_ge(loaded[s], loads(c))
                    for w in range(2):
                        wt = ring[s][:, w * KT * FC:(w + 1) * KT * FC].rearrange("p (k n) -> p k n", k=KT)
                        for f in range(2):
                            o = (2 * w + f) * P
                            for k in range(KT):
                                ins = mm(bank[4 + c % 2][:, o:o + P], wt[:, k, f * P:(f + 1) * P], xg[j][:, k, :],
                                         start=(k == 0), stop=(k == KT - 1))
                    ins.then_inc(e_up, 1)

                def down(c):
                    s = slot_use(G_MOE + j * NC_E + c)[0]
                    pe.wait_ge(e_mid, n * NC_E + (c + 1))
                    w2 = ring[s][:, 2 * KT * FC:].rearrange("p (f n) -> p f n", f=2)
                    for hf in range(2):
                        for f in range(2):
                            ins = mm(bank[2 * j + hf][:, :], mid[c % 2][:, f * P:(f + 1) * P],
                                     w2[:, f, hf * 512:(hf + 1) * 512], start=(c == 0 and f == 0),
                                     stop=(c == NC_E - 1 and f == 1))
                    ins.then_inc(freed, 1)
                    if c == NC_E - 1:
                        pe.wait_ge(freed, n * NC_E + (G_MOE + NC_E))
                        pe.sem_inc(e_dn, 1)

                pe.wait_ge(e_xg, v * 2 + 2)
                for c in range(NC_E):
                    up(c)
                    if c:
                        down(c - 1)
                    if c in (3, 5):
                        scatter(v, 1 - j, c - 3)
                    if c == 8:
                        pe.wait_ge(e_acc, v * 4 + 4)
                        gather(v + 1)
                    if c == 10:
                        placing(v + 1)
                down(NC_E - 1)

            def all_experts(b):
                v0, n0 = b * (NE + 1), b * NE
                gather(v0)
                placing(v0)
                with pe.Fori(0, NE // 2) as i:
                    for j in range(2):
                        def loads(c, j=j):
                            return i * (16 * 2 * NC_E // SLOTS) + slot_use(G_MOE + (n0 + j) * NC_E + c)[1]
                        expert(i * 2 + (v0 + j), i * 2 + (n0 + j), j, loads)
                scatter(v0 + NE, 1, 0)
                scatter(v0 + NE, 1, 2)

            all_experts(0)
            crowded = pe.value_load(over[0:1, 0:1], min_val=0, max_val=1)
            with pe.If(crowded == 1):
                all_experts(1)

        @block.scalar
        def _(ac):
            act = nc.scalar.activation

            def evacuate_h(n):
                for j in range(4):
                    ac.wait_ge(ht_ps, 4 * n + j + 1)
                    k = 4 * (j % 2)
                    act(hT[:, k:k + 4, (j // 2) * P:(j // 2 + 1) * P],
                        bank[j][:, :].rearrange("p (q n) -> p q n", q=4), ACT.Copy).then_inc(ht_ready, 1)

            def fsq2(t):
                return fsq if t == 0 else spec[:, 0].rearrange("p t n -> p (t n)").rearrange(
                    "p (o d c) -> p o d c", o=2, d=2)

            def pre(l, k):
                if k in (0, 1):
                    ac.wait_ge(f_red, 2 * l + k + 1)
                    act(fx[3], fx[2], ACT.Sin).then_inc(f_sin, 1)
                elif k in (3, 5):
                    t = (k - 3) // 2
                    ac.wait_ge(f_win, 4 * l + 2 * t + 2)
                    act(fsq2(t), filt[:, t], ACT.Square).then_inc(f_sq, 1)
                elif k == 6:
                    ac.wait_ge(f_sum, l + 1)
                    act(rnorm, bank[6][:, :], ACT.Sqrt).then_inc(f_sqrt, 1)
                elif k == 11:
                    ac.wait_ge(s_par, 16 * (l + 1))
                    act(s5v[0], W("log_dt"), ACT.Exp).then_inc(c_dt, 1)
                    ac.wait_ge(c_th, l + 1)
                    act(s5v[4], s5v[1], ACT.Exp).then_inc(c_exp, 1)
                    act(s5v[5], s5v[3], ACT.Abs).then_inc(ach, 1)
                    act(s5v[6], s5v[3], ACT.Sin, scale=TURN).then_inc(c_exp, 1)
                    ac.wait_ge(ach, l + 1)
                    act(s5v[7], s5v[5], ACT.Sin, scale=-TURN, bias=K("halfpi")).then_inc(c_exp, 1)
                elif 13 <= k < 21:
                    i = k - 13
                    v = 8 * l + i
                    ac.wait_ge(t_ph, v + 1)
                    if i >= 2:
                        ac.wait_ge(t_st[i % 2], 16 * (v // 2))
                    b = tst[:, i % 2]
                    act(b[:, 1], tfr, ACT.Sin, scale=TURN).then_inc(t_tab, 1)
                    act(b[:, 0], tfr, ACT.Abs).then_inc(t_tab, 1)
                    ac.wait_ge(t_tab, 3 * v + 2)
                    act(b[:, 0], b[:, 0], ACT.Sin, scale=-TURN, bias=K("halfpi")).then_inc(t_tab, 1)
                    ac.wait_ge(t_tab, 3 * v + 3)
                    ac.dma_start(tab[l, i].rearrange("p (s n) -> p s n", s=2), b).then_inc(t_st[i % 2], 16)

            def project(l):
                for q in range(2):
                    ac.wait_ge(t_st[q], 16 * 4 * (l + 1))
                ac.wait_ge(pj, 13 * l + 1)
                act(uT[:, :, :], bank[0][:, :].rearrange("p (t n) -> p t n", t=2), ACT.Copy).then_inc(u_ev, 1)
                for i in range(1, 6):
                    ac.wait_ge(pj, 13 * l + i + 1)
                    for q in range(2):
                        t = 2 * (i - 1) + q
                        act(cv[:, t, :], bank[i % 4][:, q * L:(q + 1) * L], ACT.Identity,
                            scale=conv_w[:, t, 1:2], bias=conv_w[:, t, 3:4]).then_inc(cv_c, 1)
                for t in range(TT):
                    ac.wait_ge(pj, 13 * l + 9 + t)
                    b = bank[(8 + t) % 4]
                    act(vg[:, t, 0:256], b[:, 0:256], ACT.Copy)
                    act(vg[:, t, 256:512], b[:, 256:512], ACT.Silu).then_inc(vg_ev, 1)
                for i in range(2):
                    ac.wait_ge(cv_ev, 5 * l + 4 + i)
                    act(cv[:, 6 + 2 * i:8 + 2 * i, :], cv[:, 6 + 2 * i:8 + 2 * i, :], ACT.Silu).then_inc(silqk, 1)
                for t in range(TT):
                    ac.wait_ge(pj, 13 * l + 11 + t)
                    b = bank[(10 + t) % 4]
                    act(vo[:, t * 512:t * 512 + 256], b[:, 0:256], ACT.Copy)
                    act(vo[:, t * 512 + 256:(t + 1) * 512], b[:, 256:512], ACT.Sigmoid).then_inc(vo_ev, 1)

            def hyena(l, n):
                u = 2 * l + n
                ac.wait_ge(z_tr, u + 1)
                act(sc[:, 0:512], bank[0][:, :], ACT.Copy).then_inc(z_tm, 1)

            def head_out(m, b, gn, k0):
                ac.wait_ge(n_tr, m + 1)
                for c in range(2):
                    ins = act(yT[:, k0 + c, :], bank[b][:, c * L:(c + 1) * L], ACT.Copy, scale=gn[:, c:c + 1])
                ins.then_inc(n_ev, 1)

            def retention(l):
                for half in range(2):
                    ac.wait_ge(r_tr, 2 * l + half + 1)
                    act(qkT[:, 2 * half:2 * half + 2, :], bank[4 + half][:, :].rearrange("p (q n) -> p q n", q=2),
                        ACT.Copy).then_inc(r_qk, 1)
                head_out(2 * l, 5, W("ret_gn"), 0)

            def mlstm(l):
                ac.wait_ge(m_gt, l + 1)
                for j in range(2):
                    act(g4[:, 2 * j:2 * j + 2, :], bank[6 + j][0:H, :].rearrange("p (k n) -> p k n", k=2),
                        ACT.Copy).then_inc(m_g4, 1)
                ac.wait_ge(m_abs, l + 1)
                act(ex, ex, ACT.Exp, scale=-1.0).then_inc(m_exp, 1)
                ac.wait_ge(m_exp, l + 1)
                act(ex, ex, ACT.Ln, bias=1.0).then_inc(m_ln, 1)
                ac.wait_ge(m_cols, l + 1)
                act(emm, colsb[:, 16:32], ACT.Exp).then_inc(m_em, 1)
                for a in range(H):
                    ac.wait_ge(m_sc, 4 * l + a + 1)
                    if a >= 2:
                        ac.wait_ge(m_sw, 4 * l + a - 1)
                    w, c = wml[:, a % 2], bank[2 + a % 2]
                    ac.wait_ge(m_msk, 4 * l + a + 1)
                    for d in range(2):
                        m, n = (0, 1) if d == 0 else (1, 0)
                        col = (d * 2 + m) * H + a
                        act(w[:, 3 * d + 2], c[:, d * L + n * P:d * L + (n + 1) * P], ACT.Exp, scale=-1.0,
                            bias=colsb[:, col:col + 1]).then_inc(m_w, 1)
                        for t in range(TT):
                            col = (d * 2 + t) * H + a
                            act(w[:, 3 * d + t], wmask[:, a % 2, d, t, :], ACT.Exp,
                                bias=colsb[:, col:col + 1]).then_inc(m_w, 1)
                head_out(2 * l + 1, 6, W("ml_gn"), 6)

            def s5(l):
                ac.wait_ge(b_y, 8 * (l + 1))
                act(sc[:, 0:512], bank[2][:, :], ACT.Copy).then_inc(b_ysb, 1)
                ac.wait_ge(b_v, l + 1)
                act(s5z, s5z, ACT.Gelu_apprx_tanh).then_inc(b_g, 1)
                ac.wait_ge(b_glu, l + 1)
                act(s5s, bank[4][:, :].rearrange("p (t n) -> p t n", t=2), ACT.Sigmoid).then_inc(b_sig, 1)

            ac.wait_ge(s_cst, 16)
            for k in range(NPRE):
                pre(0, k)
            evacuate_h(0)
            for l in range(DEPTH):
                project(l)
                hyena(l, 0)
                retention(l)
                hyena(l, 1)
                mlstm(l)
                s5(l)
                evacuate_h(2 * l + 1)
                if l == 0:
                    for u in range(2 * NC_FF):
                        ac.wait_ge(d_up, u + 1)
                        act(sil[u % 2], bank[4 + u % 2][:, 0:L], ACT.Silu).then_inc(d_sil, 1)
                        if u < NPRE:
                            pre(1, u)
                    evacuate_h(2)

            ac.wait_ge(q_l, 1)
            act(rt[2], rt[2], ACT.Exp).then_inc(q_ex, 1)

            def take_x(v, j):
                for q in range(2):
                    ac.wait_ge(e_g, v * 2 + (q + 1))
                    act(xg[j][:, 4 * q:4 * q + 4, :], bank[6 + q][:, :].rearrange("p (k s) -> p k s", k=4),
                        ACT.Copy).then_inc(e_xg, 1)

            def take_y(n, j):
                ac.wait_ge(e_dn, n)
                for q in range(2):
                    act(yex[:, q * 512:(q + 1) * 512], bank[2 * j + q][:, :], ACT.Copy).then_inc(e_y, 1)

            def expert(v, n, j):
                for c in range(NC_E):
                    ac.wait_ge(e_up, n * NC_E + (c + 1))
                    act(sil[c % 2], bank[4 + c % 2][:, 0:L], ACT.Silu).then_inc(e_sil, 1)
                    if c == 1:
                        take_y(n, 1 - j)
                    if c == 8:
                        take_x(v + 1, 1 - j)

            def all_experts(b):
                v0, n0 = b * (NE + 1), b * NE
                take_x(v0, 0)
                with ac.Fori(0, NE // 2) as i:
                    for j in range(2):
                        expert(i * 2 + (v0 + j), i * 2 + (n0 + j), j)
                take_y(n0 + NE, 1)

            all_experts(0)
            crowded = ac.value_load(over[0:1, 0:1], min_val=0, max_val=1)
            with ac.If(crowded == 1):
                all_experts(1)

        @block.vector
        def _(ve):
            tt, ts, stt = nc.vector.tensor_tensor, nc.vector.tensor_scalar, nc.vector.scalar_tensor_tensor
            count = [0]

            def link(ins):
                count[0] += 1
                ins.then_inc(dch, 1)
                ve.wait_ge(dch, count[0])

            def layer_norm(n):
                for t in range(TT):
                    for c in range(2):
                        ins = nc.vector.bn_stats(bst[:, t, c, :], h[:, t, c * 512:(c + 1) * 512])
                link(ins)
                for t in range(TT):
                    ins = nc.vector.bn_aggr(mv[:, t, :], bst[:, t].rearrange("p c s -> p (c s)"))
                link(ins)
                ts(var, mv[:, :, 1], EPS, None, ALU.add).then_inc(ln_var, 1)
                ve.wait_ge(ln_rstd, n + 1)
                for t in range(TT):
                    ins = ts(h[:, t, :], h[:, t, :], mv[:, t, 0:1], rstd[:, t:t + 1], ALU.subtract, ALU.mult)
                link(ins)
                ve.wait_ge(s_ln, 16 * (n + 1))
                link(tt(h[:, :, :], h[:, :, :], bc(lnb[:, 0:D], 1, TT), ALU.mult))
                tt(h[:, :, :], h[:, :, :], bc(lnb[:, D:2 * D], 1, TT), ALU.add).then_inc(h_ready, 1)

            def residual_psum(n):
                ve.wait_ge(mix_ready, n)
                for t in range(TT):
                    for c in range(2):
                        part = h[:, t, c * 512:(c + 1) * 512]
                        ins = stt(out=part, in0=part, scalar=ALPHA, in1=bank[2 * t + c][:, :], op0=ALU.mult, op1=ALU.add)
                link(ins)

            def pre(l, k):
                if k in (0, 1):
                    ve.wait_ge(f_mm, 2 * l + k + 1)
                    b = W("hy_b1" if k == 0 else "hy_b2", 64)
                    link(ts(fx[0], bank[6 + k][0:64, 0:L], b, W("hy_freq", 64), ALU.add, ALU.mult))
                    link(ts(fx[1], fx[0], INV2PI, MAGIC, ALU.mult, ALU.add))
                    link(ts(fx[1], fx[1], MAGIC, None, ALU.subtract))
                    link(stt(out=fx[2], in0=fx[1], scalar=-6.28125, in1=fx[0], op0=ALU.mult, op1=ALU.add))
                    link(stt(out=fx[2], in0=fx[1], scalar=-(2 * math.pi - 6.28125), in1=fx[2], op0=ALU.mult,
                             op1=ALU.add))
                    ts(fx[2], fx[2], 3.1415925, -3.1415925, ALU.min, ALU.max).then_inc(f_red, 1)
                elif k < 6:
                    j = k - 2
                    t, o = j // 2, j % 2
                    ve.wait_ge(f_raw, 4 * l + j + 1)
                    tt(filt[:, t, o], bank[6 + j % 2][:, :].rearrange("p (d c) -> p d c", d=2),
                       bc(window[:, t, :], 1, 2), ALU.mult).then_inc(f_win, 1)
                elif k == 6:
                    ve.wait_ge(f_win, 4 * l + 4)
                    for t in range(TT):
                        for s, m in enumerate(("m0", "nm0")):
                            ins = stt(out=pm[:, s, t], in0=filt[:, t, :, 1, :], scalar=K(m)[:, t:t + 1],
                                      in1=filt[:, t, :, 0, :], op0=ALU.mult, op1=ALU.add)
                    ins.then_inc(f_pm, 1)
                    ve.wait_ge(f_sqrt, l + 1)
                    link(nc.vector.reciprocal(rnorm, rnorm))
                elif k < 11:
                    j = k - 7
                    ve.wait_ge(f_spm, 4 * l + j + 1)
                    tt(spec[:, j // 2, j % 2, :], bank[6 + (j + 1) % 2][:, :], rnorm, ALU.mult).then_inc(f_spec, 1)
                elif k == 11:
                    dt_, x1, th, tf, rr, _, sn, cs, n1, n2, n3 = s5v
                    ve.wait_ge(s_par, 16 * (l + 1))
                    ve.wait_ge(c_dt, l + 1)
                    tt(x1, W("a_re"), dt_, ALU.mult)
                    link(tt(th, W("a_im"), dt_, ALU.mult))
                    link(ts(th, th, INV2PI, None, ALU.mult))
                    link(ts(tf, th, MAGIC, MAGIC, ALU.add, ALU.subtract))
                    tt(tf, th, tf, ALU.subtract).then_inc(c_th, 1)
                    ve.wait_ge(c_exp, 3 * l + 3)
                    tt(n1, rr, cs, ALU.mult)
                    link(tt(n2, rr, sn, ALU.mult))
                    link(ts(n1, n1, 1.0, None, ALU.subtract))
                    tt(sn, n1, W("a_re"), ALU.mult)
                    tt(cs, n2, W("a_im"), ALU.mult)
                    tt(dt_, n2, W("a_re"), ALU.mult)
                    tt(th, n1, W("a_im"), ALU.mult)
                    tt(n3, W("a_re"), W("a_re"), ALU.mult)
                    link(tt(x1, W("a_im"), W("a_im"), ALU.mult))
                    tt(n1, sn, cs, ALU.add)
                    tt(n2, dt_, th, ALU.subtract)
                    link(tt(n3, n3, x1, ALU.add))
                    link(nc.vector.reciprocal(n3, n3))
                    tt(n1, n1, n3, ALU.mult)
                    link(tt(n2, n2, n3, ALU.mult))
                elif k == 12:
                    n1, n2 = s5v[8], s5v[9]
                    cr, ci = s5c[:, 0], s5c[:, 1]
                    ct_ = [yTf[:, q * 512:(q + 1) * 512].rearrange("p (j c) -> p j c", c=32) for q in range(4)]
                    tt(ct_[0], cr, bc(n1, 2, 32), ALU.mult)
                    tt(ct_[1], ci, bc(n2, 2, 32), ALU.mult)
                    tt(ct_[2], cr, bc(n2, 2, 32), ALU.mult)
                    link(tt(ct_[3], ci, bc(n1, 2, 32), ALU.mult))
                    tt(cr, ct_[0], ct_[1], ALU.subtract)
                    link(stt(out=ci, in0=ct_[2], scalar=-1.0, in1=ct_[3], op0=ALU.mult, op1=ALU.subtract))
                elif k < 21:
                    i = k - 13
                    v = 8 * l + i
                    tf = s5v[3]
                    kk = cvf[:, 0:512]
                    ph = cvf[:, 512:1024]
                    pos = K("pos")
                    if i == 0:
                        ve.wait_ge(f_spec, 4 * l + 4)
                    else:
                        ve.wait_ge(t_ph, v)
                    for d in range(2):
                        ins = ts(ph[:, d * L:(d + 1) * L], pos[:, d * L:(d + 1) * L], tf[:, 2 * i + d:2 * i + d + 1],
                                 None, ALU.mult)
                    link(ins)
                    link(ts(kk, ph, MAGIC, MAGIC, ALU.add, ALU.subtract))
                    if i:
                        ve.wait_ge(t_tab, 3 * v)
                    tt(tfr, ph, kk, ALU.subtract).then_inc(t_ph, 1)

            def project(l):
                for i in range(1, 6):
                    ve.wait_ge(cv_c, 10 * l + 2 * i)
                    ve.wait_ge(pj, 13 * l + i + 1)
                    b = bank[i % 4]
                    for q in range(2):
                        t = 2 * (i - 1) + q
                        ins = stt(out=cv[:, t, 1:L], in0=b[:, q * L:q * L + L - 1], scalar=conv_w[:, t, 0:1],
                                  in1=cv[:, t, 1:L], op0=ALU.mult, op1=ALU.add)
                    link(ins)
                    for q in range(2):
                        t = 2 * (i - 1) + q
                        ins = stt(out=cv[:, t, 0:L - 1], in0=b[:, q * L + 1:(q + 1) * L], scalar=conv_w[:, t, 2:3],
                                  in1=cv[:, t, 0:L - 1], op0=ALU.mult, op1=ALU.add)
                    ins.then_inc(cv_ev, 1)
                for t in range(TT):
                    ve.wait_ge(pj, 13 * l + 7 + t)
                    b = bank[(6 + t) % 4][:, :]
                    tmp = rtmp.rearrange("p (g s c) -> p g s c", g=8, s=2)
                    b4 = b.rearrange("p (g s c) -> p g s c", g=8, s=2)
                    tt(rq[:, t, :].rearrange("p (g c) -> p g c", g=8), b.rearrange("p (g c) -> p g c", g=8),
                       bc(rot[0][:, t, :], 1, 8), ALU.mult)
                    for s in range(2):
                        ins = tt(tmp[:, :, s, :], b4[:, :, 1 - s, :], bc(rot[1][:, t, s * 32:(s + 1) * 32], 1, 8),
                                 ALU.mult)
                    link(ins)
                    ins = tt(rq[:, t, :], rq[:, t, :], rtmp, ALU.add)
                    ins.then_inc(rot_ev, 1)
                    ve.wait_ge(rot_ev, 2 * l + t + 1)
                ve.wait_ge(pj, 13 * l + 13)
                tt(gts, bank[12 % 4][:, 0:32].rearrange("p (t g) -> p t g", t=2), bc(W("gate_b"), 1, TT),
                   ALU.add).then_inc(gate_ev, 1)

            def hyena(l, n):
                u = 2 * l + n
                ve.wait_ge(z_sp, u + 1)
                if n == 0:
                    ve.wait_ge(f_spec, 4 * l + 4)
                kc, ks = (spec[:, s].rearrange("p t (o c) -> p t o c", o=2)[:, :, n, :] for s in range(2))
                t4 = [a.rearrange("p (t c) -> p t c", t=2) for a in hy_t]
                uc, us = (bank[1 + s][:, :].rearrange("p (t c) -> p t c", t=2) for s in range(2))
                tt(t4[0], uc, kc, ALU.mult)
                tt(t4[1], us, ks, ALU.mult)
                tt(t4[2], uc, ks, ALU.mult)
                link(tt(t4[3], us, kc, ALU.mult))
                tt(t4[0], t4[0], t4[1], ALU.subtract)
                tt(t4[2], t4[2], t4[3], ALU.add).then_inc(z_pr, 1)
                ve.wait_ge(z_iv, u + 1)
                for c in range(2):
                    ins = stt(out=cv[:, c, :], in0=cv[:, c, :], scalar=W("hy_bias")[:, 2 * n + c:2 * n + c + 1],
                              in1=bank[3][:, c * L:(c + 1) * L], op0=ALU.mult, op1=ALU.add)
                link(ins)
                dst = cv[:, 0:2, :] if n == 0 else yT[:, 4:6, :]
                tt(dst, cv[:, 0:2, :], cv[:, 2 + 2 * n:4 + 2 * n, :], ALU.mult).then_inc(z_out, 1)

            def head_norm(m, o, gate):
                c8, s8 = (a.rearrange("p (g c) -> p g c", g=8) for a in (cen, sqr))
                link(nc.vector.tensor_reduce(hmean, o, AX.X, ALU.add))
                link(ts(hmean, hmean, 1.0 / HD, None, ALU.mult))
                link(tt(c8, o, bc(hmean, 2, HD), ALU.subtract))
                link(tt(s8, c8, c8, ALU.mult))
                link(nc.vector.tensor_reduce(hvar, s8, AX.X, ALU.add))
                ts(hvar, hvar, 1.0 / HD, EPS, ALU.mult, ALU.add).then_inc(n_var, 1)
                ve.wait_ge(n_rstd, m + 1)
                link(tt(c8, c8, bc(hrstd, 2, HD), ALU.mult))
                tt(ytm, cen.rearrange("p (t c) -> p t c", t=2), gate, ALU.mult).then_inc(n_y, 1)

            def retention(l):
                for a in range(H):
                    ve.wait_ge(r_s, 4 * l + a + 1)
                    for m in range(TT):
                        ins = tt(st[:, a % 2, m, :], bank[6 + a % 2][:, m * L:(m + 1) * L],
                                 decay[:, a, P - P * m:P - P * m + L], ALU.mult)
                    ins.then_inc(r_st, 1)
                ve.wait_ge(r_o, l + 1)
                ve.wait_ge(r_qk, 2 * l + 2)
                head_norm(2 * l, bank[4][:, :].rearrange("p (g c) -> p g c", g=8), vg[:, :, 256:512])

            def mlstm(l):
                ve.wait_ge(m_g4, 2 * l + 2)
                ve.wait_ge(n_tr, 2 * l + 1)
                f = g4.rearrange("p (d k) n -> p d k n", k=2)[:, :, 1, :]
                i_ = g4.rearrange("p (d k) n -> p d k n", k=2)[:, :, 0, :]
                ts(lf, f, 0.0, None, ALU.min)
                stt(out=ex, in0=f, scalar=-1.0, in1=f, op0=ALU.mult, op1=ALU.max).then_inc(m_abs, 1)
                link(nc.vector.memset(onerow, 1.0))
                ve.wait_ge(m_ln, l + 1)
                link(tt(lf, lf, ex, ALU.subtract))
                scan = nc.vector.tensor_tensor_scan
                scan(acum[:, 0, :], onerow, lf[:, 0, :], 0.0, ALU.mult, ALU.add)
                link(scan(acum[:, 1, ::-1], onerow, lf[:, 1, ::-1], 0.0, ALU.mult, ALU.add))
                link(tt(brow, i_, acum, ALU.subtract))
                scan(crow[:, 0, :], onerow, brow[:, 0, :], 0.0, ALU.mult, ALU.max)
                link(scan(crow[:, 1, ::-1], onerow, brow[:, 1, ::-1], 0.0, ALU.mult, ALU.max))
                stt(out=nmrow, in0=acum, scalar=-1.0, in1=crow, op0=ALU.mult, op1=ALU.subtract).then_inc(m_rows, 1)
                ve.wait_ge(m_ct, l + 1)
                nc.vector.tensor_copy(colsb, bank[6][:, 0:32]).then_inc(m_cols, 1)

                def mask(a):
                    ve.wait_ge(m_sc, 4 * l + a + 1)
                    if a >= 2:
                        ve.wait_ge(m_w, 24 * l + 6 * a - 6)
                    for d in range(2):
                        ins = stt(out=wmask[:, a % 2, d],
                                  in0=bank[2 + a % 2][:, d * L:(d + 1) * L].rearrange("p (b n) -> p b n", b=2),
                                  scalar=-1.0, in1=bc(K("mask_fw" if d == 0 else "mask_bw"), 1, 2),
                                  op0=ALU.mult, op1=ALU.add)
                    ins.then_inc(m_msk, 1)

                mask(0)
                for a in range(H):
                    if a + 1 < H:
                        mask(a + 1)
                    w = wml[:, a % 2]
                    s4 = bank[0 + a % 2][:, :].rearrange("p (q n) -> p q n", q=4)
                    for d in range(2):
                        ve.wait_ge(m_w, 24 * l + 6 * a + 3 * d + 3)
                        stt(out=w[:, 3 * d:3 * d + 2], in0=s4[:, 0:4:3, :], scalar=HD ** -0.5,
                            in1=w[:, 3 * d:3 * d + 2], op0=ALU.mult, op1=ALU.mult)
                        q = 1 if d == 0 else 2
                        ins = stt(out=w[:, 3 * d + 2], in0=s4[:, q, :], scalar=HD ** -0.5, in1=w[:, 3 * d + 2],
                                  op0=ALU.mult, op1=ALU.mult)
                    ins.then_inc(m_sw, 1)
                ve.wait_ge(m_nd, l + 1)
                ve.wait_ge(m_em, l + 1)
                link(nc.vector.tensor_copy(rden, bank[7][:, 0:16]))
                link(stt(out=den, in0=rden, scalar=-1.0, in1=rden, op0=ALU.mult, op1=ALU.max))
                link(tt(den, den, emm, ALU.max))
                link(nc.vector.reciprocal(rden, den))
                hs = [sc[:, q * 512:(q + 1) * 512].rearrange("p (g c) -> p g c", g=8) for q in range(2)]
                for d in range(2):
                    ins = tt(hs[d], bank[4 + d][:, :].rearrange("p (g c) -> p g c", g=8),
                             bc(rden[:, 8 * d:8 * d + 8], 2, HD), ALU.mult)
                link(ins)
                link(tt(hs[0], hs[0], hs[1], ALU.add))
                head_norm(2 * l + 1, hs[0], vo[:, :].rearrange("p (t c) -> p t c", t=2)[:, :, 256:512])

            def s5(l):
                ve.wait_ge(n_tr, 2 * l + 2)
                link(ts(ncp, s5c[:, 0], -1.0, None, ALU.mult))
                rr = s5v[4]
                scan = nc.vector.tensor_tensor_scan
                for i in range(8):
                    v = 8 * l + i
                    T = tabs[:, i % 2]
                    T4 = T.rearrange("p s d n -> p (s d) n")
                    p1, p2 = s5p
                    x1, x2 = s5x
                    ve.wait_ge(b_mm, v + 1)
                    ve.wait_ge(s_tab[i % 2], 16 * (v // 2 + 1))
                    b = bank[i % 2]
                    tt(p1.rearrange("p s d n -> p (s d) n"), T4, bc(b[:, 0:L], 1, 4), ALU.mult)
                    tt(p2.rearrange("p s d n -> p (s d) n"), T4, bc(b[:, L:2 * L], 1, 4), ALU.mult).then_inc(b_p, 1)
                    ve.wait_ge(b_p, v + 1)
                    tt(p1[:, 0], p1[:, 0], p2[:, 1], ALU.add)
                    link(tt(p2[:, 0], p2[:, 0], p1[:, 1], ALU.subtract))
                    for d in range(2):
                        r = rr[:, 2 * i + d:2 * i + d + 1].broadcast_to([P, L])
                        for p in (p1, p2):
                            if d == 0:
                                ins = scan(p[:, 1, 0, :], r, p[:, 0, 0, :], 0.0, ALU.mult, ALU.add)
                            else:
                                ins = scan(p[:, 1, 1, ::-1], r, p[:, 0, 1, ::-1], 0.0, ALU.mult, ALU.add)
                    link(ins)
                    if i:
                        ve.wait_ge(b_y, v)
                    tt(x1, T, bc(p1[:, 1], 1, 2), ALU.mult).then_inc(b_x, 1)
                    tt(x2, T, bc(p2[:, 1], 1, 2), ALU.mult).then_inc(b_x, 1)
                    ve.wait_ge(b_x, 2 * (v + 1))
                ve.wait_ge(b_tr, l + 1)
                for c in range(2):
                    ins = stt(out=s5z[:, c, :], in0=uT[:, c, :], scalar=W("s5_d")[:, c:c + 1],
                              in1=bank[3][:, c * L:(c + 1) * L], op0=ALU.mult, op1=ALU.add)
                ins.then_inc(b_v, 1)
                ve.wait_ge(b_sig, l + 1)
                tt(yT[:, 2:4, :], s5z, s5s, ALU.mult).then_inc(b_out, 1)

            ve.wait_ge(s_cst, 16)
            for k in range(NPRE):
                pre(0, k)
            ve.wait_ge(s_x, 16)
            layer_norm(0)
            for l in range(DEPTH):
                ve.wait_ge(ht_ready, 8 * l + 4)
                project(l)
                hyena(l, 0)
                retention(l)
                hyena(l, 1)
                mlstm(l)
                s5(l)
                residual_psum(2 * l + 1)
                layer_norm(2 * l + 1)
                if l == 0:
                    for u in range(2 * NC_FF):
                        ve.wait_ge(d_sil, u + 1)
                        tt(mid[u % 2], sil[u % 2], bank[4 + u % 2][:, L:2 * L], ALU.mult).then_inc(d_mid, 1)
                        if u < NPRE:
                            pre(1, u)
                    residual_psum(2)
                    layer_norm(2)

            lg, sel, el = rt[0], rt[1], rt[2]
            ve.wait_ge(q_lg, 1)
            ve.wait_ge(mix_ready, 3)
            link(nc.vector.tensor_copy(lg, bank[6][:, 0:16].rearrange("p (t e) -> p t e", t=2)))
            link(nc.vector.tensor_reduce(rt1[:, 0:2], lg, AX.X, ALU.max))
            tt(el, lg, bc(rt1[:, 0:2], 2, NE), ALU.subtract).then_inc(q_l, 1)
            for t in range(TT):
                a, b = bc(lg[:, t, :], 1, NE), bc(lg[:, t, :], 2, NE)
                tt(cmp1[:, t], a, b, ALU.is_gt)
                ins = tt(cmp2[:, t], a, b, ALU.is_equal)
            link(ins)
            for t in range(TT):
                ins = tt(cmp2[:, t], cmp2[:, t], K("lower").rearrange("p (a b) -> p a b", a=NE), ALU.mult)
            link(ins)
            link(tt(cmp1, cmp1, cmp2, ALU.add))
            for t in range(TT):
                ins = nc.vector.tensor_reduce(rt[3][:, t, :], cmp1[:, t], AX.X, ALU.add)
            link(ins)
            ts(sel, rt[3], 1.5, None, ALU.is_lt).then_inc(q_sel, 1)
            ve.wait_ge(q_sel, 1)
            ve.wait_ge(q_ex, 1)
            link(tt(el, el, sel, ALU.mult))
            link(nc.vector.tensor_reduce(rt1[:, 2:4], el, AX.X, ALU.add))
            link(nc.vector.reciprocal(rt1[:, 4:6], rt1[:, 2:4]))
            link(nc.vector.memset(comb, 0.0))
            link(nc.vector.memset(posx, 4096.0))
            tt(comb[:, :, 0:NE], el, bc(rt1[:, 4:6], 2, NE), ALU.mult)
            ve.wait_ge(q_pos, 1)
            link(ts(rt[4], sel, -4096.0, 4096.0, ALU.mult, ALU.add))
            link(nc.vector.tensor_reduce(rt1[:, 6:7], bank[7][:, 16:24], AX.X, ALU.max))
            link(ts(over[:, 0:1], rt1[:, 6:7], P + 0.5, None, ALU.is_gt))
            tt(posx[:, :, 0:NE], rt[4], bank[7][:, 0:16].rearrange("p (t e) -> p t e", t=2), ALU.add).then_inc(q_px, 1)
            ve.wait_ge(q_px, 1)
            link(nc.vector.memset(acc, 0.0))

            def prepare(e):
                for t in range(TT):
                    ts(onehot[:, t, :], K("iota"), posx[:, t, bass.ds(e, 1)], None, ALU.is_equal)
                    ins = ts(gated[:, t, :], K("iota"), posx[:, t, bass.ds(e, 1)], comb[:, t, bass.ds(e, 1)],
                             ALU.is_equal, ALU.mult)
                ins.then_inc(e_p, 1)

            def placed(v, j):
                ve.wait_ge(e_tm, v + 1)
                nc.vector.tensor_copy(place[j], bank[6][:, 0:L]).then_inc(e_t, 1)

            def add(v, q0):
                for q in (q0, q0 + 1):
                    ve.wait_ge(e_sc, v * 4 + (q + 1))
                    part = acc[:, q // 2, (q % 2) * 512:(q % 2 + 1) * 512]
                    tt(part, part, bank[6 + q % 2][:, :], ALU.add).then_inc(e_acc, 1)

            def expert(e, v, n, j):
                for c in range(NC_E):
                    ve.wait_ge(e_sil, n * NC_E + (c + 1))
                    tt(mid[c % 2], sil[c % 2], bank[4 + c % 2][:, L:2 * L], ALU.mult).then_inc(e_mid, 1)
                    if c in (3, 5):
                        add(v, c - 3)
                    if c == 6:
                        ve.wait_ge(e_tm, v + 1)
                        prepare(e + 1)
                    if c == 10:
                        placed(v + 1, 1 - j)

            def all_experts(b):
                v0, n0 = b * (NE + 1), b * NE
                nc.vector.memset(place[1], 0.0).then_inc(q_px, 1)
                ve.wait_ge(q_px, 2 * b + 2)
                prepare(0)
                placed(v0, 0)
                with ve.Fori(0, NE // 2) as i:
                    for j in range(2):
                        expert(i * 2 + j, i * 2 + (v0 + j), i * 2 + (n0 + j), j)
                add(v0 + NE, 0)
                add(v0 + NE, 2)
                ve.wait_ge(e_acc, 4 * (v0 + NE) + 4)

            all_experts(0)
            crowded = ve.value_load(over[0:1, 0:1], min_val=0, max_val=1)
            with ve.If(crowded == 1):
                ts(posx, posx, float(P), None, ALU.subtract).then_inc(q_px, 1)
                ve.wait_ge(q_px, 3)
                all_experts(1)
            link(stt(out=h[:, :, :], in0=h[:, :, :], scalar=ALPHA, in1=acc, op0=ALU.mult, op1=ALU.add))
            layer_norm(4)


def constants():
    c = np.zeros((P, CONST_W), np.float64)

    def put(name, a, rows=P):
        s, e = CONST[name]
        c[0:rows, s:e] = np.asarray(a).reshape(rows, e - s)

    p = np.arange(P)
    tok = (np.arange(TT)[None, :] * P + p[:, None])
    gamma = 1.0 - 2.0 ** (-5.0 - np.arange(H))
    j = np.arange(3 * P)
    put("decay", gamma[None, :, None] ** np.abs(j[None, None, :] - P - p[:, None, None]) * HD ** -0.5)
    f = np.arange(L)
    for n, fn in (("c", np.cos), ("s", np.sin)):
        put("dft_" + n, fn(2 * np.pi * tok[:, :, None] * (f + 0.5) / (2 * L)))
        put("idft_" + n, fn(2 * np.pi * (tok[:, :, None] + 0.5) * f / (2 * L)) / L)
    rates = np.abs(np.linspace(math.log(1e-2) / 1.5, math.log(1e-2) / 0.3, DG))
    put("window", np.exp(-(tok[:, :, None] / (L - 1.0)) * rates))
    half = HD // 2
    ang = tok[:, :, None] * 10000.0 ** (-np.arange(half) / half)
    put("rot_c", np.concatenate([np.cos(ang), np.cos(ang)], -1))
    put("rot_s", np.concatenate([-np.sin(ang), np.sin(ang)], -1))
    put("mask_fw", np.where(p[:, None] <= p[None, :], 0.0, NEG))
    put("mask_bw", np.where(p[:, None] >= p[None, :], 0.0, NEG))
    put("before", p[:, None] < p[None, :])
    put("iota", np.tile(p, (P, 1)))
    put("ident", np.eye(P))
    put("ones", np.ones((P, P)))
    t = np.linspace(0.0, 1.0, L)
    w = 2 * np.pi * np.arange(L) / L
    bands = np.linspace(1e-4, 15, 16)
    put("pos", np.tile(np.stack([f, L - 1 - f]).reshape(1, -1), (P, 1)))
    put("pick", np.kron(np.eye(H), np.ones((1, P))), H)
    s, _ = CONST["pick"]
    c[64:97, s:s + L] = np.concatenate([t[None], np.cos(bands[:, None] * w), -np.sin(bands[:, None] * w)], 0)
    put("m0", tok != 0)
    put("nm0", -1.0 * (tok != 0))
    put("halfpi", np.full((P, 1), math.pi / 2 - 1e-7))
    e = np.arange(NE)
    put("lower", np.tile((e[None, :] < e[:, None]).reshape(1, -1), (P, 1)))
    return c.astype(np.float32)


def parameters(a):
    out = np.zeros((DEPTH, P, PAR_W), np.float32)
    for l in range(DEPTH):
        o = out[l]

        def put(name, v, rows=P):
            s, e = PAR[name]
            o[0:rows, s:e] = np.asarray(v).reshape(rows, e - s)

        cw = np.concatenate([a["hy_conv_w"][l], a["ml_conv_w"][l]], 1)
        cb = np.concatenate([a["hy_conv_b"][l], a["ml_conv_b"][l]])[None]
        put("conv", np.concatenate([cw, cb]).reshape(4, 10, P).transpose(2, 1, 0))
        put("hy_bias", a["hy_bias"][l].reshape(2, 2, P).transpose(2, 0, 1))
        for n, k in (("ret_gn", "ret_gn_w"), ("ml_gn", "ml_gn_w"), ("s5_d", "s5_d")):
            put(n, a[k][l].reshape(2, P).T)
        for n in ("a_re", "a_im"):
            put(n, a["s5_" + n][l].reshape(2, 8, P).transpose(2, 1, 0))
        dt = np.repeat(a["s5_log_dt"][l].reshape(2, 8, 2, 1), N_STATE, 3)
        put("log_dt", dt.reshape(2, 8, P).transpose(2, 1, 0))
        cc = np.zeros((2, N_STATE, 2, 8, 2, 2, S5_CH), np.float32)
        bb = np.zeros((4, 2, S5_CH, 2, 2, 2, N_STATE), np.float32)
        for r, n in enumerate(("re", "im")):
            cs = a["s5_c_" + n][l].reshape(2, 8, 2, S5_CH, N_STATE)
            bs = a["s5_b_" + n][l].reshape(2, 4, 2, N_STATE, S5_CH)
            for q in range(2):
                cc[q, :, r, :, :, q, :] = cs[:, :, q].transpose(3, 1, 0, 2)
                bb[:, q, :, :, r, q, :] = bs[:, :, q].transpose(1, 3, 0, 2)
        put("s5_c", cc)
        put("s5_b", bb)
        put("glu", a["s5_w_glu"][l].reshape(2, P, DG).transpose(1, 0, 2))
        put("hy_w12", a["hy_w2"][l], 64)
        s, e = PAR["hy_w12"]
        o[64:97, s:e] = a["hy_w1"][l]
        put("hy_w3", a["hy_w3"][l], 64)
        put("hy_b1", a["hy_b1"][l], 64)
        put("hy_b2", a["hy_b2"][l], 64)
        put("hy_freq", a["hy_freq"][l], 64)
        put("gate_w", a["w_in"][l][:, 3072:3088].reshape(KT, P, 16).transpose(1, 0, 2))
        gb = a["ml_gate_b"][l].reshape(1, 16)
        put("gate_b", np.broadcast_to(gb, (P, 16)))
        put("router", a["moe_router"][0].reshape(KT, P, NE).transpose(1, 0, 2))
    return out


def chunks(w1, w3, w2):
    n = w1.shape[1] // FC
    up = [w.reshape(KT, P, n, FC).transpose(2, 1, 0, 3).reshape(n, P, KT * FC) for w in (w1, w3)]
    down = w2.reshape(n, 2, P, D).transpose(0, 2, 1, 3).reshape(n, P, 2 * D)
    return np.concatenate(up + [down], 2)


def kernel(**inputs):
    import concourse.bacc as _bacc
    from concourse.bass_utils import run_bass_kernel_spmd as _run

    a = {k: np.asarray(v) for k, v in inputs.items()}
    w_in = np.stack([
        np.concatenate([a["w_in"][l][:, c0:c1] for c0, c1 in ((1024, 2560), (0, 1024), (2560, 3072))], 1)
        .reshape(KT, P, 4, WIN_COLS).transpose(2, 1, 0, 3).reshape(4, P, SLOT) for l in range(DEPTH)])
    w_out = np.stack([a["w_out"][l].reshape(KT, P, 2, 512).transpose(2, 1, 0, 3).reshape(2, P, KT * 512)
                      for l in range(DEPTH)])
    moe = np.empty((NE * NC_E, P, SLOT), np.float32)
    for e in range(NE):
        moe[e * NC_E:(e + 1) * NC_E] = chunks(a["moe_w1"][0, e], a["moe_w3"][0, e], a["moe_w2"][0, e])
    norms = [("ln_in_w", "ln_in_b", None)] + [(f"ln{k}_w", f"ln{k}_b", l) for l in range(DEPTH) for k in (1, 2)]
    rows = [np.concatenate([a[w] if l is None else a[w][l], a[b] if l is None else a[b][l]]) for w, b, l in norms]
    ln = np.broadcast_to(np.stack(rows)[:, None, :], (len(rows), P, 2 * D)).copy()
    arrays = {
        "x": a["x"].reshape(L, D), "ln": ln, "const": constants(), "par": parameters(a), "w_in": w_in,
        "w_out": w_out, "ffn": chunks(a["ffn_w1"][0], a["ffn_w3"][0], a["ffn_w2"][0]), "moe": moe}
    nc = _bacc.Bacc("TRN2", target_bir_lowering=False, num_devices=1)
    args = [nc.dram_tensor(n, list(v.shape), F32, kind="ExternalInput").ap() for n, v in arrays.items()]
    tab = nc.dram_tensor("tab", [DEPTH, 8, P, 4 * L], F32, kind="Internal").ap()
    out = nc.dram_tensor("out", [L, D], F32, kind="ExternalOutput").ap()
    trunk(nc, *args, tab, out)
    r = _run(nc, [arrays], core_ids=[0])
    return r.results[0]["out"].reshape(1, L, D)
```

```python
import math
from contextlib import ExitStack

import numpy as np
import concourse.bass as bass
from concourse import mybir

F32 = mybir.dt.float32
I32 = mybir.dt.int32
ALU = mybir.AluOpType
ACT = mybir.ActivationFunctionType
AX = mybir.AxisListType

P = 128
D = 1024
L = 256
TT = L // P
KT = D // P
DEPTH = 2
DG = 256
HD = 64
H = DG // HD
N_STATE = 64
S5_CH = 16
D_FF = 2816
D_FFE = 3584
NE = 8
EPS = 1e-5
ALPHA = (2 * DEPTH) ** 0.25
FC = 256
NC_FF = D_FF // FC
NC_E = D_FFE // FC
SLOTS = 4
SLOT = 3 * KT * FC
WIN_COLS = SLOT // KT
RING_MIX = 6
G_FF = RING_MIX
G_MIX1 = G_FF + NC_FF
G_MOE = G_MIX1 + RING_MIX
MAGIC = 12582912.0
TURN = 6.2831850
INV2PI = 1.0 / (2.0 * math.pi)
NEG = -1.0e30


def columns(sizes):
    at, out = 0, {}
    for name, n in sizes:
        out[name] = (at, at + n)
        at += n
    return out, at


CONST, CONST_W = columns([
    ("decay", H * 3 * P), ("dft_c", 512), ("dft_s", 512), ("idft_c", 512), ("idft_s", 512),
    ("window", 512), ("rot_c", 128), ("rot_s", 128), ("mask_fw", P), ("mask_bw", P), ("before", P),
    ("iota", P), ("ident", P), ("ones", P), ("pos", 2 * L), ("pick", H * P),
    ("m0", 2), ("nm0", 2), ("halfpi", 1), ("lower", NE * NE)])

PAR, PAR_W = columns([
    ("conv", 10 * 4), ("hy_bias", 4), ("ret_gn", 2), ("ml_gn", 2), ("s5_d", 2),
    ("a_re", 16), ("a_im", 16), ("log_dt", 16), ("s5_c", 2 * 16 * 32), ("s5_b", 512), ("glu", 512),
    ("hy_w12", 64), ("hy_w3", 1024), ("hy_b1", 1), ("hy_b2", 1), ("hy_freq", 1),
    ("gate_w", KT * 16), ("gate_b", 16), ("router", KT * NE)])


def trunk(nc, x, ln, const, par, w_in, w_out, ffn, moe, tab, out):
    ctx = ExitStack()
    with ctx:
        def sb(name, shape, dt=F32):
            return ctx.enter_context(nc.sbuf_tensor(name, shape, dt))

        def sem(name):
            return ctx.enter_context(nc.semaphore(name))

        def bc(ap, axis, n):
            shape = list(ap.shape)
            shape.insert(axis, n)
            return ap.unsqueeze(axis).broadcast_to(shape)

        ring = [sb(f"ring{i}", [P, SLOT]) for i in range(SLOTS)]
        h = sb("h", [P, TT, D])
        lnb = sb("lnb", [P, 2 * D])
        cst = sb("cst", [P, CONST_W])
        pr = sb("pr", [P, PAR_W])
        hT = sb("hT", [P, KT, L])
        ret = sb("ret", [P, 2048])
        vo = sb("vo", [P, 1024])
        uT = sb("uT", [P, 2, L])
        cv = sb("cv", [P, 10, L])
        yT = sb("yT", [P, KT, L])
        spec = sb("spec", [P, 2, TT, 512])
        sc = sb("sc", [P, 2048])
        small = sb("small", [P, 360])
        over = sb("over", [P, 8], I32)
        bank = [ctx.enter_context(nc.psum_tensor(f"bank{i}", [P, 512], F32)) for i in range(8)]

        def K(name, rows=P):
            a, b = CONST[name]
            return cst[0:rows, a:b]

        def W(name, rows=P):
            a, b = PAR[name]
            return pr[0:rows, a:b]

        ident = K("ident")
        decay = K("decay").rearrange("p (h j) -> p h j", h=H)
        dft = [K(n).rearrange("p (t f) -> p t f", t=TT) for n in ("dft_c", "dft_s")]
        idft = [K(n).rearrange("p (t f) -> p t f", t=TT) for n in ("idft_c", "idft_s")]
        window = K("window").rearrange("p (t c) -> p t c", t=TT)
        rot = [K(n).rearrange("p (t c) -> p t c", t=TT) for n in ("rot_c", "rot_s")]
        z_feat = cst[64:97, CONST["pick"][0]:CONST["pick"][0] + L]
        w1_feat = pr[64:97, PAR["hy_w12"][0]:PAR["hy_w12"][1]]
        conv_w = W("conv").rearrange("p (t j) -> p t j", j=4)

        vg = ret[:, 0:1024].rearrange("p (t c) -> p t c", t=TT)
        qkT = ret[:, 1024:2048].rearrange("p (f n) -> p f n", f=4)
        lnf = lnb[:, :]
        rq = lnf[:, 0:1024].rearrange("p (t c) -> p t c", t=TT)
        rtmp = lnf[:, 1024:1536]
        cen = lnf[:, 0:512]
        sqr = lnf[:, 512:1024]
        ytm = lnf[:, 1024:1536].rearrange("p (t c) -> p t c", t=TT)
        st = sc[:, 512:1536].rearrange("p (b m n) -> p b m n", b=2, m=2)
        ztm = sc[:, 0:512].rearrange("p (t c) -> p t c", t=TT)
        hTf = hT[:, :, :].rearrange("p k n -> p (k n)")
        hy_t = [hTf[:, i * 512:(i + 1) * 512] for i in range(4)]
        g4 = hTf[0:H, 0:1024].rearrange("p (k n) -> p k n", k=4)
        lf = hTf[0:H, 1024:1536].rearrange("p (k n) -> p k n", k=2)
        ex = hTf[0:H, 1536:2048].rearrange("p (k n) -> p k n", k=2)
        acum = lnf[0:H, 0:512].rearrange("p (k n) -> p k n", k=2)
        brow = lnf[0:H, 512:1024].rearrange("p (k n) -> p k n", k=2)
        crow = lnf[0:H, 1024:1536].rearrange("p (k n) -> p k n", k=2)
        nmrow = lnf[0:H, 1536:2048].rearrange("p (k n) -> p k n", k=2)
        onerow = sc[0:H, 1792:2048]
        wmask = hTf[:, 0:1024].rearrange("p (q d b n) -> p q d b n", q=2, d=2, b=2)
        wml = sc[:, 256:1792].rearrange("p (q b n) -> p q b n", q=2, b=6)
        def borrowed(l):
            return [ring[(l * G_MIX1 + RING_MIX + i) % SLOTS] for i in range(2)]

        def s5_table(l, i):
            a, b = borrowed(l)
            src = a[:, i * 1024:(i + 1) * 1024] if i < 6 else b[:, (i - 6) * 1024:(i - 5) * 1024]
            return src.rearrange("p (s d n) -> p s d n", s=2, d=2)

        def s5_work(l):
            b = borrowed(l)[1]
            v = [b[:, (2 + q) * 1024:(3 + q) * 1024].rearrange("p (s d n) -> p s d n", s=2, d=2) for q in range(4)]
            return v[0:2], v[2:4]

        s5y = sc[:, 0:512].rearrange("p (t c) -> p t c", t=TT)
        s5z = sc[:, 512:1024].rearrange("p (t n) -> p t n", t=2)
        s5s = sc[:, 1024:1536].rearrange("p (t n) -> p t n", t=2)
        cvf = cv[:, :, :].rearrange("p t n -> p (t n)")
        yTf = yT[:, :, :].rearrange("p k n -> p (k n)")
        tst = yTf.rearrange("p (b s m) -> p b s m", b=2, s=2)
        spec_half = [spec[:, s].rearrange("p t n -> p (t n)") for s in range(2)]
        work = [sc[:, :], cvf]
        filt_ = [a.rearrange("p (t o d c) -> p t o d c", t=TT, o=2, d=2) for a in (yTf, ret[:, :])]
        fsq_ = [[a.rearrange("p (o d c) -> p o d c", o=2, d=2) for a in b]
                for b in ((spec_half[1], spec_half[0]), (vo[:, :], spec_half[0]))]
        pm_ = [a[:, 0:2048].rearrange("p (s t o c) -> p s t o c", s=2, t=TT, o=2) for a in work]
        rnorm_ = [lnf[:, 1536:2048], cvf[:, 2048:2560]]
        fx_ = [[a[0:64, i * 256:(i + 1) * 256] for i in range(4)] for a in work]
        tfr_ = [sc[:, 1024:1536], uT[:, :, :].rearrange("p t n -> p (t n)")]
        ct_s = [[a[:, i * 512:(i + 1) * 512].rearrange("p (j c) -> p j c", c=32) for i in range(4)]
                for a in (sc, yTf)]
        s5c = W("s5_c").rearrange("p (r j c) -> p r j c", r=2, c=32)
        s5b = W("s5_b").rearrange("p (t r m) -> p t r m", t=2, r=2)

        def sm(a, n):
            return small[:, a:a + n]

        mv = sm(0, 4).rearrange("p (t s) -> p t s", t=2)
        bst = sm(4, 24).rearrange("p (t c s) -> p t c s", t=2, c=2)
        var, rstd = sm(28, 2), sm(30, 2)
        hmean, hvar, hrstd = sm(32, 8), sm(40, 8), sm(48, 8)
        gts = sm(56, 32).rearrange("p (t g) -> p t g", t=2)
        colsb = sm(88, 32)
        emm, den, rden = sm(120, 16), sm(136, 16), sm(152, 16)
        s5v = [sm(168 + 16 * i, 16) for i in range(11)]
        mexp = sm(344, 1)
        mhalf = sm(345, 8)
        rt = [vo[:, 16 * i:16 * i + 16].rearrange("p (t e) -> p t e", t=2) for i in range(8)]
        posx = vo[:, 128:160].rearrange("p (t e) -> p t e", t=2)
        comb = vo[:, 160:192].rearrange("p (t e) -> p t e", t=2)
        cmp1 = vo[:, 192:320].rearrange("p (t a b) -> p t a b", t=2, a=8)
        cmp2 = vo[:, 320:448].rearrange("p (t a b) -> p t a b", t=2, a=8)
        rt1 = vo[:, 448:456]
        sil = [sc[:, i * 256:(i + 1) * 256] for i in range(2)]
        mid = [sc[:, 512 + i * 256:768 + i * 256] for i in range(2)]
        onehot = sc[:, 1024:1280].rearrange("p (t s) -> p t s", t=2)
        gated = sc[:, 1280:1536].rearrange("p (t s) -> p t s", t=2)
        place = [sc[:, 1536 + i * 256:1792 + i * 256] for i in range(2)]
        acc = ret[:, :].rearrange("p (t d) -> p t d", t=2)
        xg = [cvf[:, i * 1024:(i + 1) * 1024].rearrange("p (k s) -> p k s", k=KT) for i in range(2)]
        yex = yTf[:, 0:1024]

        s_cst, s_x, s_par, s_ln = sem("const_in"), sem("x_in"), sem("params_in"), sem("ln_in")
        loaded = [sem(f"slot{i}_loaded") for i in range(SLOTS)]
        freed = sem("ring_freed")
        dch, ach, pch = sem("dve_chain"), sem("act_chain"), sem("pool_chain")
        ln_var, ln_rstd, h_ready, ht_ps, ht_ready = (
            sem("ln_var"), sem("ln_rstd"), sem("h_ready"), sem("ht_transposed"), sem("ht_ready"))
        mix_ready = sem("residual_psum")
        init = sem("init_done")
        f_mm, f_red, f_sin, f_raw, f_win, f_sq, f_sum, f_sqrt, f_pm, f_spm, f_spec = (
            sem("filt_mm"), sem("filt_reduced"), sem("filt_sin"), sem("filt_raw"), sem("filt_windowed"),
            sem("filt_squared"), sem("filt_norm_sum"), sem("filt_norm_sqrt"), sem("filt_plus_minus"),
            sem("filt_spec_mm"), sem("filt_spec"))
        c_dt, c_th, c_exp, c_cos = sem("s5_dt"), sem("s5_theta"), sem("s5_abs"), sem("s5_abar")
        t_ph, t_tab = sem("tab_phase"), sem("tab_sin")
        t_st = [sem(f"tab_stored{i}") for i in range(2)]
        s_tab = sem("s5_table_in")
        pj, u_ev, cv_c, cv_ev, rot_ev, vg_ev, vo_ev, gate_ev, silqk = (
            sem("proj_psum"), sem("u_evac"), sem("conv_centre"), sem("conv_done"), sem("rotary_done"),
            sem("ret_vg_ready"), sem("ml_vo_ready"), sem("gates_ready"), sem("ml_qk_ready"))
        z_tr, z_tm, z_sp, z_pr, z_iv, z_out = (
            sem("hy_z_transposed"), sem("hy_z_tm"), sem("hy_spec_psum"), sem("hy_product"),
            sem("hy_inverse"), sem("hy_z_ready"))
        r_tr, r_qk, r_s, r_st, r_o = (
            sem("ret_qk_transposed"), sem("ret_qkT"), sem("ret_scores"), sem("ret_decayed"), sem("ret_out"))
        n_var, n_rstd, n_y, n_tr, n_ev = (
            sem("hn_var"), sem("hn_rstd"), sem("hn_out"), sem("hn_transposed"), sem("hn_evac"))
        m_gt, m_g4, m_abs, m_exp, m_ln, m_rows, m_ct, m_cols, m_em, m_sc, m_msk, m_w, m_sw, m_nd = (
            sem("ml_gates_T"), sem("ml_gate_rows"), sem("ml_abs"), sem("ml_exp"), sem("ml_log"),
            sem("ml_rows"), sem("ml_cols_T"), sem("ml_cols"), sem("ml_floor"), sem("ml_scores"),
            sem("ml_masked"), sem("ml_weights"), sem("ml_weighted"), sem("ml_num_den"))
        b_mm, b_p, b_z, b_x, b_y, b_ysb, b_tr, b_v, b_g, b_glu, b_sig, b_out = (
            sem("s5_bu"), sem("s5_products"), sem("s5_scanned"), sem("s5_rotated"),
            sem("s5_y_psum"), sem("s5_y_tm"), sem("s5_y_transposed"), sem("s5_pre_gelu"),
            sem("s5_gelu"), sem("s5_glu_psum"), sem("s5_sigmoid"), sem("s5_out"))
        d_up, d_sil, d_mid = sem("ffn_up"), sem("ffn_silu"), sem("ffn_mid")
        q_lg, q_l, q_ex, q_sel, q_pos, q_px = (
            sem("router_logits"), sem("router_centred"), sem("router_exp"), sem("router_selected"),
            sem("router_pos_psum"), sem("router_done"))
        e_p, e_g, e_xg, e_tm, e_t, e_up, e_sil, e_mid, e_dn, e_y, e_sc, e_acc = (
            sem("ex_onehot"), sem("ex_gather_psum"), sem("ex_x"), sem("ex_place_psum"), sem("ex_place"),
            sem("ex_up"), sem("ex_silu"), sem("ex_mid"), sem("ex_down"), sem("ex_y"), sem("ex_scatter_psum"),
            sem("ex_accumulated"))
        s_out = sem("out_written")

        def slot_use(g):
            return g % SLOTS, 16 * (g // SLOTS + 1)

        def unit_evacuated(eng, l, i):
            if i == 0:
                eng.wait_ge(u_ev, l + 1)
            elif i < 6:
                eng.wait_ge(cv_ev, 5 * l + i)
            elif i < 8:
                eng.wait_ge(rot_ev, 2 * l + i - 5)
            elif i < 10:
                eng.wait_ge(vg_ev, 2 * l + i - 7)
            elif i < 12:
                eng.wait_ge(vo_ev, 2 * l + i - 9)

        NPRE = 21
        BESIDE = [(0,), (1,), (2, 3), (4, 5), (6,), (7, 8), (9, 10), (11,), (12,), (13, 14), (15, 16), (17, 18),
                  (19, 20)]
        NLN = 5

        block = ctx.enter_context(nc.Block())

        @block.sync
        def _(sp):
            def load_slot(g, src, n=SLOT):
                s, _ = slot_use(g)
                if g >= SLOTS:
                    sp.wait_ge(freed, g - SLOTS + 1)
                sp.dma_start(ring[s][:, 0:n], src).then_inc(loaded[s], 16)

            def load_ln(n):
                if n:
                    sp.wait_ge(h_ready, 2 * n)
                sp.dma_start(lnb[:, :], ln[n]).then_inc(s_ln, 16)

            sp.dma_start(cst[:, :], const).then_inc(s_cst, 16)
            sp.dma_start(pr[:, :], par[0]).then_inc(s_par, 16)
            sp.dma_start(h[:, :, :], x.rearrange("(t p) d -> p t d", p=P)).then_inc(s_x, 16)
            load_ln(0)
            for l in range(DEPTH):
                g0 = l * G_MIX1
                for i in range(4):
                    load_slot(g0 + i, w_in[l, i])
                for i in range(2):
                    load_slot(g0 + 4 + i, w_out[l, i], KT * 512)
                sp.wait_ge(freed, g0 + 4)
                for q in range(2):
                    sp.wait_ge(t_st[q], 16 * 4 * (l + 1))
                a, b = borrowed(l)
                sp.dma_start(a[:, :].rearrange("p (i m) -> p i m", i=6),
                             tab[l, 0:6].rearrange("i p m -> p i m")).then_inc(s_tab, 16)
                sp.dma_start(b[:, 0:2048].rearrange("p (i m) -> p i m", i=2),
                             tab[l, 6:8].rearrange("i p m -> p i m")).then_inc(s_tab, 16)
                sp.wait_ge(b_y, 8 * (l + 1))
                for i in range(2):
                    load_slot(g0 + RING_MIX + i, ffn[i] if l == 0 else moe[i])
                sp.wait_ge(n_tr, 2 * l + 2)
                load_ln(1 + 2 * l)
                if l == 0:
                    sp.wait_ge(b_out, 1)
                    sp.wait_ge(n_ev, 2)
                    sp.wait_ge(z_out, 2)
                    sp.dma_start(pr[:, :], par[1]).then_inc(s_par, 16)
                    for i in range(2, 4):
                        load_slot(G_FF + i, ffn[i])
                    load_ln(2)
                    for i in range(4, NC_FF):
                        load_slot(G_FF + i, ffn[i])
            for c in range(2, 4):
                load_slot(G_MOE + c, moe[c])
            load_ln(4)
            for c in range(4, 2 * NC_E):
                load_slot(G_MOE + c, moe[c])

            def load_experts(first, g0):
                with sp.Fori(first, NE // 2) as i:
                    for c in range(2 * NC_E):
                        s, _ = slot_use(g0 + c)
                        sp.wait_ge(freed, i * (2 * NC_E) + (g0 + c - SLOTS + 1))
                        sp.dma_start(ring[s][:, :], moe[bass.ds(i * (2 * NC_E) + c, 1)].rearrange("a p n -> (a p) n")
                                     ).then_inc(loaded[s], 16)

            load_experts(1, G_MOE)
            sp.wait_ge(q_px, 1)
            crowded = sp.value_load(over[0:1, 0:1], min_val=0, max_val=1)
            with sp.If(crowded == 1):
                load_experts(0, G_MOE + NE * NC_E)
            sp.wait_ge(h_ready, 2 * NLN)
            sp.dma_start(out.rearrange("(t p) d -> p t d", p=P), h[:, :, :]).then_inc(s_out, 16)
            sp.wait_ge(s_out, 16)

        @block.gpsimd
        def _(po):
            nc.gpsimd.memset(mhalf, -0.5).then_inc(init, 1)
            po.wait_ge(init, 1)
            for n in range(NLN):
                if n in (1, 3):
                    for m in range(2):
                        k = n - 1 + m
                        po.wait_ge(n_var, k + 1)
                        nc.gpsimd.tensor_tensor(hrstd, hvar, mhalf, ALU.pow).then_inc(n_rstd, 1)
                po.wait_ge(ln_var, n + 1)
                nc.gpsimd.tensor_tensor(rstd, var, mhalf[:, 0:2], ALU.pow).then_inc(ln_rstd, 1)

        @block.tensor
        def _(pe):
            mm, tr = nc.tensor.matmul, nc.tensor.transpose

            def transposes_of_h(n):
                for j in range(4):
                    pe.wait_ge(h_ready, 2 * n + j // 2 + 1)
                    for q in range(4):
                        k = 4 * (j % 2) + q
                        ins = tr(bank[j][:, q * P:(q + 1) * P], h[:, j // 2, k * P:(k + 1) * P], ident)
                    ins.then_inc(ht_ps, 1)

            def pre(l, k):
                fx, fsq, pm = fx_[l], fsq_[l], pm_[l]
                if k == 0:
                    pe.wait_ge(s_par, 16 * (l + 1))
                    mm(bank[6][0:64, 0:L], w1_feat, z_feat, start=True, stop=True).then_inc(f_mm, 1)
                elif k == 1:
                    pe.wait_ge(f_sin, 2 * l + 1)
                    mm(bank[7][0:64, 0:L], W("hy_w12", 64), fx[3], start=True, stop=True).then_inc(f_mm, 1)
                elif k < 6:
                    j = k - 2
                    if j == 0:
                        pe.wait_ge(f_sin, 2 * l + 2)
                        pe.wait_ge(f_red, 2 * l + 2)
                    if j >= 2:
                        pe.wait_ge(f_win, 4 * l + j - 1)
                    mm(bank[6 + j % 2][:, :], fx[3][:, (j // 2) * P:(j // 2 + 1) * P],
                       W("hy_w3", 64)[:, (j % 2) * 512:(j % 2 + 1) * 512], start=True, stop=True).then_inc(f_raw, 1)
                elif k == 6:
                    pe.wait_ge(f_win, 4 * l + 4)
                    for t in range(TT):
                        pe.wait_ge(f_sq, 2 * l + t + 1)
                        for d in range(2):
                            ins = mm(bank[6][:, :], K("ones"), fsq[t][:, :, d, :], start=(t == 0 and d == 0),
                                     stop=(t == 1 and d == 1))
                    ins.then_inc(f_sum, 1)
                elif k < 11:
                    j = k - 7
                    pe.wait_ge(f_pm, l + 1)
                    pe.wait_ge(f_sqrt, l + 1)
                    if j >= 2:
                        pe.wait_ge(f_spec, 4 * l + j - 1)
                    s, ft = j // 2, j % 2
                    for t in range(TT):
                        ins = mm(bank[6 + (j + 1) % 2][:, :], dft[s][:, t, ft * P:(ft + 1) * P],
                                 pm[:, s, t].rearrange("p o c -> p (o c)"), start=(t == 0), stop=(t == 1))
                    ins.then_inc(f_spm, 1)

            def project(l):
                g0 = l * G_MIX1
                pe.wait_ge(ht_ready, 8 * l + 4)
                for i in range(13):
                    b = bank[i % 4]
                    if i >= 4:
                        unit_evacuated(pe, l, i - 4)
                    if i in (0, 3, 6, 8, 10):
                        s, v = slot_use(g0 + {0: 0, 3: 1, 6: 2, 8: 3, 10: 3}[i])
                        pe.wait_ge(loaded[s], v)
                    if i < 6:
                        w = ring[(g0 + i // 3) % SLOTS][:, :].rearrange("p (k n) -> p k n", k=KT)
                        for q in range(2):
                            c = (2 * (i % 3) + q) * P
                            for k in range(KT):
                                ins = mm(b[:, q * L:(q + 1) * L], w[:, k, c:c + P], hT[:, k, :],
                                         start=(k == 0), stop=(k == KT - 1))
                    elif i < 12:
                        part, t = (i - 6) // 2, i % 2
                        w2 = [ring[(g0 + 2 + j) % SLOTS][:, :].rearrange("p (k n) -> p k n", k=KT) for j in range(2)]
                        pieces = [[(0, w2[0], 0, 512)], [(0, w2[0], 512, 256), (256, w2[1], 0, 256)],
                                  [(0, w2[1], 256, 512)]][part]
                        for o, w, c, n in pieces:
                            for k in range(KT):
                                ins = mm(b[:, o:o + n], hT[:, k, t * P:(t + 1) * P], w[:, k, c:c + n],
                                         start=(k == 0), stop=(k == KT - 1))
                    else:
                        gw = W("gate_w").rearrange("p (k n) -> p k n", k=KT)
                        for t in range(TT):
                            for k in range(KT):
                                ins = mm(b[:, t * 16:(t + 1) * 16], hT[:, k, t * P:(t + 1) * P], gw[:, k, :],
                                         start=(k == 0), stop=(k == KT - 1))
                    ins.then_inc(pj, 1)
                    if i in (2, 5, 9, 11):
                        pe.wait_ge(pj, 13 * l + i + 1)
                        pe.sem_inc(freed, 1)
                    if l == 0:
                        for k in BESIDE[i]:
                            pre(0, k)

            def hyena_forward(l, n):
                u = 2 * l + n
                pe.wait_ge(cv_ev, 5 * l + 3) if n == 0 else pe.wait_ge(z_out, 2 * l + 1)
                for t in range(TT):
                    for c in range(2):
                        src = cv[:, c, t * P:(t + 1) * P]
                        ins = tr(bank[0][:, t * DG + c * P:t * DG + (c + 1) * P], src, ident)
                ins.then_inc(z_tr, 1)
                pe.wait_ge(z_tm, u + 1)
                for s in range(2):
                    for ft in range(2):
                        for t in range(TT):
                            ins = mm(bank[1 + s][:, ft * DG:(ft + 1) * DG], dft[s][:, t, ft * P:(ft + 1) * P],
                                     ztm[:, t, :], start=(t == 0), stop=(t == 1))
                ins.then_inc(z_sp, 1)

            def hyena_inverse(l, n):
                pe.wait_ge(z_pr, 2 * l + n + 1)
                for c in range(2):
                    for s in range(2):
                        for ft in range(2):
                            ins = mm(bank[0][:, c * L:(c + 1) * L],
                                     hy_t[2 * s][:, ft * DG + c * P:ft * DG + (c + 1) * P], idft[s][:, ft, :],
                                     start=(s == 0 and ft == 0), stop=(s == 1 and ft == 1))
                ins.then_inc(z_iv, 1)

            def head_out(m, b):
                pe.wait_ge(n_y, m + 1)
                for c in range(2):
                    for t in range(TT):
                        ins = tr(bank[b][:, c * L + t * P:c * L + (t + 1) * P], ytm[:, t, c * P:(c + 1) * P], ident)
                ins.then_inc(n_tr, 1)

            def ret_transposes(l):
                for half in range(2):
                    for q in range(2):
                        for t in range(TT):
                            pe.wait_ge(rot_ev, 2 * l + t + 1)
                            ft = 2 * half + q
                            ins = tr(bank[4 + half][:, q * L + t * P:q * L + (t + 1) * P],
                                     rq[:, t, ft * P:(ft + 1) * P], ident)
                    ins.then_inc(r_tr, 1)
                pe.wait_ge(r_qk, 2 * l + 2)
                pe.wait_ge(vg_ev, 2 * l + 2)

            def ret_scores(l, a):
                o = HD * (a % 2)
                if a >= 2:
                    pe.wait_ge(r_st, 4 * l + a - 1)
                for t in range(TT):
                    ins = mm(bank[5 + a % 2][:, t * L:(t + 1) * L], qkT[o:o + HD, 2 + a // 2, t * P:(t + 1) * P],
                             qkT[o:o + HD, a // 2, :], start=True, stop=True)
                ins.then_inc(r_s, 1)

            def ret_out(l, a):
                pe.wait_ge(r_st, 4 * l + a + 1)
                for t in range(TT):
                    for m in range(TT):
                        ins = mm(bank[4][:, t * DG + a * HD:t * DG + (a + 1) * HD],
                                 st[:, a % 2, m, t * P:(t + 1) * P], vg[:, m, a * HD:(a + 1) * HD],
                                 start=(m == 0), stop=(m == 1))
                if a == H - 1:
                    ins.then_inc(r_o, 1)

            def ml_gate_rows(l):
                pe.wait_ge(n_ev, 2 * l + 1)
                for k in range(4):
                    for t in range(TT):
                        ins = tr(bank[5 + k // 2][0:H, (k % 2) * L + t * P:(k % 2) * L + (t + 1) * P],
                                 gts[:, t, 4 * k:4 * k + 4], ident)
                ins.then_inc(m_gt, 1)

            def ml_columns(l):
                pe.wait_ge(m_rows, l + 1)
                for s, row in enumerate((brow, nmrow)):
                    for d in range(2):
                        for t in range(TT):
                            c = (s * 4 + d * 2 + t) * H
                            ins = tr(bank[6][:, c:c + H], row[:, d, t * P:(t + 1) * P], ident[0:H, 0:H])
                ins.then_inc(m_ct, 1)
                pe.wait_ge(silqk, 2 * l + 2)

            def ml_scores(l, a):
                o = HD * (a % 2)
                if a >= 2:
                    pe.wait_ge(m_sw, 4 * l + a - 1)
                for t in range(TT):
                    mm(bank[a % 2][:, t * L:(t + 1) * L], cv[o:o + HD, 8 + a // 2, t * P:(t + 1) * P],
                       cv[o:o + HD, 6 + a // 2, :], start=True, stop=True)
                if a:
                    pe.wait_ge(m_w, 24 * l + 6 * a)
                for d in range(2):
                    ins = mm(bank[2][:, d * L:(d + 1) * L], K("pick", H)[:, a * P:(a + 1) * P],
                             crow[:, d, :], start=True, stop=True)
                ins.then_inc(m_sc, 1)

            def ml_out(l, a):
                if a == 0:
                    pe.wait_ge(m_cols, l + 1)
                    pe.wait_ge(vo_ev, 2 * l + 2)
                ones = K("ones")[:, 0:1]
                pe.wait_ge(m_sw, 4 * l + a + 1)
                w = wml[:, a % 2]
                for d in range(2):
                    for t in range(TT):
                        parts = [(w[:, 3 * d + t], t)]
                        if t == 1 - d:
                            parts.append((w[:, 3 * d + 2], d))
                        for j, (blk, m) in enumerate(parts):
                            s0, s1 = j == 0, j == len(parts) - 1
                            mm(bank[4 + d][:, t * DG + a * HD:t * DG + (a + 1) * HD], blk,
                               vo[:, m * 512 + a * HD:m * 512 + (a + 1) * HD], start=s0, stop=s1)
                        for j, (blk, m) in enumerate(parts):
                            s0, s1 = j == 0, j == len(parts) - 1
                            c = (d * 2 + t) * H + a
                            ins = mm(bank[6][:, c:c + 1], blk, ones, start=s0, stop=s1)
                if a == H - 1:
                    ins.then_inc(m_nd, 1)

            def s5_in(l, i):
                if i:
                    pe.wait_ge(b_p, 8 * l + i)
                r = 32 * (i % 4)
                for s in range(2):
                    ins = mm(bank[3][:, s * L:(s + 1) * L], s5b[r:r + 32, i // 4, s, :],
                             uT[r:r + 32, i // 4, :], start=True, stop=True)
                ins.then_inc(b_mm, 1)

            def s5_y(l, i):
                x1, x2 = s5_work(l)[1]
                pe.wait_ge(b_x, 2 * (8 * l + i + 1))
                for t in range(TT):
                    n = 0
                    for d in range(2):
                        for xs, part in ((x1[:, 0], 0), (x2[:, 1], 0), (x1[:, 1], 1), (x2[:, 0], 1)):
                            ins = mm(bank[7][:, t * DG + i * 32:t * DG + (i + 1) * 32],
                                     xs[:, d, t * P:(t + 1) * P], s5c[:, part, 2 * i + d, :],
                                     start=(n == 0), stop=(n == 7))
                            n += 1
                ins.then_inc(b_y, 1)

            def s5_beside(l, i):
                if i:
                    s5_y(l, i - 1)
                if i < 7:
                    s5_in(l, i + 1)

            def s5_transposes(l):
                pe.wait_ge(b_ysb, l + 1)
                for c in range(2):
                    for t in range(TT):
                        ins = tr(bank[5][:, c * L + t * P:c * L + (t + 1) * P], s5y[:, t, c * P:(c + 1) * P], ident)
                ins.then_inc(b_tr, 1)

            def s5_glu(l):
                pe.wait_ge(b_g, l + 1)
                wg = W("glu").rearrange("p (k n) -> p k n", k=2)
                for c in range(2):
                    for k in range(2):
                        ins = mm(bank[4][:, c * L:(c + 1) * L], wg[:, k, c * P:(c + 1) * P], s5z[:, k, :],
                                 start=(k == 0), stop=(k == 1))
                ins.then_inc(b_glu, 1)

            def out_projection(l, ks, first=False, last=False):
                g0 = l * G_MIX1 + 4
                for hf in range(2):
                    s, v = slot_use(g0 + hf)
                    if first:
                        pe.wait_ge(loaded[s], v)
                    w = ring[s][:, 0:KT * 512].rearrange("p (k n) -> p k n", k=KT)
                    for t in range(TT):
                        for k in ks:
                            ins = mm(bank[2 * t + hf][:, :], yT[:, k, t * P:(t + 1) * P], w[:, k, :],
                                     start=(first and k == ks[0]), stop=(last and k == ks[-1]))
                    if last:
                        ins.then_inc(freed, 1)
                if last:
                    pe.wait_ge(freed, g0 + 2)
                    pe.sem_inc(mix_ready, 1)

            def mixers(l):
                for i in range(9, 13):
                    unit_evacuated(pe, l, i)
                pe.wait_ge(gate_ev, l + 1)
                s5_in(l, 0)
                hyena_forward(l, 0)
                s5_beside(l, 0)
                hyena_inverse(l, 0)
                s5_beside(l, 1)
                ret_transposes(l)
                ret_scores(l, 0)
                ret_scores(l, 1)
                ret_out(l, 0)
                ret_scores(l, 2)
                ret_out(l, 1)
                ret_scores(l, 3)
                s5_beside(l, 2)
                ret_out(l, 2)
                ret_out(l, 3)
                s5_beside(l, 3)
                hyena_forward(l, 1)
                head_out(2 * l, 5)
                hyena_inverse(l, 1)
                ml_gate_rows(l)
                s5_beside(l, 4)
                s5_beside(l, 5)
                ml_columns(l)
                ml_scores(l, 0)
                s5_beside(l, 6)
                ml_scores(l, 1)
                ml_out(l, 0)
                ml_scores(l, 2)
                ml_out(l, 1)
                s5_beside(l, 7)
                ml_scores(l, 3)
                ml_out(l, 2)
                ml_out(l, 3)
                s5_y(l, 7)
                pe.wait_ge(z_out, 2 * l + 2)
                pe.wait_ge(m_sw, 4 * l + 4)
                pe.wait_ge(m_w, 24 * l + 24)
                pe.wait_ge(b_p, 8 * l + 8)
                out_projection(l, (0, 1, 4, 5), first=True)
                head_out(2 * l + 1, 6)
                s5_transposes(l)
                pe.wait_ge(n_ev, 2 * l + 2)
                out_projection(l, (6, 7))
                s5_glu(l)
                pe.wait_ge(b_out, l + 1)
                out_projection(l, (2, 3), last=True)

            def dense():
                NU = 2 * NC_FF

                def up(u):
                    g = G_FF + u // 2
                    s, v = slot_use(g)
                    if u % 2 == 0:
                        pe.wait_ge(loaded[s], v)
                    for w in range(2):
                        wt = ring[s][:, w * KT * FC:(w + 1) * KT * FC].rearrange("p (k n) -> p k n", k=KT)
                        for k in range(KT):
                            ins = mm(bank[4 + u % 2][:, w * L:(w + 1) * L], wt[:, k, (u % 2) * P:(u % 2 + 1) * P],
                                     hT[:, k, :], start=(k == 0), stop=(k == KT - 1))
                    ins.then_inc(d_up, 1)

                def down(u):
                    s, _ = slot_use(G_FF + u // 2)
                    pe.wait_ge(d_mid, u + 1)
                    w2 = ring[s][:, 2 * KT * FC:].rearrange("p (f n) -> p f n", f=2)
                    for t in range(TT):
                        for hf in range(2):
                            ins = mm(bank[2 * t + hf][:, :], mid[u % 2][:, t * P:(t + 1) * P],
                                     w2[:, u % 2, hf * 512:(hf + 1) * 512], start=(u == 0), stop=(u == NU - 1))
                    if u % 2:
                        ins.then_inc(freed, 1)

                pe.wait_ge(ht_ready, 8)
                for u in range(NU):
                    up(u)
                    if u:
                        down(u - 1)
                    if u < NPRE:
                        pre(1, u)
                down(NU - 1)
                pe.wait_ge(freed, G_FF + NC_FF)
                pe.sem_inc(mix_ready, 1)

            pe.wait_ge(s_cst, 16)
            transposes_of_h(0)
            for l in range(DEPTH):
                project(l)
                mixers(l)
                transposes_of_h(2 * l + 1)
                if l == 0:
                    dense()
                    transposes_of_h(2)

            pe.wait_ge(ht_ready, 16)
            rw = W("router").rearrange("p (k n) -> p k n", k=KT)
            for t in range(TT):
                for k in range(KT):
                    ins = mm(bank[6][:, t * NE:(t + 1) * NE], hT[:, k, t * P:(t + 1) * P], rw[:, k, :],
                             start=(k == 0), stop=(k == KT - 1))
            ins.then_inc(q_lg, 1)
            pe.wait_ge(q_sel, 1)
            sel = rt[1]
            mm(bank[7][:, 0:NE], K("before"), sel[:, 0, :], start=True, stop=True)
            mm(bank[7][:, NE:2 * NE], K("ones"), sel[:, 0, :], start=True, stop=False)
            mm(bank[7][:, NE:2 * NE], K("before"), sel[:, 1, :], start=False, stop=True)
            mm(bank[7][:, 2 * NE:3 * NE], K("ones"), sel[:, 0, :], start=True, stop=False)
            mm(bank[7][:, 2 * NE:3 * NE], K("ones"), sel[:, 1, :], start=False, stop=True).then_inc(q_pos, 1)

            def gather(v):
                pe.wait_ge(e_p, v + 1)
                for j in range(2):
                    for q in range(4):
                        k = 4 * j + q
                        for t in range(TT):
                            ins = mm(bank[6 + j][:, q * P:(q + 1) * P], h[:, t, k * P:(k + 1) * P],
                                     onehot[:, t, :], start=(t == 0), stop=(t == 1))
                    ins.then_inc(e_g, 1)

            def placing(v):
                pe.wait_ge(e_xg, v * 2 + 2)
                for t in range(TT):
                    ins = tr(bank[6][:, t * P:(t + 1) * P], gated[:, t, :], ident)
                ins.then_inc(e_tm, 1)

            def scatter(v, par, q0):
                if q0 == 0:
                    pe.wait_ge(e_y, v * 2 + 2)
                    pe.wait_ge(e_t, v + 1)
                for q in (q0, q0 + 1):
                    if q >= 2:
                        pe.wait_ge(e_acc, v * 4 + (q - 1))
                    mm(bank[6 + q % 2][:, :], place[par][:, (q // 2) * P:(q // 2 + 1) * P],
                       yex[:, (q % 2) * 512:(q % 2 + 1) * 512], start=True, stop=True).then_inc(e_sc, 1)

            def expert(v, n, j, loads):
                def up(c):
                    s = slot_use(G_MOE + j * NC_E + c)[0]
                    pe.wait_ge(loaded[s], loads(c))
                    for w in range(2):
                        wt = ring[s][:, w * KT * FC:(w + 1) * KT * FC].rearrange("p (k n) -> p k n", k=KT)
                        for f in range(2):
                            o = (2 * w + f) * P
                            for k in range(KT):
                                ins = mm(bank[4 + c % 2][:, o:o + P], wt[:, k, f * P:(f + 1) * P], xg[j][:, k, :],
                                         start=(k == 0), stop=(k == KT - 1))
                    ins.then_inc(e_up, 1)

                def down(c):
                    s = slot_use(G_MOE + j * NC_E + c)[0]
                    pe.wait_ge(e_mid, n * NC_E + (c + 1))
                    w2 = ring[s][:, 2 * KT * FC:].rearrange("p (f n) -> p f n", f=2)
                    for hf in range(2):
                        for f in range(2):
                            ins = mm(bank[2 * j + hf][:, :], mid[c % 2][:, f * P:(f + 1) * P],
                                     w2[:, f, hf * 512:(hf + 1) * 512], start=(c == 0 and f == 0),
                                     stop=(c == NC_E - 1 and f == 1))
                    ins.then_inc(freed, 1)
                    if c == NC_E - 1:
                        pe.wait_ge(freed, n * NC_E + (G_MOE + NC_E))
                        pe.sem_inc(e_dn, 1)

                pe.wait_ge(e_xg, v * 2 + 2)
                for c in range(NC_E):
                    up(c)
                    if c:
                        down(c - 1)
                    if c in (3, 5):
                        scatter(v, 1 - j, c - 3)
                    if c == 8:
                        pe.wait_ge(e_acc, v * 4 + 4)
                        gather(v + 1)
                    if c == 10:
                        placing(v + 1)
                down(NC_E - 1)

            def all_experts(b):
                v0, n0 = b * (NE + 1), b * NE
                gather(v0)
                placing(v0)
                with pe.Fori(0, NE // 2) as i:
                    for j in range(2):
                        def loads(c, j=j):
                            return i * (16 * 2 * NC_E // SLOTS) + slot_use(G_MOE + (n0 + j) * NC_E + c)[1]
                        expert(i * 2 + (v0 + j), i * 2 + (n0 + j), j, loads)
                scatter(v0 + NE, 1, 0)
                scatter(v0 + NE, 1, 2)

            all_experts(0)
            crowded = pe.value_load(over[0:1, 0:1], min_val=0, max_val=1)
            with pe.If(crowded == 1):
                all_experts(1)

        @block.scalar
        def _(ac):
            act = nc.scalar.activation

            def evacuate_h(n):
                for j in range(4):
                    ac.wait_ge(ht_ps, 4 * n + j + 1)
                    k = 4 * (j % 2)
                    act(hT[:, k:k + 4, (j // 2) * P:(j // 2 + 1) * P],
                        bank[j][:, :].rearrange("p (q n) -> p q n", q=4), ACT.Copy).then_inc(ht_ready, 1)

            def pre(l, k):
                fx, fsq, filt, rnorm, tfr = fx_[l], fsq_[l], filt_[l], rnorm_[l], tfr_[l]
                if k in (0, 1):
                    ac.wait_ge(f_red, 2 * l + k + 1)
                    act(fx[3], fx[2], ACT.Sin).then_inc(f_sin, 1)
                elif k in (3, 5):
                    t = (k - 3) // 2
                    ac.wait_ge(f_win, 4 * l + 2 * t + 2)
                    act(fsq[t], filt[:, t], ACT.Square).then_inc(f_sq, 1)
                elif k == 6:
                    ac.wait_ge(f_sum, l + 1)
                    act(rnorm, bank[6][:, :], ACT.Sqrt).then_inc(f_sqrt, 1)
                elif k == 11:
                    ac.wait_ge(s_par, 16 * (l + 1))
                    act(s5v[0], W("log_dt"), ACT.Exp).then_inc(c_dt, 1)
                    ac.wait_ge(c_th, l + 1)
                    act(s5v[4], s5v[1], ACT.Exp).then_inc(c_exp, 1)
                    act(s5v[5], s5v[3], ACT.Abs).then_inc(ach, 1)
                    act(s5v[6], s5v[3], ACT.Sin, scale=TURN).then_inc(c_exp, 1)
                    ac.wait_ge(ach, l + 1)
                    act(s5v[7], s5v[5], ACT.Sin, scale=-TURN, bias=K("halfpi")).then_inc(c_exp, 1)
                elif 13 <= k < 21:
                    i = k - 13
                    v = 8 * l + i
                    ac.wait_ge(t_ph, v + 1)
                    if i >= 2:
                        ac.wait_ge(t_st[i % 2], 16 * (v // 2))
                    b = tst[:, i % 2]
                    act(b[:, 1], tfr, ACT.Sin, scale=TURN).then_inc(t_tab, 1)
                    act(b[:, 0], tfr, ACT.Abs).then_inc(t_tab, 1)
                    ac.wait_ge(t_tab, 3 * v + 2)
                    act(b[:, 0], b[:, 0], ACT.Sin, scale=-TURN, bias=K("halfpi")).then_inc(t_tab, 1)
                    ac.wait_ge(t_tab, 3 * v + 3)
                    ac.dma_start(tab[l, i].rearrange("p (s n) -> p s n", s=2), b).then_inc(t_st[i % 2], 16)

            def project(l):
                for i in range(13):
                    b = bank[i % 4]
                    if i == 0:
                        ac.wait_ge(pj, 13 * l + 1)
                        act(uT[:, :, :], b[:, :].rearrange("p (t n) -> p t n", t=2), ACT.Copy).then_inc(u_ev, 1)
                    elif i < 6:
                        ac.wait_ge(pj, 13 * l + i + 1)
                        for q in range(2):
                            t = 2 * (i - 1) + q
                            act(cv[:, t, :], b[:, q * L:(q + 1) * L], ACT.Identity,
                                scale=conv_w[:, t, 1:2], bias=conv_w[:, t, 3:4]).then_inc(cv_c, 1)
                    elif i < 8:
                        ac.wait_ge(cv_ev, 5 * l + i - 2)
                        j = 6 + 2 * (i - 6)
                        act(cv[:, j:j + 2, :], cv[:, j:j + 2, :], ACT.Silu).then_inc(silqk, 1)
                    elif i < 10:
                        ac.wait_ge(pj, 13 * l + i + 1)
                        t = i - 8
                        act(vg[:, t, 0:256], b[:, 0:256], ACT.Copy)
                        act(vg[:, t, 256:512], b[:, 256:512], ACT.Silu).then_inc(vg_ev, 1)
                    elif i < 12:
                        ac.wait_ge(pj, 13 * l + i + 1)
                        t = i - 10
                        act(vo[:, t * 512:t * 512 + 256], b[:, 0:256], ACT.Copy)
                        act(vo[:, t * 512 + 256:(t + 1) * 512], b[:, 256:512], ACT.Sigmoid).then_inc(vo_ev, 1)
                    if l == 0:
                        for k in BESIDE[i]:
                            pre(0, k)

            def hyena(l, n):
                u = 2 * l + n
                ac.wait_ge(z_tr, u + 1)
                act(sc[:, 0:512], bank[0][:, :], ACT.Copy).then_inc(z_tm, 1)

            def head_out(m, b, gn, k0):
                ac.wait_ge(n_tr, m + 1)
                for q in range(2):
                    ac.wait_ge(t_st[q], 16 * 4 * (m // 2 + 1))
                for c in range(2):
                    ins = act(yT[:, k0 + c, :], bank[b][:, c * L:(c + 1) * L], ACT.Copy, scale=gn[:, c:c + 1])
                ins.then_inc(n_ev, 1)

            def ret_qk(l):
                for half in range(2):
                    ac.wait_ge(r_tr, 2 * l + half + 1)
                    act(qkT[:, 2 * half:2 * half + 2, :], bank[4 + half][:, :].rearrange("p (q n) -> p q n", q=2),
                        ACT.Copy).then_inc(r_qk, 1)
            def mlstm(l):
                ac.wait_ge(m_gt, l + 1)
                for j in range(2):
                    act(g4[:, 2 * j:2 * j + 2, :], bank[5 + j][0:H, :].rearrange("p (k n) -> p k n", k=2),
                        ACT.Copy).then_inc(m_g4, 1)
                ac.wait_ge(m_abs, l + 1)
                act(ex, ex, ACT.Exp, scale=-1.0).then_inc(m_exp, 1)
                ac.wait_ge(m_exp, l + 1)
                act(ex, ex, ACT.Ln, bias=1.0).then_inc(m_ln, 1)
                ac.wait_ge(m_cols, l + 1)
                act(emm, colsb[:, 16:32], ACT.Exp).then_inc(m_em, 1)
                for a in range(H):
                    ac.wait_ge(m_sc, 4 * l + a + 1)
                    if a >= 2:
                        ac.wait_ge(m_sw, 4 * l + a - 1)
                    w, c = wml[:, a % 2], bank[2]
                    ac.wait_ge(m_msk, 4 * l + a + 1)
                    for d in range(2):
                        m, n = (0, 1) if d == 0 else (1, 0)
                        col = (d * 2 + m) * H + a
                        act(w[:, 3 * d + 2], c[:, d * L + n * P:d * L + (n + 1) * P], ACT.Exp, scale=-1.0,
                            bias=colsb[:, col:col + 1]).then_inc(m_w, 1)
                        for t in range(TT):
                            col = (d * 2 + t) * H + a
                            act(w[:, 3 * d + t], wmask[:, a % 2, d, t, :], ACT.Exp,
                                bias=colsb[:, col:col + 1]).then_inc(m_w, 1)
                head_out(2 * l + 1, 6, W("ml_gn"), 6)

            def s5(l):
                ac.wait_ge(b_y, 8 * (l + 1))
                act(sc[:, 0:512], bank[7][:, :], ACT.Copy).then_inc(b_ysb, 1)
                ac.wait_ge(b_v, l + 1)
                act(s5z, s5z, ACT.Gelu_apprx_tanh).then_inc(b_g, 1)
                ac.wait_ge(b_glu, l + 1)
                act(s5s, bank[4][:, :].rearrange("p (t n) -> p t n", t=2), ACT.Sigmoid).then_inc(b_sig, 1)

            ac.wait_ge(s_cst, 16)
            evacuate_h(0)
            for l in range(DEPTH):
                project(l)
                hyena(l, 0)
                ret_qk(l)
                hyena(l, 1)
                head_out(2 * l, 5, W("ret_gn"), 0)
                mlstm(l)
                s5(l)
                evacuate_h(2 * l + 1)
                if l == 0:
                    for u in range(2 * NC_FF):
                        ac.wait_ge(d_up, u + 1)
                        act(sil[u % 2], bank[4 + u % 2][:, 0:L], ACT.Silu).then_inc(d_sil, 1)
                        if u < NPRE:
                            pre(1, u)
                    evacuate_h(2)

            ac.wait_ge(q_l, 1)
            act(rt[2], rt[2], ACT.Exp).then_inc(q_ex, 1)

            def take_x(v, j):
                for q in range(2):
                    ac.wait_ge(e_g, v * 2 + (q + 1))
                    act(xg[j][:, 4 * q:4 * q + 4, :], bank[6 + q][:, :].rearrange("p (k s) -> p k s", k=4),
                        ACT.Copy).then_inc(e_xg, 1)

            def take_y(n, j):
                ac.wait_ge(e_dn, n)
                for q in range(2):
                    act(yex[:, q * 512:(q + 1) * 512], bank[2 * j + q][:, :], ACT.Copy).then_inc(e_y, 1)

            def expert(v, n, j):
                for c in range(NC_E):
                    ac.wait_ge(e_up, n * NC_E + (c + 1))
                    act(sil[c % 2], bank[4 + c % 2][:, 0:L], ACT.Silu).then_inc(e_sil, 1)
                    if c == 1:
                        take_y(n, 1 - j)
                    if c == 8:
                        take_x(v + 1, 1 - j)

            def all_experts(b):
                v0, n0 = b * (NE + 1), b * NE
                take_x(v0, 0)
                with ac.Fori(0, NE // 2) as i:
                    for j in range(2):
                        expert(i * 2 + (v0 + j), i * 2 + (n0 + j), j)
                take_y(n0 + NE, 1)

            all_experts(0)
            crowded = ac.value_load(over[0:1, 0:1], min_val=0, max_val=1)
            with ac.If(crowded == 1):
                all_experts(1)

        @block.vector
        def _(ve):
            tt, ts, stt = nc.vector.tensor_tensor, nc.vector.tensor_scalar, nc.vector.scalar_tensor_tensor
            count = [0]

            def link(ins):
                count[0] += 1
                ins.then_inc(dch, 1)
                ve.wait_ge(dch, count[0])

            def layer_norm(n):
                for t in range(TT):
                    for c in range(2):
                        ins = nc.vector.bn_stats(bst[:, t, c, :], h[:, t, c * 512:(c + 1) * 512])
                link(ins)
                for t in range(TT):
                    ins = nc.vector.bn_aggr(mv[:, t, :], bst[:, t].rearrange("p c s -> p (c s)"))
                link(ins)
                ts(var, mv[:, :, 1], EPS, None, ALU.add).then_inc(ln_var, 1)
                ve.wait_ge(s_ln, 16 * (n + 1))
                for t in range(TT):
                    ins = stt(out=h[:, t, :], in0=h[:, t, :], scalar=mv[:, t, 0:1], in1=lnb[:, 0:D],
                              op0=ALU.subtract, op1=ALU.mult)
                link(ins)
                ve.wait_ge(ln_rstd, n + 1)
                for t in range(TT):
                    stt(out=h[:, t, :], in0=h[:, t, :], scalar=rstd[:, t:t + 1], in1=lnb[:, D:2 * D],
                        op0=ALU.mult, op1=ALU.add).then_inc(h_ready, 1)

            def residual_psum(n):
                ve.wait_ge(mix_ready, n)
                for t in range(TT):
                    for c in range(2):
                        part = h[:, t, c * 512:(c + 1) * 512]
                        ins = stt(out=part, in0=part, scalar=ALPHA, in1=bank[2 * t + c][:, :], op0=ALU.mult, op1=ALU.add)
                link(ins)

            def pre(l, k):
                fx, filt, pm, rnorm, tfr = fx_[l], filt_[l], pm_[l], rnorm_[l], tfr_[l]
                if k in (0, 1):
                    ve.wait_ge(f_mm, 2 * l + k + 1)
                    b = W("hy_b1" if k == 0 else "hy_b2", 64)
                    link(ts(fx[0], bank[6 + k][0:64, 0:L], b, W("hy_freq", 64), ALU.add, ALU.mult))
                    link(ts(fx[1], fx[0], INV2PI, MAGIC, ALU.mult, ALU.add))
                    link(ts(fx[1], fx[1], MAGIC, None, ALU.subtract))
                    link(stt(out=fx[2], in0=fx[1], scalar=-6.28125, in1=fx[0], op0=ALU.mult, op1=ALU.add))
                    link(stt(out=fx[2], in0=fx[1], scalar=-(2 * math.pi - 6.28125), in1=fx[2], op0=ALU.mult,
                             op1=ALU.add))
                    ts(fx[2], fx[2], 3.1415925, -3.1415925, ALU.min, ALU.max).then_inc(f_red, 1)
                elif k < 6:
                    j = k - 2
                    t, o = j // 2, j % 2
                    ve.wait_ge(f_raw, 4 * l + j + 1)
                    tt(filt[:, t, o], bank[6 + j % 2][:, :].rearrange("p (d c) -> p d c", d=2),
                       bc(window[:, t, :], 1, 2), ALU.mult).then_inc(f_win, 1)
                elif k == 6:
                    ve.wait_ge(f_win, 4 * l + 4)
                    for t in range(TT):
                        for s, m in enumerate(("m0", "nm0")):
                            ins = stt(out=pm[:, s, t], in0=filt[:, t, :, 1, :], scalar=K(m)[:, t:t + 1],
                                      in1=filt[:, t, :, 0, :], op0=ALU.mult, op1=ALU.add)
                    ins.then_inc(f_pm, 1)
                    ve.wait_ge(f_sqrt, l + 1)
                    link(nc.vector.reciprocal(rnorm, rnorm))
                elif k < 11:
                    j = k - 7
                    ve.wait_ge(f_spm, 4 * l + j + 1)
                    tt(spec[:, j // 2, j % 2, :], bank[6 + (j + 1) % 2][:, :], rnorm, ALU.mult).then_inc(f_spec, 1)
                elif k == 11:
                    dt_, x1, th, tf, rr, _, sn, cs, n1, n2, n3 = s5v
                    ve.wait_ge(s_par, 16 * (l + 1))
                    ve.wait_ge(c_dt, l + 1)
                    tt(x1, W("a_re"), dt_, ALU.mult)
                    link(tt(th, W("a_im"), dt_, ALU.mult))
                    link(ts(th, th, INV2PI, None, ALU.mult))
                    link(ts(tf, th, MAGIC, MAGIC, ALU.add, ALU.subtract))
                    tt(tf, th, tf, ALU.subtract).then_inc(c_th, 1)
                    ve.wait_ge(c_exp, 3 * l + 3)
                    tt(n1, rr, cs, ALU.mult)
                    link(tt(n2, rr, sn, ALU.mult))
                    link(ts(n1, n1, 1.0, None, ALU.subtract))
                    tt(sn, n1, W("a_re"), ALU.mult)
                    tt(cs, n2, W("a_im"), ALU.mult)
                    tt(dt_, n2, W("a_re"), ALU.mult)
                    tt(th, n1, W("a_im"), ALU.mult)
                    tt(n3, W("a_re"), W("a_re"), ALU.mult)
                    link(tt(x1, W("a_im"), W("a_im"), ALU.mult))
                    tt(n1, sn, cs, ALU.add)
                    tt(n2, dt_, th, ALU.subtract)
                    link(tt(n3, n3, x1, ALU.add))
                    link(nc.vector.reciprocal(n3, n3))
                    tt(n1, n1, n3, ALU.mult)
                    link(tt(n2, n2, n3, ALU.mult))
                elif k == 12:
                    n1, n2 = s5v[8], s5v[9]
                    cr, ci = s5c[:, 0], s5c[:, 1]
                    ct_ = ct_s[l]
                    ve.wait_ge(f_spec, 4 * l + 4)
                    tt(ct_[0], cr, bc(n1, 2, 32), ALU.mult)
                    tt(ct_[1], ci, bc(n2, 2, 32), ALU.mult)
                    tt(ct_[2], cr, bc(n2, 2, 32), ALU.mult)
                    link(tt(ct_[3], ci, bc(n1, 2, 32), ALU.mult))
                    tt(cr, ct_[0], ct_[1], ALU.subtract)
                    link(stt(out=ci, in0=ct_[2], scalar=-1.0, in1=ct_[3], op0=ALU.mult, op1=ALU.subtract))
                elif k < 21:
                    i = k - 13
                    v = 8 * l + i
                    tf = s5v[3]
                    kk, ph = work[l][:, 0:512], work[l][:, 512:1024]
                    pos = K("pos")
                    if i == 0:
                        ve.wait_ge(f_spec, 4 * l + 4)
                    else:
                        ve.wait_ge(t_ph, v)
                    for d in range(2):
                        ins = ts(ph[:, d * L:(d + 1) * L], pos[:, d * L:(d + 1) * L], tf[:, 2 * i + d:2 * i + d + 1],
                                 None, ALU.mult)
                    link(ins)
                    link(ts(kk, ph, MAGIC, MAGIC, ALU.add, ALU.subtract))
                    if i:
                        ve.wait_ge(t_tab, 3 * v)
                    tt(tfr, ph, kk, ALU.subtract).then_inc(t_ph, 1)

            def project(l):
                for i in range(13):
                    b = bank[i % 4]
                    if 1 <= i < 6:
                        ve.wait_ge(cv_c, 10 * l + 2 * i)
                        for q in range(2):
                            t = 2 * (i - 1) + q
                            ins = stt(out=cv[:, t, 1:L], in0=b[:, q * L:q * L + L - 1], scalar=conv_w[:, t, 0:1],
                                      in1=cv[:, t, 1:L], op0=ALU.mult, op1=ALU.add)
                        link(ins)
                        for q in range(2):
                            t = 2 * (i - 1) + q
                            ins = stt(out=cv[:, t, 0:L - 1], in0=b[:, q * L + 1:(q + 1) * L],
                                      scalar=conv_w[:, t, 2:3], in1=cv[:, t, 0:L - 1], op0=ALU.mult, op1=ALU.add)
                        ins.then_inc(cv_ev, 1)
                    elif i in (6, 7):
                        t = i - 6
                        ve.wait_ge(pj, 13 * l + i + 1)
                        tmp = rtmp.rearrange("p (g s c) -> p g s c", g=8, s=2)
                        b4 = b[:, :].rearrange("p (g s c) -> p g s c", g=8, s=2)
                        if t:
                            ve.wait_ge(rot_ev, 2 * l + t)
                        tt(rq[:, t, :].rearrange("p (g c) -> p g c", g=8),
                           b[:, :].rearrange("p (g c) -> p g c", g=8), bc(rot[0][:, t, :], 1, 8), ALU.mult)
                        for q in range(2):
                            ins = tt(tmp[:, :, q, :], b4[:, :, 1 - q, :],
                                     bc(rot[1][:, t, q * 32:(q + 1) * 32], 1, 8), ALU.mult)
                        link(ins)
                        tt(rq[:, t, :], rq[:, t, :], rtmp, ALU.add).then_inc(rot_ev, 1)
                    elif i == 12:
                        ve.wait_ge(pj, 13 * l + 13)
                        tt(gts, b[:, 0:32].rearrange("p (t g) -> p t g", t=2), bc(W("gate_b"), 1, TT),
                           ALU.add).then_inc(gate_ev, 1)
                    if l == 0:
                        for k in BESIDE[i]:
                            pre(0, k)

            def hyena_product(l, n):
                u = 2 * l + n
                ve.wait_ge(z_sp, u + 1)
                if n == 0:
                    ve.wait_ge(f_spec, 4 * l + 4)
                kc, ks = (spec[:, s].rearrange("p t (o c) -> p t o c", o=2)[:, :, n, :] for s in range(2))
                t4 = [a.rearrange("p (t c) -> p t c", t=2) for a in hy_t]
                uc, us = (bank[1 + s][:, :].rearrange("p (t c) -> p t c", t=2) for s in range(2))
                tt(t4[0], uc, kc, ALU.mult)
                tt(t4[1], us, ks, ALU.mult)
                tt(t4[2], uc, ks, ALU.mult)
                link(tt(t4[3], us, kc, ALU.mult))
                tt(t4[0], t4[0], t4[1], ALU.subtract)
                tt(t4[2], t4[2], t4[3], ALU.add).then_inc(z_pr, 1)

            def hyena_gate(l, n):
                ve.wait_ge(z_iv, 2 * l + n + 1)
                if n:
                    for q in range(2):
                        ve.wait_ge(t_st[q], 16 * 4 * (l + 1))
                for c in range(2):
                    ins = stt(out=cv[:, c, :], in0=cv[:, c, :], scalar=W("hy_bias")[:, 2 * n + c:2 * n + c + 1],
                              in1=bank[0][:, c * L:(c + 1) * L], op0=ALU.mult, op1=ALU.add)
                link(ins)
                dst = cv[:, 0:2, :] if n == 0 else yT[:, 4:6, :]
                tt(dst, cv[:, 0:2, :], cv[:, 2 + 2 * n:4 + 2 * n, :], ALU.mult).then_inc(z_out, 1)

            def head_norm(m, o, gate):
                c8, s8 = (a.rearrange("p (g c) -> p g c", g=8) for a in (cen, sqr))
                link(nc.vector.tensor_reduce(hmean, o, AX.X, ALU.add))
                link(ts(hmean, hmean, 1.0 / HD, None, ALU.mult))
                link(tt(c8, o, bc(hmean, 2, HD), ALU.subtract))
                link(tt(s8, c8, c8, ALU.mult))
                link(nc.vector.tensor_reduce(hvar, s8, AX.X, ALU.add))
                ts(hvar, hvar, 1.0 / HD, EPS, ALU.mult, ALU.add).then_inc(n_var, 1)
                ve.wait_ge(n_rstd, m + 1)
                link(tt(c8, c8, bc(hrstd, 2, HD), ALU.mult))
                tt(ytm, cen.rearrange("p (t c) -> p t c", t=2), gate, ALU.mult).then_inc(n_y, 1)

            def ret_decay(l, a):
                ve.wait_ge(r_s, 4 * l + a + 1)
                for m in range(TT):
                    ins = tt(st[:, a % 2, m, :], bank[5 + a % 2][:, m * L:(m + 1) * L],
                             decay[:, a, P - P * m:P - P * m + L], ALU.mult)
                ins.then_inc(r_st, 1)

            def ret_norm(l):
                ve.wait_ge(r_o, l + 1)
                ve.wait_ge(r_qk, 2 * l + 2)
                head_norm(2 * l, bank[4][:, :].rearrange("p (g c) -> p g c", g=8), vg[:, :, 256:512])

            def ml_rows_a(l):
                ve.wait_ge(m_g4, 2 * l + 2)
                ve.wait_ge(n_tr, 2 * l + 1)
                f = g4.rearrange("p (d k) n -> p d k n", k=2)[:, :, 1, :]
                ts(lf, f, 0.0, None, ALU.min)
                stt(out=ex, in0=f, scalar=-1.0, in1=f, op0=ALU.mult, op1=ALU.max).then_inc(m_abs, 1)
                link(nc.vector.memset(onerow, 1.0))

            def ml_rows_b(l):
                i_ = g4.rearrange("p (d k) n -> p d k n", k=2)[:, :, 0, :]
                ve.wait_ge(m_ln, l + 1)
                link(tt(lf, lf, ex, ALU.subtract))
                scan = nc.vector.tensor_tensor_scan
                scan(acum[:, 0, :], onerow, lf[:, 0, :], 0.0, ALU.mult, ALU.add)
                link(scan(acum[:, 1, ::-1], onerow, lf[:, 1, ::-1], 0.0, ALU.mult, ALU.add))
                link(tt(brow, i_, acum, ALU.subtract))
                scan(crow[:, 0, :], onerow, brow[:, 0, :], 0.0, ALU.mult, ALU.max)
                link(scan(crow[:, 1, ::-1], onerow, brow[:, 1, ::-1], 0.0, ALU.mult, ALU.max))
                stt(out=nmrow, in0=acum, scalar=-1.0, in1=crow, op0=ALU.mult, op1=ALU.subtract).then_inc(m_rows, 1)

            def ml_cols(l):
                ve.wait_ge(m_ct, l + 1)
                nc.vector.tensor_copy(colsb, bank[6][:, 0:32]).then_inc(m_cols, 1)

            def ml_weights(l, a):
                ve.wait_ge(m_sc, 4 * l + a + 1)
                if a >= 2:
                    ve.wait_ge(m_w, 24 * l + 6 * a - 6)
                for d in range(2):
                    ins = stt(out=wmask[:, a % 2, d],
                              in0=bank[2][:, d * L:(d + 1) * L].rearrange("p (b n) -> p b n", b=2),
                              scalar=-1.0, in1=bc(K("mask_fw" if d == 0 else "mask_bw"), 1, 2),
                              op0=ALU.mult, op1=ALU.add)
                ins.then_inc(m_msk, 1)
                w = wml[:, a % 2]
                s4 = bank[a % 2][:, :].rearrange("p (q n) -> p q n", q=4)
                for d in range(2):
                    ve.wait_ge(m_w, 24 * l + 6 * a + 3 * d + 3)
                    stt(out=w[:, 3 * d:3 * d + 2], in0=s4[:, 0:4:3, :], scalar=HD ** -0.5,
                        in1=w[:, 3 * d:3 * d + 2], op0=ALU.mult, op1=ALU.mult)
                    q = 1 if d == 0 else 2
                    ins = stt(out=w[:, 3 * d + 2], in0=s4[:, q, :], scalar=HD ** -0.5, in1=w[:, 3 * d + 2],
                              op0=ALU.mult, op1=ALU.mult)
                ins.then_inc(m_sw, 1)

            def ml_norm(l):
                ve.wait_ge(m_nd, l + 1)
                ve.wait_ge(m_em, l + 1)
                link(nc.vector.tensor_copy(rden, bank[6][:, 0:16]))
                link(stt(out=den, in0=rden, scalar=-1.0, in1=rden, op0=ALU.mult, op1=ALU.max))
                link(tt(den, den, emm, ALU.max))
                link(nc.vector.reciprocal(rden, den))
                hs = [sc[:, q * 512:(q + 1) * 512].rearrange("p (g c) -> p g c", g=8) for q in range(2)]
                for d in range(2):
                    ins = tt(hs[d], bank[4 + d][:, :].rearrange("p (g c) -> p g c", g=8),
                             bc(rden[:, 8 * d:8 * d + 8], 2, HD), ALU.mult)
                link(ins)
                link(tt(hs[0], hs[0], hs[1], ALU.add))
                head_norm(2 * l + 1, hs[0], vo[:, :].rearrange("p (t c) -> p t c", t=2)[:, :, 256:512])

            def s5_tile(l, i):
                rr = s5v[4]
                scan = nc.vector.tensor_tensor_scan
                v = 8 * l + i
                T = s5_table(l, i)
                T4 = T.rearrange("p s d n -> p (s d) n")
                (p1, p2), (x1, x2) = s5_work(l)
                ve.wait_ge(b_mm, v + 1)
                if i == 0:
                    ve.wait_ge(s_tab, 32 * (l + 1))
                b = bank[3]
                tt(p1.rearrange("p s d n -> p (s d) n"), T4, bc(b[:, 0:L], 1, 4), ALU.mult)
                tt(p2.rearrange("p s d n -> p (s d) n"), T4, bc(b[:, L:2 * L], 1, 4), ALU.mult).then_inc(b_p, 1)
                ve.wait_ge(b_p, v + 1)
                tt(p1[:, 0], p1[:, 0], p2[:, 1], ALU.add)
                link(tt(p2[:, 0], p2[:, 0], p1[:, 1], ALU.subtract))
                for d in range(2):
                    r = rr[:, 2 * i + d:2 * i + d + 1].broadcast_to([P, L])
                    for p in (p1, p2):
                        if d == 0:
                            ins = scan(p[:, 1, 0, :], r, p[:, 0, 0, :], 0.0, ALU.mult, ALU.add)
                        else:
                            ins = scan(p[:, 1, 1, ::-1], r, p[:, 0, 1, ::-1], 0.0, ALU.mult, ALU.add)
                link(ins)
                if i:
                    ve.wait_ge(b_y, v)
                tt(x1, T, bc(p1[:, 1], 1, 2), ALU.mult).then_inc(b_x, 1)
                tt(x2[:, 0], T[:, 0], p2[:, 1], ALU.mult)
                stt(out=x2[:, 1], in0=T[:, 1], scalar=-1.0, in1=p2[:, 1], op0=ALU.mult, op1=ALU.mult).then_inc(b_x, 1)
                ve.wait_ge(b_x, 2 * (v + 1))

            def s5_end(l):
                ve.wait_ge(b_tr, l + 1)
                for c in range(2):
                    ins = stt(out=s5z[:, c, :], in0=uT[:, c, :], scalar=W("s5_d")[:, c:c + 1],
                              in1=bank[5][:, c * L:(c + 1) * L], op0=ALU.mult, op1=ALU.add)
                ins.then_inc(b_v, 1)
                ve.wait_ge(b_sig, l + 1)
                tt(yT[:, 2:4, :], s5z, s5s, ALU.mult).then_inc(b_out, 1)

            def mixers(l):
                s5_tile(l, 0)
                hyena_product(l, 0)
                s5_tile(l, 1)
                hyena_gate(l, 0)
                ret_decay(l, 0)
                ret_decay(l, 1)
                s5_tile(l, 2)
                ret_decay(l, 2)
                ret_decay(l, 3)
                s5_tile(l, 3)
                ret_norm(l)
                hyena_product(l, 1)
                s5_tile(l, 4)
                hyena_gate(l, 1)
                ml_rows_a(l)
                s5_tile(l, 5)
                ml_rows_b(l)
                s5_tile(l, 6)
                ml_cols(l)
                ml_weights(l, 0)
                ml_weights(l, 1)
                s5_tile(l, 7)
                ml_weights(l, 2)
                ml_weights(l, 3)
                ml_norm(l)
                s5_end(l)

            ve.wait_ge(s_cst, 16)
            ve.wait_ge(s_x, 16)
            layer_norm(0)
            for l in range(DEPTH):
                ve.wait_ge(ht_ready, 8 * l + 4)
                project(l)
                mixers(l)
                residual_psum(2 * l + 1)
                layer_norm(2 * l + 1)
                if l == 0:
                    for u in range(2 * NC_FF):
                        ve.wait_ge(d_sil, u + 1)
                        tt(mid[u % 2], sil[u % 2], bank[4 + u % 2][:, L:2 * L], ALU.mult).then_inc(d_mid, 1)
                        if u < NPRE:
                            pre(1, u)
                    residual_psum(2)
                    layer_norm(2)

            lg, sel, el = rt[0], rt[1], rt[2]
            ve.wait_ge(q_lg, 1)
            ve.wait_ge(mix_ready, 3)
            link(nc.vector.tensor_copy(lg, bank[6][:, 0:16].rearrange("p (t e) -> p t e", t=2)))
            link(nc.vector.tensor_reduce(rt1[:, 0:2], lg, AX.X, ALU.max))
            tt(el, lg, bc(rt1[:, 0:2], 2, NE), ALU.subtract).then_inc(q_l, 1)
            for t in range(TT):
                a, b = bc(lg[:, t, :], 1, NE), bc(lg[:, t, :], 2, NE)
                tt(cmp1[:, t], a, b, ALU.is_gt)
                ins = tt(cmp2[:, t], a, b, ALU.is_equal)
            link(ins)
            for t in range(TT):
                ins = tt(cmp2[:, t], cmp2[:, t], K("lower").rearrange("p (a b) -> p a b", a=NE), ALU.mult)
            link(ins)
            link(tt(cmp1, cmp1, cmp2, ALU.add))
            for t in range(TT):
                ins = nc.vector.tensor_reduce(rt[3][:, t, :], cmp1[:, t], AX.X, ALU.add)
            link(ins)
            ts(sel, rt[3], 1.5, None, ALU.is_lt).then_inc(q_sel, 1)
            ve.wait_ge(q_sel, 1)
            ve.wait_ge(q_ex, 1)
            link(tt(el, el, sel, ALU.mult))
            link(nc.vector.tensor_reduce(rt1[:, 2:4], el, AX.X, ALU.add))
            link(nc.vector.reciprocal(rt1[:, 4:6], rt1[:, 2:4]))
            link(nc.vector.memset(comb, 0.0))
            link(nc.vector.memset(posx, 4096.0))
            tt(comb[:, :, 0:NE], el, bc(rt1[:, 4:6], 2, NE), ALU.mult)
            ve.wait_ge(q_pos, 1)
            link(ts(rt[4], sel, -4096.0, 4096.0, ALU.mult, ALU.add))
            link(nc.vector.tensor_reduce(rt1[:, 6:7], bank[7][:, 16:24], AX.X, ALU.max))
            link(ts(over[:, 0:1], rt1[:, 6:7], P + 0.5, None, ALU.is_gt))
            tt(posx[:, :, 0:NE], rt[4], bank[7][:, 0:16].rearrange("p (t e) -> p t e", t=2), ALU.add).then_inc(q_px, 1)
            ve.wait_ge(q_px, 1)
            link(nc.vector.memset(acc, 0.0))

            def prepare(e):
                for t in range(TT):
                    ts(onehot[:, t, :], K("iota"), posx[:, t, bass.ds(e, 1)], None, ALU.is_equal)
                    ins = ts(gated[:, t, :], K("iota"), posx[:, t, bass.ds(e, 1)], comb[:, t, bass.ds(e, 1)],
                             ALU.is_equal, ALU.mult)
                ins.then_inc(e_p, 1)

            def placed(v, j):
                ve.wait_ge(e_tm, v + 1)
                nc.vector.tensor_copy(place[j], bank[6][:, 0:L]).then_inc(e_t, 1)

            def add(v, q0):
                for q in (q0, q0 + 1):
                    ve.wait_ge(e_sc, v * 4 + (q + 1))
                    part = acc[:, q // 2, (q % 2) * 512:(q % 2 + 1) * 512]
                    tt(part, part, bank[6 + q % 2][:, :], ALU.add).then_inc(e_acc, 1)

            def expert(e, v, n, j):
                for c in range(NC_E):
                    ve.wait_ge(e_sil, n * NC_E + (c + 1))
                    tt(mid[c % 2], sil[c % 2], bank[4 + c % 2][:, L:2 * L], ALU.mult).then_inc(e_mid, 1)
                    if c in (3, 5):
                        add(v, c - 3)
                    if c == 6:
                        ve.wait_ge(e_tm, v + 1)
                        prepare(e + 1)
                    if c == 10:
                        placed(v + 1, 1 - j)

            def all_experts(b):
                v0, n0 = b * (NE + 1), b * NE
                nc.vector.memset(place[1], 0.0).then_inc(q_px, 1)
                ve.wait_ge(q_px, 2 * b + 2)
                prepare(0)
                placed(v0, 0)
                with ve.Fori(0, NE // 2) as i:
                    for j in range(2):
                        expert(i * 2 + j, i * 2 + (v0 + j), i * 2 + (n0 + j), j)
                add(v0 + NE, 0)
                add(v0 + NE, 2)
                ve.wait_ge(e_acc, 4 * (v0 + NE) + 4)

            all_experts(0)
            crowded = ve.value_load(over[0:1, 0:1], min_val=0, max_val=1)
            with ve.If(crowded == 1):
                ts(posx, posx, float(P), None, ALU.subtract).then_inc(q_px, 1)
                ve.wait_ge(q_px, 3)
                all_experts(1)
            link(stt(out=h[:, :, :], in0=h[:, :, :], scalar=ALPHA, in1=acc, op0=ALU.mult, op1=ALU.add))
            layer_norm(4)


def constants():
    c = np.zeros((P, CONST_W), np.float64)

    def put(name, a, rows=P):
        s, e = CONST[name]
        c[0:rows, s:e] = np.asarray(a).reshape(rows, e - s)

    p = np.arange(P)
    tok = (np.arange(TT)[None, :] * P + p[:, None])
    gamma = 1.0 - 2.0 ** (-5.0 - np.arange(H))
    j = np.arange(3 * P)
    put("decay", gamma[None, :, None] ** np.abs(j[None, None, :] - P - p[:, None, None]) * HD ** -0.5)
    f = np.arange(L)
    for n, fn in (("c", np.cos), ("s", np.sin)):
        put("dft_" + n, fn(2 * np.pi * tok[:, :, None] * (f + 0.5) / (2 * L)))
        put("idft_" + n, fn(2 * np.pi * (tok[:, :, None] + 0.5) * f / (2 * L)) / L)
    rates = np.abs(np.linspace(math.log(1e-2) / 1.5, math.log(1e-2) / 0.3, DG))
    put("window", np.exp(-(tok[:, :, None] / (L - 1.0)) * rates))
    half = HD // 2
    ang = tok[:, :, None] * 10000.0 ** (-np.arange(half) / half)
    put("rot_c", np.concatenate([np.cos(ang), np.cos(ang)], -1))
    put("rot_s", np.concatenate([-np.sin(ang), np.sin(ang)], -1))
    put("mask_fw", np.where(p[:, None] <= p[None, :], 0.0, NEG))
    put("mask_bw", np.where(p[:, None] >= p[None, :], 0.0, NEG))
    put("before", p[:, None] < p[None, :])
    put("iota", np.tile(p, (P, 1)))
    put("ident", np.eye(P))
    put("ones", np.ones((P, P)))
    t = np.linspace(0.0, 1.0, L)
    w = 2 * np.pi * np.arange(L) / L
    bands = np.linspace(1e-4, 15, 16)
    put("pos", np.tile(np.stack([f, L - 1 - f]).reshape(1, -1), (P, 1)))
    put("pick", np.kron(np.eye(H), np.ones((1, P))), H)
    s, _ = CONST["pick"]
    c[64:97, s:s + L] = np.concatenate([t[None], np.cos(bands[:, None] * w), -np.sin(bands[:, None] * w)], 0)
    put("m0", tok != 0)
    put("nm0", -1.0 * (tok != 0))
    put("halfpi", np.full((P, 1), math.pi / 2 - 1e-7))
    e = np.arange(NE)
    put("lower", np.tile((e[None, :] < e[:, None]).reshape(1, -1), (P, 1)))
    return c.astype(np.float32)


def parameters(a):
    out = np.zeros((DEPTH, P, PAR_W), np.float32)
    for l in range(DEPTH):
        o = out[l]

        def put(name, v, rows=P):
            s, e = PAR[name]
            o[0:rows, s:e] = np.asarray(v).reshape(rows, e - s)

        cw = np.concatenate([a["hy_conv_w"][l], a["ml_conv_w"][l]], 1)
        cb = np.concatenate([a["hy_conv_b"][l], a["ml_conv_b"][l]])[None]
        put("conv", np.concatenate([cw, cb]).reshape(4, 10, P).transpose(2, 1, 0))
        put("hy_bias", a["hy_bias"][l].reshape(2, 2, P).transpose(2, 0, 1))
        for n, k in (("ret_gn", "ret_gn_w"), ("ml_gn", "ml_gn_w"), ("s5_d", "s5_d")):
            put(n, a[k][l].reshape(2, P).T)
        for n in ("a_re", "a_im"):
            put(n, a["s5_" + n][l].reshape(2, 8, P).transpose(2, 1, 0))
        dt = np.repeat(a["s5_log_dt"][l].reshape(2, 8, 2, 1), N_STATE, 3)
        put("log_dt", dt.reshape(2, 8, P).transpose(2, 1, 0))
        cc = np.zeros((2, N_STATE, 2, 8, 2, 2, S5_CH), np.float32)
        bb = np.zeros((4, 2, S5_CH, 2, 2, 2, N_STATE), np.float32)
        for r, n in enumerate(("re", "im")):
            cs = a["s5_c_" + n][l].reshape(2, 8, 2, S5_CH, N_STATE)
            bs = a["s5_b_" + n][l].reshape(2, 4, 2, N_STATE, S5_CH)
            for q in range(2):
                cc[q, :, r, :, :, q, :] = cs[:, :, q].transpose(3, 1, 0, 2)
                bb[:, q, :, :, r, q, :] = bs[:, :, q].transpose(1, 3, 0, 2)
        put("s5_c", cc)
        put("s5_b", bb)
        put("glu", a["s5_w_glu"][l].reshape(2, P, DG).transpose(1, 0, 2))
        put("hy_w12", a["hy_w2"][l], 64)
        s, e = PAR["hy_w12"]
        o[64:97, s:e] = a["hy_w1"][l]
        put("hy_w3", a["hy_w3"][l], 64)
        put("hy_b1", a["hy_b1"][l], 64)
        put("hy_b2", a["hy_b2"][l], 64)
        put("hy_freq", a["hy_freq"][l], 64)
        put("gate_w", a["w_in"][l][:, 3072:3088].reshape(KT, P, 16).transpose(1, 0, 2))
        gb = a["ml_gate_b"][l].reshape(1, 16)
        put("gate_b", np.broadcast_to(gb, (P, 16)))
        put("router", a["moe_router"][0].reshape(KT, P, NE).transpose(1, 0, 2))
    return out


def chunks(w1, w3, w2):
    n = w1.shape[1] // FC
    up = [w.reshape(KT, P, n, FC).transpose(2, 1, 0, 3).reshape(n, P, KT * FC) for w in (w1, w3)]
    down = w2.reshape(n, 2, P, D).transpose(0, 2, 1, 3).reshape(n, P, 2 * D)
    return np.concatenate(up + [down], 2)


def kernel(**inputs):
    import concourse.bacc as _bacc
    from concourse.bass_utils import run_bass_kernel_spmd as _run

    a = {k: np.asarray(v) for k, v in inputs.items()}
    w_in = np.stack([
        np.concatenate([a["w_in"][l][:, c0:c1] for c0, c1 in ((1024, 2560), (0, 1024), (2560, 3072))], 1)
        .reshape(KT, P, 4, WIN_COLS).transpose(2, 1, 0, 3).reshape(4, P, SLOT) for l in range(DEPTH)])
    w_out = np.stack([a["w_out"][l].reshape(KT, P, 2, 512).transpose(2, 1, 0, 3).reshape(2, P, KT * 512)
                      for l in range(DEPTH)])
    moe = np.empty((NE * NC_E, P, SLOT), np.float32)
    for e in range(NE):
        moe[e * NC_E:(e + 1) * NC_E] = chunks(a["moe_w1"][0, e], a["moe_w3"][0, e], a["moe_w2"][0, e])
    norms = [("ln_in_w", "ln_in_b", None)] + [(f"ln{k}_w", f"ln{k}_b", l) for l in range(DEPTH) for k in (1, 2)]
    rows = [np.concatenate([a[w] if l is None else a[w][l], a[b] if l is None else a[b][l]]) for w, b, l in norms]
    ln = np.broadcast_to(np.stack(rows)[:, None, :], (len(rows), P, 2 * D)).copy()
    arrays = {
        "x": a["x"].reshape(L, D), "ln": ln, "const": constants(), "par": parameters(a), "w_in": w_in,
        "w_out": w_out, "ffn": chunks(a["ffn_w1"][0], a["ffn_w3"][0], a["ffn_w2"][0]), "moe": moe}
    nc = _bacc.Bacc("TRN2", target_bir_lowering=False, num_devices=1)
    args = [nc.dram_tensor(n, list(v.shape), F32, kind="ExternalInput").ap() for n, v in arrays.items()]
    tab = nc.dram_tensor("tab", [DEPTH, 8, P, 4 * L], F32, kind="Internal").ap()
    out = nc.dram_tensor("out", [L, D], F32, kind="ExternalOutput").ap()
    trunk(nc, *args, tab, out)
    r = _run(nc, [arrays], core_ids=[0])
    return r.results[0]["out"].reshape(1, L, D)
```

```python
import math
from contextlib import ExitStack

import numpy as np
import concourse.bass as bass
from concourse import mybir

F32 = mybir.dt.float32
F32R = mybir.dt.float32r
I32 = mybir.dt.int32
ALU = mybir.AluOpType
ACT = mybir.ActivationFunctionType
AX = mybir.AxisListType

P = 128
D = 1024
L = 256
TT = L // P
KT = D // P
DEPTH = 2
DG = 256
HD = 64
H = DG // HD
N_STATE = 64
S5_CH = 16
D_FF = 2816
D_FFE = 3584
NE = 8
EPS = 1e-5
ALPHA = (2 * DEPTH) ** 0.25
FC = 256
NC_FF = D_FF // FC
NC_E = D_FFE // FC
SLOTS = 4
SLOT = 3 * KT * FC
WIN_COLS = SLOT // KT
RING_MIX = 6
G_FF = RING_MIX
G_MIX1 = G_FF + NC_FF
G_MOE = G_MIX1 + RING_MIX
NS = 6
HS = NS // 2
SPLIT = ((0, 0), (1, 0), (0, 1))
SPLIT_SLOT = 1
PLAN = [0, 1, 2, 3] + [0, 1] + [(2, 3, 0)[i % 3] for i in range(NC_FF)] + [0, 2, 3, 1] + [0, 2]
MOE_SLOTS = (3, 1, 0, 2)
MAGIC = 12582912.0
TURN = 6.2831850
INV2PI = 1.0 / (2.0 * math.pi)
NEG = -1.0e30


def columns(sizes):
    at, out = 0, {}
    for name, n in sizes:
        out[name] = (at, at + n)
        at += n
    return out, at


CONST, CONST_W = columns([
    ("decay", H * 3 * P), ("dft_c", 512), ("dft_s", 512), ("idft_c", 512), ("idft_s", 512),
    ("window", 512), ("rot_c", 128), ("rot_s", 128), ("mask_fw", P), ("mask_bw", P), ("before", P),
    ("iota", P), ("ident", P), ("ones", P), ("pos", 2 * L), ("pick", H * P),
    ("m0", 2), ("nm0", 2), ("halfpi", 1), ("lower", NE * NE)])

PAR, PAR_W = columns([
    ("conv", 10 * 4), ("hy_bias", 4), ("ret_gn", 2), ("ml_gn", 2), ("s5_d", 2),
    ("a_re", 16), ("a_im", 16), ("log_dt", 16), ("s5_c", 2 * 16 * 32), ("s5_b", 512), ("glu", 512),
    ("hy_w12", 64), ("hy_w3", 1024), ("hy_b1", 1), ("hy_b2", 1), ("hy_freq", 1),
    ("gate_w", KT * 16), ("gate_b", 16), ("router", KT * NE)])


def trunk(nc, x, ln, const, par, w_in, w_out, ffn, moe, tab, out):
    ctx = ExitStack()
    with ctx:
        place_of = {}

        def sb(name, shape, dt=F32):
            tensor = ctx.enter_context(nc.sbuf_tensor(name, shape, dt))
            place_of[name] = nc.sbuf_base - 4 * math.prod(shape[1:])
            return tensor

        def sem(name):
            return ctx.enter_context(nc.semaphore(name))

        def bc(ap, axis, n):
            shape = list(ap.shape)
            shape.insert(axis, n)
            return ap.unsqueeze(axis).broadcast_to(shape)

        ring = [sb(f"ring{i}", [P, SLOT]) for i in range(SLOTS)]
        h = sb("h", [P, TT, D])
        lnb = sb("lnb", [P, 2 * D])
        cst = sb("cst", [P, CONST_W])
        pr = sb("pr", [P, PAR_W])
        hT = sb("hT", [P, KT, L])
        ret = sb("ret", [P, 2048])
        vo = sb("vo", [P, 1024])
        uT = sb("uT", [P, 2, L])
        cv = sb("cv", [P, 10, L])
        yT = sb("yT", [P, KT, L])
        spec = sb("spec", [P, 2, TT, 512])
        sc = sb("sc", [P, 2048])
        small = sb("small", [P, 360])
        over = sb("over", [P, 8], I32)

        def over_sb(name, under, first, shape):
            return nc.alloc_sbuf_tensor_at(name, shape, F32R, offset=place_of[under] + 4 * first)

        xs = f"ring{SPLIT_SLOT}"
        ff_x = [over_sb("ff_x_hi", "hT", 0, [P, KT, L]), over_sb("ff_x_lo", xs, 0, [P, KT, L])]
        ff_up = [over_sb(f"ff_up_{n}", xs, (1 + i) * KT * L, [P, 2, KT, P]) for i, n in enumerate(("hi", "lo"))]
        ff_w2 = [over_sb(f"ff_w2_{n}", "lnb", i * D, [P, D]) for i, n in enumerate(("hi", "lo"))]
        ff_mid = [over_sb(f"ff_mid_{n}", "sc", 1024 + i * 512, [P, 2, L]) for i, n in enumerate(("hi", "lo"))]
        ex_w2 = [over_sb(f"ex_w2_{n}", a, 0, [P, 2, D]) for n, a in (("hi", "hT"), ("lo", "spec"))]
        ex_mid = [over_sb("ex_mid_hi", "cv", 2048, [P, 2, L]), over_sb("ex_mid_lo", "uT", 0, [P, 2, L])]
        UP = NS * 2 * FC
        assert UP + NS * P <= CONST["mask_fw"][0] and UP <= PAR["gate_w"][0]
        ex_up = [over_sb("ex_up_hi", "cst", 0, [P, NS, 2 * FC]), over_sb("ex_up_lo", "pr", 0, [P, NS, 2 * FC])]
        ex_x = [[over_sb("ex_x0_hi", "cv", 0, [P, NS, P]), over_sb("ex_x0_lo", "cv", NS * P, [P, NS, P])],
                [over_sb("ex_x1_hi", "cst", UP, [P, NS, P]), over_sb("ex_x1_lo", "yT", 1024, [P, NS, P])]]
        bank = [ctx.enter_context(nc.psum_tensor(f"bank{i}", [P, 512], F32)) for i in range(8)]

        def K(name, rows=P):
            a, b = CONST[name]
            return cst[0:rows, a:b]

        def W(name, rows=P):
            a, b = PAR[name]
            return pr[0:rows, a:b]

        ident = K("ident")
        decay = K("decay").rearrange("p (h j) -> p h j", h=H)
        dft = [K(n).rearrange("p (t f) -> p t f", t=TT) for n in ("dft_c", "dft_s")]
        idft = [K(n).rearrange("p (t f) -> p t f", t=TT) for n in ("idft_c", "idft_s")]
        window = K("window").rearrange("p (t c) -> p t c", t=TT)
        rot = [K(n).rearrange("p (t c) -> p t c", t=TT) for n in ("rot_c", "rot_s")]
        z_feat = cst[64:97, CONST["pick"][0]:CONST["pick"][0] + L]
        w1_feat = pr[64:97, PAR["hy_w12"][0]:PAR["hy_w12"][1]]
        conv_w = W("conv").rearrange("p (t j) -> p t j", j=4)

        vg = ret[:, 0:1024].rearrange("p (t c) -> p t c", t=TT)
        qkT = ret[:, 1024:2048].rearrange("p (f n) -> p f n", f=4)
        lnf = lnb[:, :]
        rq = lnf[:, 0:1024].rearrange("p (t c) -> p t c", t=TT)
        rtmp = lnf[:, 1024:1536]
        cen = lnf[:, 0:512]
        sqr = lnf[:, 512:1024]
        ytm = lnf[:, 1024:1536].rearrange("p (t c) -> p t c", t=TT)
        st = sc[:, 512:1536].rearrange("p (b m n) -> p b m n", b=2, m=2)
        ztm = sc[:, 0:512].rearrange("p (t c) -> p t c", t=TT)
        hTf = hT[:, :, :].rearrange("p k n -> p (k n)")
        hy_t = [hTf[:, i * 512:(i + 1) * 512] for i in range(4)]
        g4 = hTf[0:H, 0:1024].rearrange("p (k n) -> p k n", k=4)
        lf = hTf[0:H, 1024:1536].rearrange("p (k n) -> p k n", k=2)
        ex = hTf[0:H, 1536:2048].rearrange("p (k n) -> p k n", k=2)
        acum = lnf[0:H, 0:512].rearrange("p (k n) -> p k n", k=2)
        brow = lnf[0:H, 512:1024].rearrange("p (k n) -> p k n", k=2)
        crow = lnf[0:H, 1024:1536].rearrange("p (k n) -> p k n", k=2)
        nmrow = lnf[0:H, 1536:2048].rearrange("p (k n) -> p k n", k=2)
        onerow = sc[0:H, 1792:2048]
        wmask = hTf[:, 0:1024].rearrange("p (q d b n) -> p q d b n", q=2, d=2, b=2)
        wml = sc[:, 256:1792].rearrange("p (q b n) -> p q b n", q=2, b=6)
        def borrowed(l):
            return [ring[slot_use(l * G_MIX1 + RING_MIX + i)[0]] for i in range(2)]

        def s5_table(l, i):
            a, b = borrowed(l)
            src = a[:, i * 1024:(i + 1) * 1024] if i < 6 else b[:, (i - 6) * 1024:(i - 5) * 1024]
            return src.rearrange("p (s d n) -> p s d n", s=2, d=2)

        def s5_work(l):
            b = borrowed(l)[1]
            v = [b[:, (2 + q) * 1024:(3 + q) * 1024].rearrange("p (s d n) -> p s d n", s=2, d=2) for q in range(4)]
            return v[0:2], v[2:4]

        s5y = sc[:, 0:512].rearrange("p (t c) -> p t c", t=TT)
        s5z = sc[:, 512:1024].rearrange("p (t n) -> p t n", t=2)
        s5s = sc[:, 1024:1536].rearrange("p (t n) -> p t n", t=2)
        cvf = cv[:, :, :].rearrange("p t n -> p (t n)")
        yTf = yT[:, :, :].rearrange("p k n -> p (k n)")
        tst = yTf.rearrange("p (b s m) -> p b s m", b=2, s=2)
        spec_half = [spec[:, s].rearrange("p t n -> p (t n)") for s in range(2)]
        work = [sc[:, :], cvf]
        filt_ = [a.rearrange("p (t o d c) -> p t o d c", t=TT, o=2, d=2) for a in (yTf, ret[:, :])]
        fsq_ = [[a.rearrange("p (o d c) -> p o d c", o=2, d=2) for a in b]
                for b in ((spec_half[1], spec_half[0]), (vo[:, :], spec_half[0]))]
        pm_ = [a[:, 0:2048].rearrange("p (s t o c) -> p s t o c", s=2, t=TT, o=2) for a in work]
        rnorm_ = [lnf[:, 1536:2048], cvf[:, 2048:2560]]
        fx_ = [[a[0:64, i * 256:(i + 1) * 256] for i in range(4)] for a in work]
        tfr_ = [sc[:, 1024:1536], uT[:, :, :].rearrange("p t n -> p (t n)")]
        ct_s = [[a[:, i * 512:(i + 1) * 512].rearrange("p (j c) -> p j c", c=32) for i in range(4)]
                for a in (sc, yTf)]
        s5c = W("s5_c").rearrange("p (r j c) -> p r j c", r=2, c=32)
        s5b = W("s5_b").rearrange("p (t r m) -> p t r m", t=2, r=2)

        def sm(a, n):
            return small[:, a:a + n]

        mv = sm(0, 4).rearrange("p (t s) -> p t s", t=2)
        bst = sm(4, 24).rearrange("p (t c s) -> p t c s", t=2, c=2)
        var, rstd = sm(28, 2), sm(30, 2)
        hmean, hvar, hrstd = sm(32, 8), sm(40, 8), sm(48, 8)
        gts = sm(56, 32).rearrange("p (t g) -> p t g", t=2)
        colsb = sm(88, 32)
        emm, den, rden = sm(120, 16), sm(136, 16), sm(152, 16)
        s5v = [sm(168 + 16 * i, 16) for i in range(11)]
        mexp = sm(344, 1)
        mhalf = sm(345, 8)
        rt = [vo[:, 16 * i:16 * i + 16].rearrange("p (t e) -> p t e", t=2) for i in range(8)]
        posx = vo[:, 128:160].rearrange("p (t e) -> p t e", t=2)
        comb = vo[:, 160:192].rearrange("p (t e) -> p t e", t=2)
        cmp1 = vo[:, 192:320].rearrange("p (t a b) -> p t a b", t=2, a=8)
        cmp2 = vo[:, 320:448].rearrange("p (t a b) -> p t a b", t=2, a=8)
        rt1 = vo[:, 448:456]
        sil = [sc[:, i * 256:(i + 1) * 256] for i in range(2)]
        mid = sc[:, 512:768]
        onehot = sc[:, 1024:1280].rearrange("p (t s) -> p t s", t=2)
        gated = sc[:, 1280:1536].rearrange("p (t s) -> p t s", t=2)
        place = [sc[:, 1536 + i * 256:1792 + i * 256] for i in range(2)]
        acc = ret[:, :].rearrange("p (t d) -> p t d", t=2)
        xf = [a.rearrange("p (k s) -> p k s", s=P) for a in (cvf[:, 2 * NS * P:(NS + KT) * P], sc[:, 768:1024])]
        yex = yTf[:, 0:1024]

        s_id, s_cst, s_x, s_par, s_ln = sem("identity_in"), sem("const_in"), sem("x_in"), sem("params_in"), sem("ln_in")
        loaded = [sem(f"slot{i}_loaded") for i in range(SLOTS)]
        freed = sem("ring_freed")
        dch, ach, pch = sem("dve_chain"), sem("act_chain"), sem("pool_chain")
        ln_var, ln_rstd, h_ready, ht_ps, ht_ready = (
            sem("ln_var"), sem("ln_rstd"), sem("h_ready"), sem("ht_transposed"), sem("ht_ready"))
        mix_ready = sem("residual_psum")
        init = sem("init_done")
        f_mm, f_red, f_sin, f_raw, f_win, f_sq, f_sum, f_sqrt, f_pm, f_spm, f_spec = (
            sem("filt_mm"), sem("filt_reduced"), sem("filt_sin"), sem("filt_raw"), sem("filt_windowed"),
            sem("filt_squared"), sem("filt_norm_sum"), sem("filt_norm_sqrt"), sem("filt_plus_minus"),
            sem("filt_spec_mm"), sem("filt_spec"))
        c_dt, c_th, c_exp, c_cos = sem("s5_dt"), sem("s5_theta"), sem("s5_abs"), sem("s5_abar")
        t_ph, t_tab = sem("tab_phase"), sem("tab_sin")
        t_st = [sem(f"tab_stored{i}") for i in range(2)]
        s_tab = [sem(f"s5_table_in{i}") for i in range(2)]
        pj, u_ev, cv_c, cv_ev, rot_ev, vg_ev, vo_ev, gate_ev, silqk = (
            sem("proj_psum"), sem("u_evac"), sem("conv_centre"), sem("conv_done"), sem("rotary_done"),
            sem("ret_vg_ready"), sem("ml_vo_ready"), sem("gates_ready"), sem("ml_qk_ready"))
        z_tr, z_tm, z_sp, z_pr, z_iv, z_out = (
            sem("hy_z_transposed"), sem("hy_z_tm"), sem("hy_spec_psum"), sem("hy_product"),
            sem("hy_inverse"), sem("hy_z_ready"))
        r_tr, r_qk, r_s, r_st, r_o = (
            sem("ret_qk_transposed"), sem("ret_qkT"), sem("ret_scores"), sem("ret_decayed"), sem("ret_out"))
        n_var, n_rstd, n_y, n_tr, n_ev = (
            sem("hn_var"), sem("hn_rstd"), sem("hn_out"), sem("hn_transposed"), sem("hn_evac"))
        m_gt, m_g4, m_abs, m_exp, m_ln, m_rows, m_ct, m_cols, m_em, m_sc, m_msk, m_w, m_sw, m_nd = (
            sem("ml_gates_T"), sem("ml_gate_rows"), sem("ml_abs"), sem("ml_exp"), sem("ml_log"),
            sem("ml_rows"), sem("ml_cols_T"), sem("ml_cols"), sem("ml_floor"), sem("ml_scores"),
            sem("ml_masked"), sem("ml_weights"), sem("ml_weighted"), sem("ml_num_den"))
        b_sum = sem("s5_states_summed")
        b_mm, b_p, b_z, b_x, b_y, b_ysb, b_tr, b_v, b_g, b_glu, b_sig, b_out = (
            sem("s5_bu"), sem("s5_products"), sem("s5_scanned"), sem("s5_rotated"),
            sem("s5_y_psum"), sem("s5_y_tm"), sem("s5_y_transposed"), sem("s5_pre_gelu"),
            sem("s5_gelu"), sem("s5_glu_psum"), sem("s5_sigmoid"), sem("s5_out"))
        d_x, d_uh, d_ul, d_up, d_sil, d_pr, d_mh, d_mid, d_wh, d_dn = (
            sem("ffn_x_split"), sem("ffn_up_hi"), sem("ffn_up_split"), sem("ffn_up"), sem("ffn_silu"), sem("ffn_mid_f32"), sem("ffn_mid_hi"), sem("ffn_mid"),
            sem("ffn_w2_hi"), sem("ffn_down"))
        q_res = sem("residual_scaled")
        q_lg, q_l, q_ex, q_sel, q_pos, q_px = (
            sem("router_logits"), sem("router_centred"), sem("router_exp"), sem("router_selected"),
            sem("router_pos_psum"), sem("router_done"))
        e_pr, e_mt, e_mh, e_wh, e_uh, e_ul, e_uu, e_xh = (
            sem("ex_mid_f32"), sem("ex_mid_transposed"), sem("ex_mid_hi"), sem("ex_w2_hi"), sem("ex_up_hi_ready"),
            sem("ex_up_split"), sem("ex_up_used"), sem("ex_x_hi"))
        e_p, e_g, e_xg, e_tm, e_t, e_up, e_sil, e_mid, e_dn, e_y, e_sc, e_acc = (
            sem("ex_onehot"), sem("ex_gather_psum"), sem("ex_x"), sem("ex_place_psum"), sem("ex_place"),
            sem("ex_up"), sem("ex_silu"), sem("ex_mid"), sem("ex_down"), sem("ex_y"), sem("ex_scatter_psum"),
            sem("ex_accumulated"))
        s_out = sem("out_written")

        def slot_use(g):
            if g < G_MOE:
                return PLAN[g], 16 * PLAN[:g + 1].count(PLAN[g])
            s = MOE_SLOTS[(g - G_MOE) % SLOTS]
            return s, 16 * (PLAN.count(s) + (g - G_MOE) // SLOTS + 1)

        def uses_before(g):
            if g >= G_MOE + SLOTS:
                return g - SLOTS + 1
            s = slot_use(g)[0]
            return max([i + 1 for i in range(min(g, G_MOE)) if PLAN[i] == s], default=0)

        def unit_evacuated(eng, l, i):
            if i == 0:
                eng.wait_ge(u_ev, l + 1)
            elif i < 6:
                eng.wait_ge(cv_ev, 5 * l + i)
            elif i < 8:
                eng.wait_ge(rot_ev, 2 * l + i - 5)
            elif i < 10:
                eng.wait_ge(vg_ev, 2 * l + i - 7)
            elif i < 12:
                eng.wait_ge(vo_ev, 2 * l + i - 9)

        NPRE = 21
        BESIDE = [(0,), (1,), (2, 3), (4, 5, 6), (7, 8, 9), (10, 11), (12, 13), (14, 15), (16, 17), (18, 19), (20,),
                  (), ()]
        NLN = 5

        block = ctx.enter_context(nc.Block())

        @block.sync
        def _(sp):
            def load_slot(g, src, n=SLOT):
                s, _ = slot_use(g)
                if uses_before(g):
                    sp.wait_ge(freed, uses_before(g))
                sp.dma_start(ring[s][:, 0:n], src).then_inc(loaded[s], 16)

            def load_ln(n):
                if n:
                    sp.wait_ge(h_ready, 2 * n)
                sp.dma_start(lnb[:, :], ln[n]).then_inc(s_ln, 16)

            sp.dma_start(h[:, :, :], x.rearrange("(t p) d -> p t d", p=P)).then_inc(s_x, 16)
            load_ln(0)
            first = slice(*CONST["ident"])
            sp.dma_start(cst[:, first], const[:, first]).then_inc(s_id, 16)
            for l in range(DEPTH):
                g0 = l * G_MIX1
                for i in range(4):
                    if l == 1 and i == 2:
                        sp.wait_ge(d_dn, 2 * NC_FF)
                        load_ln(2)
                    load_slot(g0 + i, w_in[l, i])
                    if l == 0 and i == 0:
                        sp.dma_start(pr[:, :], par[0]).then_inc(s_par, 16)
                        for a, b in ((0, first.start), (first.stop, CONST_W)):
                            sp.dma_start(cst[:, a:b], const[:, a:b]).then_inc(s_cst, 16)
                for i in range(2):
                    load_slot(g0 + 4 + i, w_out[l, i], KT * 512)
                sp.wait_ge(freed, g0 + 3)
                for q in range(2):
                    sp.wait_ge(t_st[q], 16 * 4 * (l + 1))
                a, b = borrowed(l)
                sp.dma_start(a[:, :].rearrange("p (i m) -> p i m", i=6),
                             tab[l, 0:6].rearrange("i p m -> p i m")).then_inc(s_tab[0], 16)
                sp.wait_ge(freed, g0 + 4)
                sp.dma_start(b[:, 0:2048].rearrange("p (i m) -> p i m", i=2),
                             tab[l, 6:8].rearrange("i p m -> p i m")).then_inc(s_tab[1], 16)
                sp.wait_ge(b_y, 8 * (l + 1))
                for i in range(2):
                    load_slot(g0 + RING_MIX + i, ffn[i] if l == 0 else moe[i])
                sp.wait_ge(n_tr, 2 * l + 2)
                load_ln(1 + 2 * l)
                if l == 0:
                    sp.wait_ge(b_out, 1)
                    sp.wait_ge(n_ev, 2)
                    sp.wait_ge(z_out, 2)
                    sp.dma_start(pr[:, :], par[1]).then_inc(s_par, 16)
                    for i in range(2, 4):
                        load_slot(G_FF + i, ffn[i])
                    for i in range(4, NC_FF):
                        load_slot(G_FF + i, ffn[i])
            for c in range(2, 4):
                load_slot(G_MOE + c, moe[c])
            load_ln(4)
            for c in range(4, 2 * NC_E):
                load_slot(G_MOE + c, moe[c])

            def load_experts(first, g0):
                with sp.Fori(first, NE // 2) as i:
                    for c in range(2 * NC_E):
                        s, _ = slot_use(g0 + c)
                        sp.wait_ge(freed, i * (2 * NC_E) + (g0 + c - SLOTS + 1))
                        sp.dma_start(ring[s][:, :], moe[bass.ds(i * (2 * NC_E) + c, 1)].rearrange("a p n -> (a p) n")
                                     ).then_inc(loaded[s], 16)

            load_experts(1, G_MOE)
            load_slot(G_MOE + NE * NC_E, moe[0])
            sp.wait_ge(q_px, 1)
            crowded = sp.value_load(over[0:1, 0:1], min_val=0, max_val=1)
            with sp.If(crowded == 1):
                for c in range(1, 2 * NC_E):
                    load_slot(G_MOE + NE * NC_E + c, moe[c])
                load_experts(1, G_MOE + NE * NC_E)
                load_slot(G_MOE + 2 * NE * NC_E, moe[0])
            for t in range(TT):
                sp.wait_ge(h_ready, 2 * NLN - TT + t + 1)
                sp.dma_start(out[t * P:(t + 1) * P, :], h[:, t, :]).then_inc(s_out, 16)
            sp.wait_ge(s_out, 16 * TT)

        @block.gpsimd
        def _(po):
            nc.gpsimd.memset(mhalf, -0.5).then_inc(init, 1)
            po.wait_ge(init, 1)
            for n in range(NLN):
                if n in (1, 3):
                    l = n // 2
                    for m in range(2):
                        for i in range(4 * m, 4 * m + 4):
                            po.wait_ge(b_x, 2 * (8 * l + i + 1))
                            T = s5_table(l, i)
                            nc.gpsimd.tensor_tensor(T, T, s5_work(l)[1][i % 2], ALU.add).then_inc(b_sum, 1)
                        k = n - 1 + m
                        po.wait_ge(n_var, k + 1)
                        nc.gpsimd.tensor_tensor(hrstd, hvar, mhalf, ALU.pow).then_inc(n_rstd, 1)
                po.wait_ge(ln_var, n + 1)
                nc.gpsimd.tensor_tensor(rstd, var, mhalf[:, 0:2], ALU.pow).then_inc(ln_rstd, 1)
                if n == 3:
                    nc.gpsimd.memset(comb, 0.0)
                    nc.gpsimd.memset(posx, 4096.0)
                    nc.gpsimd.memset(place[1], 0.0).then_inc(init, 1)

        @block.tensor
        def _(pe):
            mm, tr = nc.tensor.matmul, nc.tensor.transpose

            def transposes_of_h(n):
                for j in range(4):
                    pe.wait_ge(h_ready, 2 * n + j // 2 + 1)
                    for q in range(4):
                        k = 4 * (j % 2) + q
                        ins = tr(bank[j][:, q * P:(q + 1) * P], h[:, j // 2, k * P:(k + 1) * P], ident)
                    ins.then_inc(ht_ps, 1)

            def pre(l, k):
                fx, fsq, pm = fx_[l], fsq_[l], pm_[l]
                if k == 0:
                    pe.wait_ge(s_par, 16 * (l + 1))
                    pe.wait_ge(s_cst, 32)
                    mm(bank[6][0:64, 0:L], w1_feat, z_feat, start=True, stop=True).then_inc(f_mm, 1)
                elif k == 1:
                    pe.wait_ge(f_sin, 2 * l + 1)
                    mm(bank[7][0:64, 0:L], W("hy_w12", 64), fx[3], start=True, stop=True).then_inc(f_mm, 1)
                elif k < 6:
                    j = k - 2
                    if j == 0:
                        pe.wait_ge(f_sin, 2 * l + 2)
                        pe.wait_ge(f_red, 2 * l + 2)
                    if j >= 2:
                        pe.wait_ge(f_win, 4 * l + j - 1)
                    mm(bank[6 + j % 2][:, :], fx[3][:, (j // 2) * P:(j // 2 + 1) * P],
                       W("hy_w3", 64)[:, (j % 2) * 512:(j % 2 + 1) * 512], start=True, stop=True).then_inc(f_raw, 1)
                elif k == 6:
                    pe.wait_ge(f_win, 4 * l + 4)
                    for t in range(TT):
                        pe.wait_ge(f_sq, 2 * l + t + 1)
                        for d in range(2):
                            ins = mm(bank[6][:, :], K("ones"), fsq[t][:, :, d, :], start=(t == 0 and d == 0),
                                     stop=(t == 1 and d == 1))
                    ins.then_inc(f_sum, 1)
                elif k < 11:
                    j = k - 7
                    pe.wait_ge(f_pm, l + 1)
                    pe.wait_ge(f_sqrt, l + 1)
                    if j >= 2:
                        pe.wait_ge(f_spec, 4 * l + j - 1)
                    s, ft = j // 2, j % 2
                    for t in range(TT):
                        ins = mm(bank[6 + (j + 1) % 2][:, :], dft[s][:, t, ft * P:(ft + 1) * P],
                                 pm[:, s, t].rearrange("p o c -> p (o c)"), start=(t == 0), stop=(t == 1))
                    ins.then_inc(f_spm, 1)

            def project(l):
                g0 = l * G_MIX1
                pe.wait_ge(ht_ready, 8 * l + 4)
                for i in range(13):
                    b = bank[i % 4]
                    if i >= 4:
                        unit_evacuated(pe, l, i - 4)
                    if i in (0, 3, 6, 8, 10):
                        s, v = slot_use(g0 + {0: 0, 3: 1, 6: 2, 8: 3, 10: 3}[i])
                        pe.wait_ge(loaded[s], v)
                    if i < 6:
                        w = ring[slot_use(g0 + i // 3)[0]][:, :].rearrange("p (k n) -> p k n", k=KT)
                        for q in range(2):
                            c = (2 * (i % 3) + q) * P
                            for k in range(KT):
                                ins = mm(b[:, q * L:(q + 1) * L], w[:, k, c:c + P], hT[:, k, :],
                                         start=(k == 0), stop=(k == KT - 1))
                    elif i < 12:
                        part, t = (i - 6) // 2, i % 2
                        w2 = [ring[slot_use(g0 + 2 + j)[0]][:, :].rearrange("p (k n) -> p k n", k=KT) for j in range(2)]
                        pieces = [[(0, w2[0], 0, 512)], [(0, w2[0], 512, 256), (256, w2[1], 0, 256)],
                                  [(0, w2[1], 256, 512)]][part]
                        for o, w, c, n in pieces:
                            for k in range(KT):
                                ins = mm(b[:, o:o + n], hT[:, k, t * P:(t + 1) * P], w[:, k, c:c + n],
                                         start=(k == 0), stop=(k == KT - 1))
                    else:
                        gw = W("gate_w").rearrange("p (k n) -> p k n", k=KT)
                        for t in range(TT):
                            for k in range(KT):
                                ins = mm(b[:, t * 16:(t + 1) * 16], hT[:, k, t * P:(t + 1) * P], gw[:, k, :],
                                         start=(k == 0), stop=(k == KT - 1))
                    ins.then_inc(pj, 1)
                    if i in (2, 5, 9, 11):
                        pe.wait_ge(pj, 13 * l + i + 1)
                        pe.sem_inc(freed, 1)
                    if l == 0:
                        for k in BESIDE[i]:
                            pre(0, k)

            def hyena_forward(l, n):
                u = 2 * l + n
                pe.wait_ge(cv_ev, 5 * l + 3) if n == 0 else pe.wait_ge(z_out, 2 * l + 1)
                for t in range(TT):
                    for c in range(2):
                        src = cv[:, c, t * P:(t + 1) * P]
                        ins = tr(bank[0][:, t * DG + c * P:t * DG + (c + 1) * P], src, ident)
                ins.then_inc(z_tr, 1)
                pe.wait_ge(z_tm, u + 1)
                for s in range(2):
                    for ft in range(2):
                        for t in range(TT):
                            ins = mm(bank[1 + s][:, ft * DG:(ft + 1) * DG], dft[s][:, t, ft * P:(ft + 1) * P],
                                     ztm[:, t, :], start=(t == 0), stop=(t == 1))
                ins.then_inc(z_sp, 1)

            def hyena_inverse(l, n):
                pe.wait_ge(z_pr, 2 * l + n + 1)
                for c in range(2):
                    for s in range(2):
                        for ft in range(2):
                            ins = mm(bank[0][:, c * L:(c + 1) * L],
                                     hy_t[2 * s][:, ft * DG + c * P:ft * DG + (c + 1) * P], idft[s][:, ft, :],
                                     start=(s == 0 and ft == 0), stop=(s == 1 and ft == 1))
                ins.then_inc(z_iv, 1)

            def head_out(m, b):
                pe.wait_ge(n_y, m + 1)
                for c in range(2):
                    for t in range(TT):
                        ins = tr(bank[b][:, c * L + t * P:c * L + (t + 1) * P], ytm[:, t, c * P:(c + 1) * P], ident)
                ins.then_inc(n_tr, 1)

            def ret_transposes(l):
                for half in range(2):
                    for q in range(2):
                        for t in range(TT):
                            pe.wait_ge(rot_ev, 2 * l + t + 1)
                            ft = 2 * half + q
                            ins = tr(bank[4 + half][:, q * L + t * P:q * L + (t + 1) * P],
                                     rq[:, t, ft * P:(ft + 1) * P], ident)
                    ins.then_inc(r_tr, 1)
                pe.wait_ge(r_qk, 2 * l + 2)
                pe.wait_ge(vg_ev, 2 * l + 2)

            def ret_scores(l, a):
                o = HD * (a % 2)
                if a >= 2:
                    pe.wait_ge(r_st, 4 * l + a - 1)
                for t in range(TT):
                    ins = mm(bank[5 + a % 2][:, t * L:(t + 1) * L], qkT[o:o + HD, 2 + a // 2, t * P:(t + 1) * P],
                             qkT[o:o + HD, a // 2, :], start=True, stop=True)
                ins.then_inc(r_s, 1)

            def ret_out(l, a):
                pe.wait_ge(r_st, 4 * l + a + 1)
                for t in range(TT):
                    for m in range(TT):
                        ins = mm(bank[4][:, t * DG + a * HD:t * DG + (a + 1) * HD],
                                 st[:, a % 2, m, t * P:(t + 1) * P], vg[:, m, a * HD:(a + 1) * HD],
                                 start=(m == 0), stop=(m == 1))
                if a == H - 1:
                    ins.then_inc(r_o, 1)

            def ml_gate_rows(l):
                pe.wait_ge(n_ev, 2 * l + 1)
                for k in range(4):
                    for t in range(TT):
                        ins = tr(bank[5 + k // 2][0:H, (k % 2) * L + t * P:(k % 2) * L + (t + 1) * P],
                                 gts[:, t, 4 * k:4 * k + 4], ident)
                ins.then_inc(m_gt, 1)

            def ml_columns(l):
                pe.wait_ge(m_rows, l + 1)
                for s, row in enumerate((brow, nmrow)):
                    for d in range(2):
                        for t in range(TT):
                            c = (s * 4 + d * 2 + t) * H
                            ins = tr(bank[6][:, c:c + H], row[:, d, t * P:(t + 1) * P], ident[0:H, 0:H])
                ins.then_inc(m_ct, 1)
                pe.wait_ge(silqk, 2 * l + 2)

            def ml_scores(l, a):
                o = HD * (a % 2)
                if a >= 2:
                    pe.wait_ge(m_sw, 4 * l + a - 1)
                for t in range(TT):
                    mm(bank[a % 2][:, t * L:(t + 1) * L], cv[o:o + HD, 8 + a // 2, t * P:(t + 1) * P],
                       cv[o:o + HD, 6 + a // 2, :], start=True, stop=True)
                if a:
                    pe.wait_ge(m_w, 24 * l + 6 * a)
                for d in range(2):
                    ins = mm(bank[2][:, d * L:(d + 1) * L], K("pick", H)[:, a * P:(a + 1) * P],
                             crow[:, d, :], start=True, stop=True)
                ins.then_inc(m_sc, 1)

            def ml_out(l, a):
                if a == 0:
                    pe.wait_ge(m_cols, l + 1)
                    pe.wait_ge(vo_ev, 2 * l + 2)
                ones = K("ones")[:, 0:1]
                pe.wait_ge(m_sw, 4 * l + a + 1)
                w = wml[:, a % 2]
                for d in range(2):
                    for t in range(TT):
                        parts = [(w[:, 3 * d + t], t)]
                        if t == 1 - d:
                            parts.append((w[:, 3 * d + 2], d))
                        for j, (blk, m) in enumerate(parts):
                            s0, s1 = j == 0, j == len(parts) - 1
                            mm(bank[4 + d][:, t * DG + a * HD:t * DG + (a + 1) * HD], blk,
                               vo[:, m * 512 + a * HD:m * 512 + (a + 1) * HD], start=s0, stop=s1)
                        for j, (blk, m) in enumerate(parts):
                            s0, s1 = j == 0, j == len(parts) - 1
                            c = (d * 2 + t) * H + a
                            ins = mm(bank[6][:, c:c + 1], blk, ones, start=s0, stop=s1)
                if a == H - 1:
                    ins.then_inc(m_nd, 1)

            def s5_in(l, i):
                if i:
                    pe.wait_ge(b_p, 8 * l + i)
                r = 32 * (i % 4)
                for s in range(2):
                    ins = mm(bank[3][:, s * L:(s + 1) * L], s5b[r:r + 32, i // 4, s, :],
                             uT[r:r + 32, i // 4, :], start=True, stop=True)
                ins.then_inc(b_mm, 1)

            def s5_y(l, i):
                xs = s5_table(l, i)
                pe.wait_ge(b_sum, 8 * l + i + 1)
                for t in range(TT):
                    n = 0
                    for d in range(2):
                        for part in range(2):
                            ins = mm(bank[7][:, t * DG + i * 32:t * DG + (i + 1) * 32],
                                     xs[:, part, d, t * P:(t + 1) * P], s5c[:, part, 2 * i + d, :],
                                     start=(n == 0), stop=(n == 3))
                            n += 1
                ins.then_inc(b_y, 1)

            def s5_beside(l, i):
                if i:
                    s5_y(l, i - 1)
                if i < 7:
                    s5_in(l, i + 1)

            def s5_transposes(l):
                pe.wait_ge(b_ysb, l + 1)
                for c in range(2):
                    for t in range(TT):
                        ins = tr(bank[5][:, c * L + t * P:c * L + (t + 1) * P], s5y[:, t, c * P:(c + 1) * P], ident)
                ins.then_inc(b_tr, 1)

            def s5_glu(l):
                pe.wait_ge(b_g, l + 1)
                wg = W("glu").rearrange("p (k n) -> p k n", k=2)
                for c in range(2):
                    for k in range(2):
                        ins = mm(bank[4][:, c * L:(c + 1) * L], wg[:, k, c * P:(c + 1) * P], s5z[:, k, :],
                                 start=(k == 0), stop=(k == 1))
                ins.then_inc(b_glu, 1)

            def out_projection(l, ks, first=False, last=False):
                g0 = l * G_MIX1 + 4
                for hf in range(2):
                    s, v = slot_use(g0 + hf)
                    if first:
                        pe.wait_ge(loaded[s], v)
                    w = ring[s][:, 0:KT * 512].rearrange("p (k n) -> p k n", k=KT)
                    for t in range(TT):
                        for k in ks:
                            ins = mm(bank[2 * t + hf][:, :], yT[:, k, t * P:(t + 1) * P], w[:, k, :],
                                     start=(first and k == ks[0]), stop=(last and k == ks[-1]))
                    if last:
                        ins.then_inc(freed, 1)
                if last:
                    pe.wait_ge(freed, g0 + 2)
                    pe.sem_inc(mix_ready, 1)

            def mixers(l):
                for i in range(9, 13):
                    unit_evacuated(pe, l, i)
                pe.wait_ge(gate_ev, l + 1)
                s5_in(l, 0)
                hyena_forward(l, 0)
                s5_beside(l, 0)
                hyena_inverse(l, 0)
                s5_beside(l, 1)
                ret_transposes(l)
                ret_scores(l, 0)
                ret_scores(l, 1)
                ret_out(l, 0)
                ret_scores(l, 2)
                ret_out(l, 1)
                ret_scores(l, 3)
                s5_beside(l, 2)
                ret_out(l, 2)
                ret_out(l, 3)
                s5_beside(l, 3)
                hyena_forward(l, 1)
                head_out(2 * l, 5)
                hyena_inverse(l, 1)
                ml_gate_rows(l)
                s5_beside(l, 4)
                s5_beside(l, 5)
                ml_columns(l)
                ml_scores(l, 0)
                s5_beside(l, 6)
                ml_scores(l, 1)
                ml_out(l, 0)
                ml_scores(l, 2)
                ml_out(l, 1)
                s5_beside(l, 7)
                ml_scores(l, 3)
                ml_out(l, 2)
                ml_out(l, 3)
                s5_y(l, 7)
                pe.wait_ge(z_out, 2 * l + 2)
                pe.wait_ge(m_sw, 4 * l + 4)
                pe.wait_ge(m_w, 24 * l + 24)
                pe.wait_ge(b_p, 8 * l + 8)
                out_projection(l, (0, 1), first=True)
                head_out(2 * l + 1, 6)
                s5_transposes(l)
                out_projection(l, (4, 5))
                s5_glu(l)
                pe.wait_ge(n_ev, 2 * l + 2)
                out_projection(l, (6, 7))
                pe.wait_ge(b_out, l + 1)
                out_projection(l, (2, 3), last=True)

            def dense():
                NU = 2 * NC_FF

                def up(u):
                    for w in range(2):
                        pe.wait_ge(d_ul, 2 * u + w + 1)
                        for k in range(KT):
                            for n, (i, j) in enumerate(SPLIT):
                                ins = mm(bank[4 + u % 2][:, w * L:(w + 1) * L], ff_up[j][:, w, k, :],
                                         ff_x[i][:, k, :], start=(k == 0 and n == 0), stop=(k == KT - 1 and n == 2))
                        ins.then_inc(d_up, 1)

                def down(u):
                    pe.wait_ge(d_mid, 2 * u + 2)
                    for t in range(TT):
                        for hf in range(2):
                            for n, (i, j) in enumerate(SPLIT):
                                ins = mm(bank[2 * t + hf][:, :], ff_mid[i][:, u % 2, t * P:(t + 1) * P],
                                         ff_w2[j][:, hf * 512:(hf + 1) * 512], start=(u == 0 and n == 0),
                                         stop=(u == NU - 1 and n == 2))
                    ins.then_inc(d_dn, 1)

                pe.wait_ge(d_x, 4)
                for u in range(NU):
                    up(u)
                    if u:
                        down(u - 1)
                    if u < NPRE:
                        pre(1, u)
                down(NU - 1)

            pe.wait_ge(s_id, 16)
            transposes_of_h(0)
            for l in range(DEPTH):
                project(l)
                mixers(l)
                transposes_of_h(2 * l + 1)
                if l == 0:
                    dense()
                    transposes_of_h(2)

            pe.wait_ge(ht_ready, 16)
            rw = W("router").rearrange("p (k n) -> p k n", k=KT)
            for t in range(TT):
                for k in range(KT):
                    ins = mm(bank[6][:, t * NE:(t + 1) * NE], hT[:, k, t * P:(t + 1) * P], rw[:, k, :],
                             start=(k == 0), stop=(k == KT - 1))
            ins.then_inc(q_lg, 1)
            pe.wait_ge(q_sel, 1)
            sel = rt[1]
            mm(bank[7][:, 0:NE], K("before"), sel[:, 0, :], start=True, stop=True)
            mm(bank[7][:, NE:2 * NE], K("ones"), sel[:, 0, :], start=True, stop=False)
            mm(bank[7][:, NE:2 * NE], K("before"), sel[:, 1, :], start=False, stop=True)
            mm(bank[7][:, 2 * NE:3 * NE], K("ones"), sel[:, 0, :], start=True, stop=False)
            mm(bank[7][:, 2 * NE:3 * NE], K("ones"), sel[:, 1, :], start=False, stop=True).then_inc(q_pos, 1)

            def gather(v, j):
                pe.wait_ge(e_p, v + 1)
                for q in range(4):
                    k = 4 * j + q
                    for t in range(TT):
                        ins = mm(bank[6 + j][:, q * P:(q + 1) * P], h[:, t, k * P:(k + 1) * P],
                                 onehot[:, t, :], start=(t == 0), stop=(t == 1))
                ins.then_inc(e_g, 1)

            def placing(v):
                pe.wait_ge(e_xg, v * 2 + 1)
                for t in range(TT):
                    ins = tr(bank[6][:, t * P:(t + 1) * P], gated[:, t, :], ident)
                ins.then_inc(e_tm, 1)

            def scatter(v, par, q0):
                if q0 == 0:
                    pe.wait_ge(e_y, v * 2 + 2)
                    pe.wait_ge(e_t, v + 1)
                    pe.wait_ge(e_xg, v * 2 + 2)
                for q in (q0, q0 + 1):
                    if q >= 2:
                        pe.wait_ge(e_acc, v * 4 + (q - 1))
                    mm(bank[6 + q % 2][:, :], place[par][:, (q // 2) * P:(q // 2 + 1) * P],
                       yex[:, (q % 2) * 512:(q % 2 + 1) * 512], start=True, stop=True).then_inc(e_sc, 1)

            def expert(v, n, j, loads):
                def up(c):
                    s = slot_use(G_MOE + j * NC_E + c)[0]
                    pe.wait_ge(loaded[s], loads(c))
                    b = bank[4 + c % 2]
                    for q in range(2):
                        pe.wait_ge(e_ul, (n * NC_E + c) * 2 + (q + 1))
                        if c == 0:
                            pe.wait_ge(e_xg, v * 2 + (q + 1))
                        for k in range(HS * q, HS * (q + 1)):
                            for m, (x_, w_) in enumerate(SPLIT):
                                ins = mm(b[:, :], ex_x[j][x_][:, k, :], ex_up[w_][:, k, :],
                                         start=(k == 0 and m == 0), stop=False)
                        ins.then_inc(e_uu, 1)
                        if q == 0 and c:
                            mid_transposes(c - 1)
                    wt = ring[s][:, 0:2 * KT * FC].rearrange("p (k n) -> p k n", k=KT)
                    for k in range(NS, KT):
                        ins = mm(b[:, :], xf[j][:, k - NS, :], wt[:, k, :], start=False, stop=(k == KT - 1))
                    ins.then_inc(e_up, 1)

                def mid_transposes(c):
                    pe.wait_ge(e_pr, n * NC_E + (c + 1))
                    for f in range(2):
                        ins = tr(bank[4 + c % 2][:, f * P:(f + 1) * P], mid[:, f * P:(f + 1) * P], ident)
                    ins.then_inc(e_mt, 1)

                def down(c):
                    pe.wait_ge(e_mid, n * NC_E + (c + 1))
                    pe.wait_ge(freed, n * NC_E + (G_MOE + c + 1))
                    for hf in range(2):
                        for f in range(2):
                            for m, (a, b) in enumerate(SPLIT):
                                ins = mm(bank[2 * j + hf][:, :], ex_mid[a][:, c % 2, f * P:(f + 1) * P],
                                         ex_w2[b][:, f, hf * 512:(hf + 1) * 512],
                                         start=(c == 0 and f == 0 and m == 0),
                                         stop=(c == NC_E - 1 and f == 1 and m == 2))
                    ins.then_inc(e_dn, 1)

                for c in range(NC_E):
                    up(c)
                    if c:
                        down(c - 1)
                    if c in (3, 5):
                        scatter(v, 1 - j, c - 3)
                    if c == 8:
                        pe.wait_ge(e_acc, v * 4 + 4)
                        gather(v + 1, 0)
                    if c == 10:
                        placing(v + 1)
                mid_transposes(NC_E - 1)
                gather(v + 1, 1)
                down(NC_E - 1)

            pe.sem_inc(e_dn, 1)

            def all_experts(b):
                v0, n0 = b * (NE + 1), b * NE
                gather(v0, 0)
                gather(v0, 1)
                placing(v0)
                with pe.Fori(0, NE // 2) as i:
                    for j in range(2):
                        def loads(c, j=j):
                            return i * (16 * 2 * NC_E // SLOTS) + slot_use(G_MOE + (n0 + j) * NC_E + c)[1]
                        expert(i * 2 + (v0 + j), i * 2 + (n0 + j), j, loads)
                scatter(v0 + NE, 1, 0)
                scatter(v0 + NE, 1, 2)

            all_experts(0)
            crowded = pe.value_load(over[0:1, 0:1], min_val=0, max_val=1)
            with pe.If(crowded == 1):
                all_experts(1)

        @block.scalar
        def _(ac):
            act = nc.scalar.activation

            def evacuate_h(n):
                dst = ff_x[0] if n == 1 else hT
                for j in range(4):
                    ac.wait_ge(ht_ps, 4 * n + j + 1)
                    k = 4 * (j % 2)
                    act(dst[:, k:k + 4, (j // 2) * P:(j // 2 + 1) * P],
                        bank[j][:, :].rearrange("p (q n) -> p q n", q=4), ACT.Copy).then_inc(ht_ready, 1)

            def pre(l, k):
                fx, fsq, filt, rnorm, tfr = fx_[l], fsq_[l], filt_[l], rnorm_[l], tfr_[l]
                if k in (0, 1):
                    ac.wait_ge(f_red, 2 * l + k + 1)
                    act(fx[3], fx[2], ACT.Sin).then_inc(f_sin, 1)
                elif k in (3, 5):
                    t = (k - 3) // 2
                    ac.wait_ge(f_win, 4 * l + 2 * t + 2)
                    act(fsq[t], filt[:, t], ACT.Square).then_inc(f_sq, 1)
                elif k == 6:
                    ac.wait_ge(f_sum, l + 1)
                    act(rnorm, bank[6][:, :], ACT.Sqrt).then_inc(f_sqrt, 1)
                elif k == 11:
                    ac.wait_ge(s_par, 16 * (l + 1))
                    act(s5v[0], W("log_dt"), ACT.Exp).then_inc(c_dt, 1)
                    ac.wait_ge(c_th, l + 1)
                    act(s5v[4], s5v[1], ACT.Exp).then_inc(c_exp, 1)
                    act(s5v[5], s5v[3], ACT.Abs).then_inc(ach, 1)
                    act(s5v[6], s5v[3], ACT.Sin, scale=TURN).then_inc(c_exp, 1)
                    ac.wait_ge(ach, l + 1)
                    act(s5v[7], s5v[5], ACT.Sin, scale=-TURN, bias=K("halfpi")).then_inc(c_exp, 1)
                elif 13 <= k < 21:
                    i = k - 13
                    v = 8 * l + i
                    ac.wait_ge(t_ph, v + 1)
                    if i >= 2:
                        ac.wait_ge(t_st[i % 2], 16 * (v // 2))
                    b = tst[:, i % 2]
                    act(b[:, 1], tfr, ACT.Sin, scale=TURN).then_inc(t_tab, 1)
                    act(b[:, 0], tfr, ACT.Abs).then_inc(t_tab, 1)
                    ac.wait_ge(t_tab, 3 * v + 2)
                    act(b[:, 0], b[:, 0], ACT.Sin, scale=-TURN, bias=K("halfpi")).then_inc(t_tab, 1)
                    ac.wait_ge(t_tab, 3 * v + 3)
                    ac.dma_start(tab[l, i].rearrange("p (s n) -> p s n", s=2), b).then_inc(t_st[i % 2], 16)

            def project(l):
                for i in range(13):
                    b = bank[i % 4]
                    if i == 0:
                        ac.wait_ge(pj, 13 * l + 1)
                        act(uT[:, :, :], b[:, :].rearrange("p (t n) -> p t n", t=2), ACT.Copy).then_inc(u_ev, 1)
                    elif i < 6:
                        ac.wait_ge(pj, 13 * l + i + 1)
                        for q in range(2):
                            t = 2 * (i - 1) + q
                            act(cv[:, t, :], b[:, q * L:(q + 1) * L], ACT.Identity,
                                scale=conv_w[:, t, 1:2], bias=conv_w[:, t, 3:4]).then_inc(cv_c, 1)
                    elif i < 8:
                        ac.wait_ge(cv_ev, 5 * l + i - 2)
                        j = 6 + 2 * (i - 6)
                        act(cv[:, j:j + 2, :], cv[:, j:j + 2, :], ACT.Silu).then_inc(silqk, 1)
                    elif i < 10:
                        ac.wait_ge(pj, 13 * l + i + 1)
                        t = i - 8
                        act(vg[:, t, 0:256], b[:, 0:256], ACT.Copy)
                        act(vg[:, t, 256:512], b[:, 256:512], ACT.Silu).then_inc(vg_ev, 1)
                    elif i < 12:
                        ac.wait_ge(pj, 13 * l + i + 1)
                        t = i - 10
                        act(vo[:, t * 512:t * 512 + 256], b[:, 0:256], ACT.Copy)
                        act(vo[:, t * 512 + 256:(t + 1) * 512], b[:, 256:512], ACT.Sigmoid).then_inc(vo_ev, 1)
                    if l == 0:
                        for k in BESIDE[i]:
                            pre(0, k)

            def hyena(l, n):
                u = 2 * l + n
                ac.wait_ge(z_tr, u + 1)
                act(sc[:, 0:512], bank[0][:, :], ACT.Copy).then_inc(z_tm, 1)

            def head_out(m, b, gn, k0):
                ac.wait_ge(n_tr, m + 1)
                for q in range(2):
                    ac.wait_ge(t_st[q], 16 * 4 * (m // 2 + 1))
                for c in range(2):
                    ins = act(yT[:, k0 + c, :], bank[b][:, c * L:(c + 1) * L], ACT.Copy, scale=gn[:, c:c + 1])
                ins.then_inc(n_ev, 1)

            def ret_qk(l):
                for half in range(2):
                    ac.wait_ge(r_tr, 2 * l + half + 1)
                    act(qkT[:, 2 * half:2 * half + 2, :], bank[4 + half][:, :].rearrange("p (q n) -> p q n", q=2),
                        ACT.Copy).then_inc(r_qk, 1)
            def mlstm(l):
                ac.wait_ge(m_gt, l + 1)
                for j in range(2):
                    act(g4[:, 2 * j:2 * j + 2, :], bank[5 + j][0:H, :].rearrange("p (k n) -> p k n", k=2),
                        ACT.Copy).then_inc(m_g4, 1)
                ac.wait_ge(m_abs, l + 1)
                act(ex, ex, ACT.Exp, scale=-1.0).then_inc(m_exp, 1)
                ac.wait_ge(m_exp, l + 1)
                act(ex, ex, ACT.Ln, bias=1.0).then_inc(m_ln, 1)
                ac.wait_ge(m_cols, l + 1)
                act(emm, colsb[:, 16:32], ACT.Exp).then_inc(m_em, 1)
                for a in range(H):
                    ac.wait_ge(m_sc, 4 * l + a + 1)
                    if a >= 2:
                        ac.wait_ge(m_sw, 4 * l + a - 1)
                    w, c = wml[:, a % 2], bank[2]
                    ac.wait_ge(m_msk, 4 * l + a + 1)
                    for d in range(2):
                        m, n = (0, 1) if d == 0 else (1, 0)
                        col = (d * 2 + m) * H + a
                        act(w[:, 3 * d + 2], c[:, d * L + n * P:d * L + (n + 1) * P], ACT.Exp, scale=-1.0,
                            bias=colsb[:, col:col + 1]).then_inc(m_w, 1)
                        for t in range(TT):
                            col = (d * 2 + t) * H + a
                            act(w[:, 3 * d + t], wmask[:, a % 2, d, t, :], ACT.Exp,
                                bias=colsb[:, col:col + 1]).then_inc(m_w, 1)

            def s5(l):
                ac.wait_ge(b_y, 8 * (l + 1))
                ac.wait_ge(n_y, 2 * l + 2)
                act(sc[:, 0:512], bank[7][:, :], ACT.Copy).then_inc(b_ysb, 1)
                head_out(2 * l + 1, 6, W("ml_gn"), 6)
                ac.wait_ge(b_v, l + 1)
                act(s5z, s5z, ACT.Gelu_apprx_tanh).then_inc(b_g, 1)
                ac.wait_ge(b_glu, l + 1)
                act(s5s, bank[4][:, :].rearrange("p (t n) -> p t n", t=2), ACT.Sigmoid).then_inc(b_sig, 1)

            def split_up(g, q, loaded_value, s):
                if q == 0:
                    ac.wait_ge(loaded[s], loaded_value)
                wt = ring[s][:, 0:2 * KT * FC].rearrange("p (k n) -> p k n", k=KT)
                act(ex_up[0][:, HS * q:HS * (q + 1), :], wt[:, HS * q:HS * (q + 1), :], ACT.Copy).then_inc(e_uh, 1)

            def ff_up_hi(u, w):
                s, v = slot_use(G_FF + u // 2)
                if w == 0 and u % 2 == 0:
                    ac.wait_ge(loaded[s], v)
                wt = ring[s][:, 0:2 * KT * FC].rearrange("p (k w n) -> p k w n", k=KT, w=2)
                act(ff_up[0][:, w], wt[:, :, w, (u % 2) * P:(u % 2 + 1) * P], ACT.Copy).then_inc(d_uh, 1)

            evacuate_h(0)
            ac.wait_ge(s_par, 16)
            ac.wait_ge(s_cst, 32)
            for l in range(DEPTH):
                project(l)
                hyena(l, 0)
                ret_qk(l)
                hyena(l, 1)
                head_out(2 * l, 5, W("ret_gn"), 0)
                mlstm(l)
                s5(l)
                if l == 1:
                    ac.wait_ge(mix_ready, 2)
                    for q in range(2):
                        split_up(0, q, slot_use(G_MOE)[1], slot_use(G_MOE)[0])
                evacuate_h(2 * l + 1)
                if l == 0:
                    for w in range(2):
                        ff_up_hi(0, w)
                    for u in range(2 * NC_FF):
                        if u < 2 * NC_FF - 1:
                            ac.wait_ge(d_up, 2 * u + 1)
                            ff_up_hi(u + 1, 0)
                        if u:
                            pre(1, u - 1)
                        ac.wait_ge(d_up, 2 * u + 2)
                        act(sil[u % 2], bank[4 + u % 2][:, 0:L], ACT.Silu).then_inc(d_sil, 1)
                        if u < 2 * NC_FF - 1:
                            ff_up_hi(u + 1, 1)
                        ac.wait_ge(d_pr, u + 1)
                        act(ff_mid[0][:, u % 2, :], mid, ACT.Copy).then_inc(d_mh, 1)
                        if u:
                            ac.wait_ge(d_dn, u)
                        w2 = ring[slot_use(G_FF + u // 2)[0]][:, 2 * KT * FC + (u % 2) * D:][:, 0:D]
                        act(ff_w2[0][:, :], w2, ACT.Copy).then_inc(d_wh, 1)
                    evacuate_h(2)

            ac.wait_ge(q_l, 1)
            act(rt[2], rt[2], ACT.Exp).then_inc(q_ex, 1)
            act(acc, h[:, :, :], ACT.Copy, scale=ALPHA).then_inc(q_res, 1)

            def take_x(v, j, q):
                ac.wait_ge(e_g, v * 2 + (q + 1))
                b = bank[6 + q][:, :].rearrange("p (k s) -> p k s", k=4)
                if q:
                    act(xf[j], b[:, NS - 4:4, :], ACT.Copy)
                act(ex_x[j][0][:, 4 * q:min(4 * q + 4, NS), :], b[:, 0:min(4, NS - 4 * q), :], ACT.Copy
                    ).then_inc(e_xh, 1)

            def take_y(n, j):
                ac.wait_ge(e_dn, n * NC_E + 1)
                for q in range(2):
                    act(yex[:, q * 512:(q + 1) * 512], bank[2 * j + q][:, :], ACT.Copy).then_inc(e_y, 1)

            def expert(v, n, j, loads):
                def mid_hi(c):
                    ac.wait_ge(e_mt, n * NC_E + (c + 1))
                    act(ex_mid[0][:, c % 2, :], bank[4 + c % 2][:, 0:L], ACT.Copy).then_inc(e_mh, 1)

                for c in range(NC_E):
                    if c:
                        mid_hi(c - 1)
                    for q in range(2):
                        ac.wait_ge(e_uu, (n * NC_E + c) * 2 + (q + 1))
                        split_up(n * NC_E + (c + 1), q, loads(c + 1), slot_use(G_MOE + j * NC_E + c + 1)[0])
                    ac.wait_ge(e_up, n * NC_E + (c + 1))
                    act(sil[c % 2], bank[4 + c % 2][:, 0:L], ACT.Silu).then_inc(e_sil, 1)
                    ac.wait_ge(e_dn, n * NC_E + (c + 1))
                    w2 = ring[slot_use(G_MOE + j * NC_E + c)[0]][:, 2 * KT * FC:].rearrange("p (f n) -> p f n", f=2)
                    for f in range(2):
                        act(ex_w2[0][:, f, :], w2[:, f, :], ACT.Copy).then_inc(e_wh, 1)
                    if c == 1:
                        take_y(n, 1 - j)
                    if c == 8:
                        take_x(v + 1, 1 - j, 0)
                mid_hi(NC_E - 1)
                take_x(v + 1, 1 - j, 1)

            def all_experts(b):
                v0, n0 = b * (NE + 1), b * NE
                take_x(v0, 0, 0)
                take_x(v0, 0, 1)
                with ac.Fori(0, NE // 2) as i:
                    for j in range(2):
                        def loads(c, j=j):
                            return i * (16 * 2 * NC_E // SLOTS) + slot_use(G_MOE + (n0 + j) * NC_E + c)[1]
                        expert(i * 2 + (v0 + j), i * 2 + (n0 + j), j, loads)
                take_y(n0 + NE, 1)

            all_experts(0)
            crowded = ac.value_load(over[0:1, 0:1], min_val=0, max_val=1)
            with ac.If(crowded == 1):
                all_experts(1)

        @block.vector
        def _(ve):
            tt, ts, stt = nc.vector.tensor_tensor, nc.vector.tensor_scalar, nc.vector.scalar_tensor_tensor
            count = [0]

            def link(ins):
                count[0] += 1
                ins.then_inc(dch, 1)
                ve.wait_ge(dch, count[0])

            def layer_norm(n, src=h):
                for t in range(TT):
                    for c in range(2):
                        ins = nc.vector.bn_stats(bst[:, t, c, :], src[:, t, c * 512:(c + 1) * 512])
                link(ins)
                for t in range(TT):
                    ins = nc.vector.bn_aggr(mv[:, t, :], bst[:, t].rearrange("p c s -> p (c s)"))
                link(ins)
                ts(var, mv[:, :, 1], EPS, None, ALU.add).then_inc(ln_var, 1)
                ve.wait_ge(s_ln, 16 * (n + 1))
                for t in range(TT):
                    ins = stt(out=h[:, t, :], in0=src[:, t, :], scalar=mv[:, t, 0:1], in1=lnb[:, 0:D],
                              op0=ALU.subtract, op1=ALU.mult)
                link(ins)
                ve.wait_ge(ln_rstd, n + 1)
                for t in range(TT):
                    stt(out=h[:, t, :], in0=h[:, t, :], scalar=rstd[:, t:t + 1], in1=lnb[:, D:2 * D],
                        op0=ALU.mult, op1=ALU.add).then_inc(h_ready, 1)

            def residual_psum():
                for t in range(TT):
                    for c in range(2):
                        part = h[:, t, c * 512:(c + 1) * 512]
                        ins = stt(out=part, in0=part, scalar=ALPHA, in1=bank[2 * t + c][:, :], op0=ALU.mult, op1=ALU.add)
                link(ins)

            def pre(l, k):
                fx, filt, pm, rnorm, tfr = fx_[l], filt_[l], pm_[l], rnorm_[l], tfr_[l]
                if k in (0, 1):
                    ve.wait_ge(f_mm, 2 * l + k + 1)
                    b = W("hy_b1" if k == 0 else "hy_b2", 64)
                    link(ts(fx[0], bank[6 + k][0:64, 0:L], b, W("hy_freq", 64), ALU.add, ALU.mult))
                    link(ts(fx[1], fx[0], INV2PI, MAGIC, ALU.mult, ALU.add))
                    link(ts(fx[1], fx[1], MAGIC, None, ALU.subtract))
                    link(stt(out=fx[2], in0=fx[1], scalar=-6.28125, in1=fx[0], op0=ALU.mult, op1=ALU.add))
                    link(stt(out=fx[2], in0=fx[1], scalar=-(2 * math.pi - 6.28125), in1=fx[2], op0=ALU.mult,
                             op1=ALU.add))
                    ts(fx[2], fx[2], 3.1415925, -3.1415925, ALU.min, ALU.max).then_inc(f_red, 1)
                elif k < 6:
                    j = k - 2
                    t, o = j // 2, j % 2
                    ve.wait_ge(f_raw, 4 * l + j + 1)
                    tt(filt[:, t, o], bank[6 + j % 2][:, :].rearrange("p (d c) -> p d c", d=2),
                       bc(window[:, t, :], 1, 2), ALU.mult).then_inc(f_win, 1)
                elif k == 6:
                    ve.wait_ge(f_win, 4 * l + 4)
                    for t in range(TT):
                        for s, m in enumerate(("m0", "nm0")):
                            ins = stt(out=pm[:, s, t], in0=filt[:, t, :, 1, :], scalar=K(m)[:, t:t + 1],
                                      in1=filt[:, t, :, 0, :], op0=ALU.mult, op1=ALU.add)
                    ins.then_inc(f_pm, 1)
                    ve.wait_ge(f_sqrt, l + 1)
                    link(nc.vector.reciprocal(rnorm, rnorm))
                elif k < 11:
                    j = k - 7
                    ve.wait_ge(f_spm, 4 * l + j + 1)
                    tt(spec[:, j // 2, j % 2, :], bank[6 + (j + 1) % 2][:, :], rnorm, ALU.mult).then_inc(f_spec, 1)
                elif k == 11:
                    dt_, x1, th, tf, rr, _, sn, cs, n1, n2, n3 = s5v
                    ve.wait_ge(s_par, 16 * (l + 1))
                    ve.wait_ge(c_dt, l + 1)
                    tt(x1, W("a_re"), dt_, ALU.mult)
                    link(tt(th, W("a_im"), dt_, ALU.mult))
                    link(ts(th, th, INV2PI, None, ALU.mult))
                    link(ts(tf, th, MAGIC, MAGIC, ALU.add, ALU.subtract))
                    tt(tf, th, tf, ALU.subtract).then_inc(c_th, 1)
                    ve.wait_ge(c_exp, 3 * l + 3)
                    tt(n1, rr, cs, ALU.mult)
                    link(tt(n2, rr, sn, ALU.mult))
                    link(ts(n1, n1, 1.0, None, ALU.subtract))
                    tt(sn, n1, W("a_re"), ALU.mult)
                    tt(cs, n2, W("a_im"), ALU.mult)
                    tt(dt_, n2, W("a_re"), ALU.mult)
                    tt(th, n1, W("a_im"), ALU.mult)
                    tt(n3, W("a_re"), W("a_re"), ALU.mult)
                    link(tt(x1, W("a_im"), W("a_im"), ALU.mult))
                    tt(n1, sn, cs, ALU.add)
                    tt(n2, dt_, th, ALU.subtract)
                    link(tt(n3, n3, x1, ALU.add))
                    link(nc.vector.reciprocal(n3, n3))
                    tt(n1, n1, n3, ALU.mult)
                    link(tt(n2, n2, n3, ALU.mult))
                elif k == 12:
                    n1, n2 = s5v[8], s5v[9]
                    cr, ci = s5c[:, 0], s5c[:, 1]
                    ct_ = ct_s[l]
                    ve.wait_ge(f_spec, 4 * l + 4)
                    tt(ct_[0], cr, bc(n1, 2, 32), ALU.mult)
                    tt(ct_[1], ci, bc(n2, 2, 32), ALU.mult)
                    tt(ct_[2], cr, bc(n2, 2, 32), ALU.mult)
                    link(tt(ct_[3], ci, bc(n1, 2, 32), ALU.mult))
                    tt(cr, ct_[0], ct_[1], ALU.subtract)
                    link(stt(out=ci, in0=ct_[2], scalar=-1.0, in1=ct_[3], op0=ALU.mult, op1=ALU.subtract))
                elif k < 21:
                    i = k - 13
                    v = 8 * l + i
                    tf = s5v[3]
                    kk, ph = work[l][:, 0:512], work[l][:, 512:1024]
                    pos = K("pos")
                    if i == 0:
                        ve.wait_ge(f_spec, 4 * l + 4)
                    else:
                        ve.wait_ge(t_ph, v)
                    for d in range(2):
                        ins = ts(ph[:, d * L:(d + 1) * L], pos[:, d * L:(d + 1) * L], tf[:, 2 * i + d:2 * i + d + 1],
                                 None, ALU.mult)
                    link(ins)
                    link(ts(kk, ph, MAGIC, MAGIC, ALU.add, ALU.subtract))
                    if i:
                        ve.wait_ge(t_tab, 3 * v)
                    tt(tfr, ph, kk, ALU.subtract).then_inc(t_ph, 1)

            def project(l):
                for i in range(13):
                    b = bank[i % 4]
                    if 1 <= i < 6:
                        ve.wait_ge(cv_c, 10 * l + 2 * i)
                        for q in range(2):
                            t = 2 * (i - 1) + q
                            ins = stt(out=cv[:, t, 1:L], in0=b[:, q * L:q * L + L - 1], scalar=conv_w[:, t, 0:1],
                                      in1=cv[:, t, 1:L], op0=ALU.mult, op1=ALU.add)
                        link(ins)
                        for q in range(2):
                            t = 2 * (i - 1) + q
                            ins = stt(out=cv[:, t, 0:L - 1], in0=b[:, q * L + 1:(q + 1) * L],
                                      scalar=conv_w[:, t, 2:3], in1=cv[:, t, 0:L - 1], op0=ALU.mult, op1=ALU.add)
                        ins.then_inc(cv_ev, 1)
                    elif i in (6, 7):
                        t = i - 6
                        ve.wait_ge(pj, 13 * l + i + 1)
                        tmp = rtmp.rearrange("p (g s c) -> p g s c", g=8, s=2)
                        b4 = b[:, :].rearrange("p (g s c) -> p g s c", g=8, s=2)
                        if t:
                            ve.wait_ge(rot_ev, 2 * l + t)
                        tt(rq[:, t, :].rearrange("p (g c) -> p g c", g=8),
                           b[:, :].rearrange("p (g c) -> p g c", g=8), bc(rot[0][:, t, :], 1, 8), ALU.mult)
                        for q in range(2):
                            ins = tt(tmp[:, :, q, :], b4[:, :, 1 - q, :],
                                     bc(rot[1][:, t, q * 32:(q + 1) * 32], 1, 8), ALU.mult)
                        link(ins)
                        tt(rq[:, t, :], rq[:, t, :], rtmp, ALU.add).then_inc(rot_ev, 1)
                    elif i == 12:
                        ve.wait_ge(pj, 13 * l + 13)
                        tt(gts, b[:, 0:32].rearrange("p (t g) -> p t g", t=2), bc(W("gate_b"), 1, TT),
                           ALU.add).then_inc(gate_ev, 1)
                    if l == 0:
                        for k in BESIDE[i]:
                            pre(0, k)

            def hyena_product(l, n):
                u = 2 * l + n
                ve.wait_ge(z_sp, u + 1)
                if n == 0:
                    ve.wait_ge(f_spec, 4 * l + 4)
                kc, ks = (spec[:, s].rearrange("p t (o c) -> p t o c", o=2)[:, :, n, :] for s in range(2))
                t4 = [a.rearrange("p (t c) -> p t c", t=2) for a in hy_t]
                uc, us = (bank[1 + s][:, :].rearrange("p (t c) -> p t c", t=2) for s in range(2))
                tt(t4[0], uc, kc, ALU.mult)
                tt(t4[1], us, ks, ALU.mult)
                tt(t4[2], uc, ks, ALU.mult)
                link(tt(t4[3], us, kc, ALU.mult))
                tt(t4[0], t4[0], t4[1], ALU.subtract)
                tt(t4[2], t4[2], t4[3], ALU.add).then_inc(z_pr, 1)

            def hyena_gate(l, n):
                ve.wait_ge(z_iv, 2 * l + n + 1)
                if n:
                    for q in range(2):
                        ve.wait_ge(t_st[q], 16 * 4 * (l + 1))
                for c in range(2):
                    ins = stt(out=cv[:, c, :], in0=cv[:, c, :], scalar=W("hy_bias")[:, 2 * n + c:2 * n + c + 1],
                              in1=bank[0][:, c * L:(c + 1) * L], op0=ALU.mult, op1=ALU.add)
                link(ins)
                dst = cv[:, 0:2, :] if n == 0 else yT[:, 4:6, :]
                tt(dst, cv[:, 0:2, :], cv[:, 2 + 2 * n:4 + 2 * n, :], ALU.mult).then_inc(z_out, 1)

            def head_norm(m, o, gate):
                c8, s8 = (a.rearrange("p (g c) -> p g c", g=8) for a in (cen, sqr))
                link(nc.vector.tensor_reduce(hmean, o, AX.X, ALU.add))
                link(ts(hmean, hmean, 1.0 / HD, None, ALU.mult))
                link(tt(c8, o, bc(hmean, 2, HD), ALU.subtract))
                link(tt(s8, c8, c8, ALU.mult))
                link(nc.vector.tensor_reduce(hvar, s8, AX.X, ALU.add))
                ts(hvar, hvar, 1.0 / HD, EPS, ALU.mult, ALU.add).then_inc(n_var, 1)
                ve.wait_ge(n_rstd, m + 1)
                link(tt(c8, c8, bc(hrstd, 2, HD), ALU.mult))
                tt(ytm, cen.rearrange("p (t c) -> p t c", t=2), gate, ALU.mult).then_inc(n_y, 1)

            def ret_decay(l, a):
                ve.wait_ge(r_s, 4 * l + a + 1)
                for m in range(TT):
                    ins = tt(st[:, a % 2, m, :], bank[5 + a % 2][:, m * L:(m + 1) * L],
                             decay[:, a, P - P * m:P - P * m + L], ALU.mult)
                ins.then_inc(r_st, 1)

            def ret_norm(l):
                ve.wait_ge(r_o, l + 1)
                ve.wait_ge(r_qk, 2 * l + 2)
                head_norm(2 * l, bank[4][:, :].rearrange("p (g c) -> p g c", g=8), vg[:, :, 256:512])

            def ml_rows_a(l):
                ve.wait_ge(m_g4, 2 * l + 2)
                ve.wait_ge(n_tr, 2 * l + 1)
                f = g4.rearrange("p (d k) n -> p d k n", k=2)[:, :, 1, :]
                ts(lf, f, 0.0, None, ALU.min)
                stt(out=ex, in0=f, scalar=-1.0, in1=f, op0=ALU.mult, op1=ALU.max).then_inc(m_abs, 1)
                link(nc.vector.memset(onerow, 1.0))

            def ml_rows_b(l):
                i_ = g4.rearrange("p (d k) n -> p d k n", k=2)[:, :, 0, :]
                ve.wait_ge(m_ln, l + 1)
                link(tt(lf, lf, ex, ALU.subtract))
                scan = nc.vector.tensor_tensor_scan
                scan(acum[:, 0, :], onerow, lf[:, 0, :], 0.0, ALU.mult, ALU.add)
                link(scan(acum[:, 1, ::-1], onerow, lf[:, 1, ::-1], 0.0, ALU.mult, ALU.add))
                link(tt(brow, i_, acum, ALU.subtract))
                scan(crow[:, 0, :], onerow, brow[:, 0, :], 0.0, ALU.mult, ALU.max)
                link(scan(crow[:, 1, ::-1], onerow, brow[:, 1, ::-1], 0.0, ALU.mult, ALU.max))
                stt(out=nmrow, in0=acum, scalar=-1.0, in1=crow, op0=ALU.mult, op1=ALU.subtract).then_inc(m_rows, 1)

            def ml_cols(l):
                ve.wait_ge(m_ct, l + 1)
                nc.vector.tensor_copy(colsb, bank[6][:, 0:32]).then_inc(m_cols, 1)

            def ml_weights(l, a):
                ve.wait_ge(m_sc, 4 * l + a + 1)
                if a >= 2:
                    ve.wait_ge(m_w, 24 * l + 6 * a - 6)
                for d in range(2):
                    ins = stt(out=wmask[:, a % 2, d],
                              in0=bank[2][:, d * L:(d + 1) * L].rearrange("p (b n) -> p b n", b=2),
                              scalar=-1.0, in1=bc(K("mask_fw" if d == 0 else "mask_bw"), 1, 2),
                              op0=ALU.mult, op1=ALU.add)
                ins.then_inc(m_msk, 1)
                w = wml[:, a % 2]
                s4 = bank[a % 2][:, :].rearrange("p (q n) -> p q n", q=4)
                for d in range(2):
                    ve.wait_ge(m_w, 24 * l + 6 * a + 3 * d + 3)
                    stt(out=w[:, 3 * d:3 * d + 2], in0=s4[:, 0:4:3, :], scalar=HD ** -0.5,
                        in1=w[:, 3 * d:3 * d + 2], op0=ALU.mult, op1=ALU.mult)
                    q = 1 if d == 0 else 2
                    ins = stt(out=w[:, 3 * d + 2], in0=s4[:, q, :], scalar=HD ** -0.5, in1=w[:, 3 * d + 2],
                              op0=ALU.mult, op1=ALU.mult)
                ins.then_inc(m_sw, 1)

            def ml_norm(l):
                ve.wait_ge(m_nd, l + 1)
                ve.wait_ge(m_em, l + 1)
                link(nc.vector.tensor_copy(rden, bank[6][:, 0:16]))
                link(stt(out=den, in0=rden, scalar=-1.0, in1=rden, op0=ALU.mult, op1=ALU.max))
                link(tt(den, den, emm, ALU.max))
                link(nc.vector.reciprocal(rden, den))
                hs = [sc[:, q * 512:(q + 1) * 512].rearrange("p (g c) -> p g c", g=8) for q in range(2)]
                for d in range(2):
                    ins = tt(hs[d], bank[4 + d][:, :].rearrange("p (g c) -> p g c", g=8),
                             bc(rden[:, 8 * d:8 * d + 8], 2, HD), ALU.mult)
                link(ins)
                link(tt(hs[0], hs[0], hs[1], ALU.add))
                head_norm(2 * l + 1, hs[0], vo[:, :].rearrange("p (t c) -> p t c", t=2)[:, :, 256:512])

            def s5_tile(l, i):
                rr = s5v[4]
                scan = nc.vector.tensor_tensor_scan
                v = 8 * l + i
                T = s5_table(l, i)
                T4 = T.rearrange("p s d n -> p (s d) n")
                (p1, p2), xs = s5_work(l)
                x1, x2 = T, xs[i % 2]
                ve.wait_ge(b_mm, v + 1)
                if i in (0, 6):
                    ve.wait_ge(s_tab[i // 6], 16 * (l + 1))
                b = bank[3]
                tt(p1.rearrange("p s d n -> p (s d) n"), T4, bc(b[:, 0:L], 1, 4), ALU.mult)
                tt(p2.rearrange("p s d n -> p (s d) n"), T4, bc(b[:, L:2 * L], 1, 4), ALU.mult).then_inc(b_p, 1)
                ve.wait_ge(b_p, v + 1)
                tt(p1[:, 0], p1[:, 0], p2[:, 1], ALU.add)
                link(tt(p2[:, 0], p2[:, 0], p1[:, 1], ALU.subtract))
                for d in range(2):
                    r = rr[:, 2 * i + d:2 * i + d + 1].broadcast_to([P, L])
                    for p in (p1, p2):
                        if d == 0:
                            ins = scan(p[:, 1, 0, :], r, p[:, 0, 0, :], 0.0, ALU.mult, ALU.add)
                        else:
                            ins = scan(p[:, 1, 1, ::-1], r, p[:, 0, 1, ::-1], 0.0, ALU.mult, ALU.add)
                link(ins)
                if i >= 2:
                    ve.wait_ge(b_sum, v - 1)
                tt(x2[:, 1], T[:, 0], p2[:, 1], ALU.mult)
                stt(out=x2[:, 0], in0=T[:, 1], scalar=-1.0, in1=p2[:, 1], op0=ALU.mult, op1=ALU.mult).then_inc(b_x, 1)
                ve.wait_ge(b_x, 2 * v + 1)
                tt(x1, T, bc(p1[:, 1], 1, 2), ALU.mult).then_inc(b_x, 1)
                ve.wait_ge(b_x, 2 * (v + 1))

            def s5_end(l):
                ve.wait_ge(b_tr, l + 1)
                for c in range(2):
                    ins = stt(out=s5z[:, c, :], in0=uT[:, c, :], scalar=W("s5_d")[:, c:c + 1],
                              in1=bank[5][:, c * L:(c + 1) * L], op0=ALU.mult, op1=ALU.add)
                ins.then_inc(b_v, 1)
                ve.wait_ge(b_sig, l + 1)
                tt(yT[:, 2:4, :], s5z, s5s, ALU.mult).then_inc(b_out, 1)

            def mixers(l):
                s5_tile(l, 0)
                hyena_product(l, 0)
                s5_tile(l, 1)
                hyena_gate(l, 0)
                ret_decay(l, 0)
                ret_decay(l, 1)
                s5_tile(l, 2)
                ret_decay(l, 2)
                ret_decay(l, 3)
                s5_tile(l, 3)
                ret_norm(l)
                hyena_product(l, 1)
                s5_tile(l, 4)
                hyena_gate(l, 1)
                ml_rows_a(l)
                s5_tile(l, 5)
                ml_rows_b(l)
                s5_tile(l, 6)
                ml_cols(l)
                ml_weights(l, 0)
                ml_weights(l, 1)
                s5_tile(l, 7)
                ml_weights(l, 2)
                ml_weights(l, 3)
                ml_norm(l)
                s5_end(l)

            def up_lo(g, q, s):
                ve.wait_ge(e_uh, g * 2 + (q + 1))
                wt = ring[s][:, 0:2 * KT * FC].rearrange("p (k n) -> p k n", k=KT)
                k = slice(HS * q, HS * (q + 1))
                tt(ex_up[1][:, k, :], wt[:, k, :], ex_up[0][:, k, :].bitcast(F32), ALU.subtract).then_inc(e_ul, 1)

            def ff_up_lo(u, w):
                ve.wait_ge(d_uh, 2 * u + w + 1)
                wt = ring[slot_use(G_FF + u // 2)[0]][:, 0:2 * KT * FC].rearrange("p (k w n) -> p k w n", k=KT, w=2)
                tt(ff_up[1][:, w], wt[:, :, w, (u % 2) * P:(u % 2 + 1) * P], ff_up[0][:, w].bitcast(F32),
                   ALU.subtract).then_inc(d_ul, 1)

            ve.wait_ge(s_x, 16)
            layer_norm(0)
            ve.wait_ge(s_par, 16)
            ve.wait_ge(s_cst, 32)
            for l in range(DEPTH):
                ve.wait_ge(ht_ready, 8 * l + 4)
                project(l)
                mixers(l)
                ve.wait_ge(mix_ready, l + 1)
                residual_psum()
                layer_norm(2 * l + 1)
                if l == 0:
                    for j in range(4):
                        ve.wait_ge(ht_ready, 4 + j + 1)
                        k, c = 4 * (j % 2), (j // 2) * P
                        tt(ff_x[1][:, k:k + 4, c:c + P], bank[j][:, :].rearrange("p (q n) -> p q n", q=4),
                           ff_x[0][:, k:k + 4, c:c + P].bitcast(F32), ALU.subtract).then_inc(d_x, 1)
                    for w in range(2):
                        ff_up_lo(0, w)
                    for u in range(2 * NC_FF):
                        if u < 2 * NC_FF - 1:
                            ff_up_lo(u + 1, 0)
                        ve.wait_ge(d_sil, u + 1)
                        tt(mid, sil[u % 2], bank[4 + u % 2][:, L:2 * L], ALU.mult).then_inc(d_pr, 1)
                        if u < 2 * NC_FF - 1:
                            ff_up_lo(u + 1, 1)
                        ve.wait_ge(d_mh, u + 1)
                        tt(ff_mid[1][:, u % 2, :], mid, ff_mid[0][:, u % 2, :].bitcast(F32), ALU.subtract
                           ).then_inc(d_mid, 1)
                        ve.wait_ge(d_wh, u + 1)
                        w2 = ring[slot_use(G_FF + u // 2)[0]][:, 2 * KT * FC + (u % 2) * D:][:, 0:D]
                        tt(ff_w2[1][:, :], w2, ff_w2[0][:, :].bitcast(F32), ALU.subtract).then_inc(d_mid, 1)
                        ve.wait_ge(d_mid, 2 * u + 2)
                        if u % 2:
                            ve.sem_inc(freed, 1)
                        if u < NPRE:
                            pre(1, u)
                    ve.wait_ge(d_dn, 2 * NC_FF)
                    residual_psum()
                    layer_norm(2)

            lg, sel, el = rt[0], rt[1], rt[2]
            for q in range(2):
                up_lo(0, q, slot_use(G_MOE)[0])
            ve.wait_ge(q_lg, 1)
            ve.wait_ge(mix_ready, 2)
            link(nc.vector.tensor_copy(lg, bank[6][:, 0:16].rearrange("p (t e) -> p t e", t=2)))
            link(nc.vector.tensor_reduce(rt1[:, 0:2], lg, AX.X, ALU.max))
            tt(el, lg, bc(rt1[:, 0:2], 2, NE), ALU.subtract).then_inc(q_l, 1)
            for t in range(TT):
                a, b = bc(lg[:, t, :], 1, NE), bc(lg[:, t, :], 2, NE)
                tt(cmp1[:, t], a, b, ALU.is_gt)
                ins = tt(cmp2[:, t], a, b, ALU.is_equal)
            link(ins)
            for t in range(TT):
                ins = tt(cmp2[:, t], cmp2[:, t], K("lower").rearrange("p (a b) -> p a b", a=NE), ALU.mult)
            link(ins)
            link(tt(cmp1, cmp1, cmp2, ALU.add))
            for t in range(TT):
                ins = nc.vector.tensor_reduce(rt[3][:, t, :], cmp1[:, t], AX.X, ALU.add)
            link(ins)
            ts(sel, rt[3], 1.5, None, ALU.is_lt).then_inc(q_sel, 1)
            ve.wait_ge(q_sel, 1)
            ve.wait_ge(q_ex, 1)
            link(tt(el, el, sel, ALU.mult))
            link(nc.vector.tensor_reduce(rt1[:, 2:4], el, AX.X, ALU.add))
            link(nc.vector.reciprocal(rt1[:, 4:6], rt1[:, 2:4]))
            ve.wait_ge(init, 2)
            tt(comb[:, :, 0:NE], el, bc(rt1[:, 4:6], 2, NE), ALU.mult)
            ve.wait_ge(q_pos, 1)
            link(ts(rt[4], sel, -4096.0, 4096.0, ALU.mult, ALU.add))
            link(nc.vector.tensor_reduce(rt1[:, 6:7], bank[7][:, 16:24], AX.X, ALU.max))
            link(ts(over[:, 0:1], rt1[:, 6:7], P + 0.5, None, ALU.is_gt))
            tt(posx[:, :, 0:NE], rt[4], bank[7][:, 0:16].rearrange("p (t e) -> p t e", t=2), ALU.add).then_inc(q_px, 1)
            ve.wait_ge(q_px, 1)

            def prepare(e):
                for t in range(TT):
                    ts(onehot[:, t, :], K("iota"), posx[:, t, bass.ds(e, 1)], None, ALU.is_equal)
                    ins = ts(gated[:, t, :], K("iota"), posx[:, t, bass.ds(e, 1)], comb[:, t, bass.ds(e, 1)],
                             ALU.is_equal, ALU.mult)
                ins.then_inc(e_p, 1)

            def placed(v, j):
                ve.wait_ge(e_tm, v + 1)
                nc.vector.tensor_copy(place[j], bank[6][:, 0:L]).then_inc(e_t, 1)

            def add(v, q0):
                for q in (q0, q0 + 1):
                    ve.wait_ge(e_sc, v * 4 + (q + 1))
                    part = acc[:, q // 2, (q % 2) * 512:(q % 2 + 1) * 512]
                    tt(part, part, bank[6 + q % 2][:, :], ALU.add).then_inc(e_acc, 1)

            def x_lo(v, j, q):
                ve.wait_ge(e_xh, v * 2 + (q + 1))
                a, b = 4 * q, min(4 * q + 4, NS)
                tt(ex_x[j][1][:, a:b, :], bank[6 + q][:, 0:(b - a) * P].rearrange("p (k s) -> p k s", s=P),
                   ex_x[j][0][:, a:b, :].bitcast(F32), ALU.subtract).then_inc(e_xg, 1)

            def expert(e, v, n, j):
                def mid_lo(c):
                    ve.wait_ge(e_mh, n * NC_E + (c + 1))
                    tt(ex_mid[1][:, c % 2, :], bank[4 + c % 2][:, 0:L], ex_mid[0][:, c % 2, :].bitcast(F32),
                       ALU.subtract).then_inc(e_mid, 1)

                for c in range(NC_E):
                    if c:
                        mid_lo(c - 1)
                    for q in range(2):
                        up_lo(n * NC_E + (c + 1), q, slot_use(G_MOE + j * NC_E + c + 1)[0])
                    ve.wait_ge(e_sil, n * NC_E + (c + 1))
                    tt(mid, sil[c % 2], bank[4 + c % 2][:, L:2 * L], ALU.mult).then_inc(e_pr, 1)
                    w2 = ring[slot_use(G_MOE + j * NC_E + c)[0]][:, 2 * KT * FC:].rearrange("p (f n) -> p f n", f=2)
                    for f in range(2):
                        ve.wait_ge(e_wh, (n * NC_E + c) * 2 + (f + 1))
                        ins = tt(ex_w2[1][:, f, :], w2[:, f, :], ex_w2[0][:, f, :].bitcast(F32), ALU.subtract)
                    ins.then_inc(freed, 1)
                    if c in (3, 5):
                        add(v, c - 3)
                    if c == 6:
                        ve.wait_ge(e_tm, v + 1)
                        prepare(e + 1)
                    if c == 8:
                        x_lo(v + 1, 1 - j, 0)
                    if c == 10:
                        placed(v + 1, 1 - j)
                mid_lo(NC_E - 1)
                x_lo(v + 1, 1 - j, 1)

            def all_experts(b):
                v0, n0 = b * (NE + 1), b * NE
                if b:
                    nc.vector.memset(place[1], 0.0).then_inc(q_px, 1)
                    ve.wait_ge(q_px, 3)
                prepare(0)
                x_lo(v0, 0, 0)
                x_lo(v0, 0, 1)
                placed(v0, 0)
                with ve.Fori(0, NE // 2) as i:
                    for j in range(2):
                        expert(i * 2 + j, i * 2 + (v0 + j), i * 2 + (n0 + j), j)
                add(v0 + NE, 0)
                add(v0 + NE, 2)
                ve.wait_ge(e_acc, 4 * (v0 + NE) + 4)

            ve.wait_ge(q_res, 1)
            all_experts(0)
            crowded = ve.value_load(over[0:1, 0:1], min_val=0, max_val=1)
            with ve.If(crowded == 1):
                ts(posx, posx, float(P), None, ALU.subtract).then_inc(q_px, 1)
                ve.wait_ge(q_px, 2)
                all_experts(1)
            layer_norm(4, acc)


def constants():
    c = np.zeros((P, CONST_W), np.float64)

    def put(name, a, rows=P):
        s, e = CONST[name]
        c[0:rows, s:e] = np.asarray(a).reshape(rows, e - s)

    p = np.arange(P)
    tok = (np.arange(TT)[None, :] * P + p[:, None])
    gamma = 1.0 - 2.0 ** (-5.0 - np.arange(H))
    j = np.arange(3 * P)
    put("decay", gamma[None, :, None] ** np.abs(j[None, None, :] - P - p[:, None, None]) * HD ** -0.5)
    f = np.arange(L)
    for n, fn in (("c", np.cos), ("s", np.sin)):
        put("dft_" + n, fn(2 * np.pi * tok[:, :, None] * (f + 0.5) / (2 * L)))
        put("idft_" + n, fn(2 * np.pi * (tok[:, :, None] + 0.5) * f / (2 * L)) / L)
    rates = np.abs(np.linspace(math.log(1e-2) / 1.5, math.log(1e-2) / 0.3, DG))
    put("window", np.exp(-(tok[:, :, None] / (L - 1.0)) * rates))
    half = HD // 2
    ang = tok[:, :, None] * 10000.0 ** (-np.arange(half) / half)
    put("rot_c", np.concatenate([np.cos(ang), np.cos(ang)], -1))
    put("rot_s", np.concatenate([-np.sin(ang), np.sin(ang)], -1))
    put("mask_fw", np.where(p[:, None] <= p[None, :], 0.0, NEG))
    put("mask_bw", np.where(p[:, None] >= p[None, :], 0.0, NEG))
    put("before", p[:, None] < p[None, :])
    put("iota", np.tile(p, (P, 1)))
    put("ident", np.eye(P))
    put("ones", np.ones((P, P)))
    t = np.linspace(0.0, 1.0, L)
    w = 2 * np.pi * np.arange(L) / L
    bands = np.linspace(1e-4, 15, 16)
    put("pos", np.tile(np.stack([f, L - 1 - f]).reshape(1, -1), (P, 1)))
    put("pick", np.kron(np.eye(H), np.ones((1, P))), H)
    s, _ = CONST["pick"]
    c[64:97, s:s + L] = np.concatenate([t[None], np.cos(bands[:, None] * w), -np.sin(bands[:, None] * w)], 0)
    put("m0", tok != 0)
    put("nm0", -1.0 * (tok != 0))
    put("halfpi", np.full((P, 1), math.pi / 2 - 1e-7))
    e = np.arange(NE)
    put("lower", np.tile((e[None, :] < e[:, None]).reshape(1, -1), (P, 1)))
    return c.astype(np.float32)


def parameters(a):
    out = np.zeros((DEPTH, P, PAR_W), np.float32)
    for l in range(DEPTH):
        o = out[l]

        def put(name, v, rows=P):
            s, e = PAR[name]
            o[0:rows, s:e] = np.asarray(v).reshape(rows, e - s)

        cw = np.concatenate([a["hy_conv_w"][l], a["ml_conv_w"][l]], 1)
        cb = np.concatenate([a["hy_conv_b"][l], a["ml_conv_b"][l]])[None]
        put("conv", np.concatenate([cw, cb]).reshape(4, 10, P).transpose(2, 1, 0))
        put("hy_bias", a["hy_bias"][l].reshape(2, 2, P).transpose(2, 0, 1))
        for n, k in (("ret_gn", "ret_gn_w"), ("ml_gn", "ml_gn_w"), ("s5_d", "s5_d")):
            put(n, a[k][l].reshape(2, P).T)
        for n in ("a_re", "a_im"):
            put(n, a["s5_" + n][l].reshape(2, 8, P).transpose(2, 1, 0))
        dt = np.repeat(a["s5_log_dt"][l].reshape(2, 8, 2, 1), N_STATE, 3)
        put("log_dt", dt.reshape(2, 8, P).transpose(2, 1, 0))
        cc = np.zeros((2, N_STATE, 2, 8, 2, 2, S5_CH), np.float32)
        bb = np.zeros((4, 2, S5_CH, 2, 2, 2, N_STATE), np.float32)
        for r, n in enumerate(("re", "im")):
            cs = a["s5_c_" + n][l].reshape(2, 8, 2, S5_CH, N_STATE)
            bs = a["s5_b_" + n][l].reshape(2, 4, 2, N_STATE, S5_CH)
            for q in range(2):
                cc[q, :, r, :, :, q, :] = cs[:, :, q].transpose(3, 1, 0, 2)
                bb[:, q, :, :, r, q, :] = bs[:, :, q].transpose(1, 3, 0, 2)
        put("s5_c", cc)
        put("s5_b", bb)
        put("glu", a["s5_w_glu"][l].reshape(2, P, DG).transpose(1, 0, 2))
        put("hy_w12", a["hy_w2"][l], 64)
        s, e = PAR["hy_w12"]
        o[64:97, s:e] = a["hy_w1"][l]
        put("hy_w3", a["hy_w3"][l], 64)
        put("hy_b1", a["hy_b1"][l], 64)
        put("hy_b2", a["hy_b2"][l], 64)
        put("hy_freq", a["hy_freq"][l], 64)
        put("gate_w", a["w_in"][l][:, 3072:3088].reshape(KT, P, 16).transpose(1, 0, 2))
        gb = a["ml_gate_b"][l].reshape(1, 16)
        put("gate_b", np.broadcast_to(gb, (P, 16)))
        put("router", a["moe_router"][0].reshape(KT, P, NE).transpose(1, 0, 2))
    return out


def chunks(w1, w3, w2):
    n = w1.shape[1] // FC
    up = np.stack([w.reshape(KT, P, n, FC).transpose(2, 1, 0, 3) for w in (w1, w3)], 3).reshape(n, P, 2 * KT * FC)
    down = w2.reshape(n, 2, P, D).transpose(0, 2, 1, 3).reshape(n, P, 2 * D)
    return np.concatenate([up, down], 2)


def kernel(**inputs):
    import concourse.bacc as _bacc
    from concourse.bass_utils import run_bass_kernel_spmd as _run

    a = {k: np.asarray(v) for k, v in inputs.items()}
    w_in = np.stack([
        np.concatenate([a["w_in"][l][:, c0:c1] for c0, c1 in ((1024, 2560), (0, 1024), (2560, 3072))], 1)
        .reshape(KT, P, 4, WIN_COLS).transpose(2, 1, 0, 3).reshape(4, P, SLOT) for l in range(DEPTH)])
    w_out = np.stack([a["w_out"][l].reshape(KT, P, 2, 512).transpose(2, 1, 0, 3).reshape(2, P, KT * 512)
                      for l in range(DEPTH)])
    moe = np.empty((NE * NC_E, P, SLOT), np.float32)
    for e in range(NE):
        moe[e * NC_E:(e + 1) * NC_E] = chunks(a["moe_w1"][0, e], a["moe_w3"][0, e], a["moe_w2"][0, e])
    norms = [("ln_in_w", "ln_in_b", None)] + [(f"ln{k}_w", f"ln{k}_b", l) for l in range(DEPTH) for k in (1, 2)]
    rows = [np.concatenate([a[w] if l is None else a[w][l], a[b] if l is None else a[b][l]]) for w, b, l in norms]
    ln = np.broadcast_to(np.stack(rows)[:, None, :], (len(rows), P, 2 * D)).copy()
    arrays = {
        "x": a["x"].reshape(L, D), "ln": ln, "const": constants(), "par": parameters(a), "w_in": w_in,
        "w_out": w_out, "ffn": chunks(a["ffn_w1"][0], a["ffn_w3"][0], a["ffn_w2"][0]), "moe": moe}
    nc = _bacc.Bacc("TRN2", target_bir_lowering=False, num_devices=1)
    args = [nc.dram_tensor(n, list(v.shape), F32, kind="ExternalInput").ap() for n, v in arrays.items()]
    tab = nc.dram_tensor("tab", [DEPTH, 8, P, 4 * L], F32, kind="Internal").ap()
    out = nc.dram_tensor("out", [L, D], F32, kind="ExternalOutput").ap()
    trunk(nc, *args, tab, out)
    r = _run(nc, [arrays], core_ids=[0])
    return r.results[0]["out"].reshape(1, L, D)
```
